# Optimizing a Trainium2 kernel written in Bass

```python
import jax
import jax.numpy as jnp
from jax import lax
import numpy as np

D_MODEL = 1024
BATCH = 1
SEQ = 512
DEPTH = 2

GRID_W = 64
CTX_LEN = 256

POOL_WINDOWS = (2, 4, 8, 16)
POOL_GROUPS = len(POOL_WINDOWS)
POOL_DIM = D_MODEL // 4
POOL_GROUP_DIM = POOL_DIM // POOL_GROUPS

HG_HEADS = 4
HG_DK = 128
HG_DV = (D_MODEL // 4) // HG_HEADS
HG_QK = HG_HEADS * HG_DK
HG_V = HG_HEADS * HG_DV
HG_CHUNK = 64

MLA_HEADS = 8
MLA_NOPE = 64
MLA_ROPE = 32
MLA_V = (D_MODEL // 2) // MLA_HEADS
MLA_Q_LORA = D_MODEL // 4
MLA_KV_LORA = D_MODEL // 8
MLA_QK = MLA_NOPE + MLA_ROPE
MLA_SCALE = MLA_QK ** -0.5
ROPE_BASE = 10000.0
Q_BLOCK = 128

MIX_DIM = POOL_DIM + HG_V + MLA_HEADS * MLA_V
COL_WIDTHS = (POOL_DIM, HG_QK, HG_QK, HG_QK, HG_V, HG_V, MLA_Q_LORA, MLA_KV_LORA, MLA_ROPE)
IN_DIM = sum(COL_WIDTHS)
COL_SPLITS = tuple(int(s) for s in np.cumsum(COL_WIDTHS)[:-1])

N_GROUPS = 4
EXPERTS_PER_GROUP = 8
N_EXPERTS = N_GROUPS * EXPERTS_PER_GROUP
TOP_K = 2
D_EXPERT = D_MODEL // 2
MOE_BLOCK = 128

ALPHA = (2 * DEPTH) ** 0.25
BETA = (8 * DEPTH) ** -0.25
EPS = 1e-6

kernel_name = "hybrid_pool_hgrn2_mla_hmoe_diffusion"

F32 = jnp.float32

def layer_norm(x):
    xf = x.astype(F32)
    mu = jnp.mean(xf, axis=-1, keepdims=True)
    var = jnp.mean(jnp.square(xf - mu), axis=-1, keepdims=True)
    return (xf - mu) * lax.rsqrt(var + EPS)

def modulate(x, shift, scale):
    return (layer_norm(x) * (1.0 + scale.astype(F32)) + shift.astype(F32)).astype(x.dtype)

def post_norm(x, g, b):
    return (layer_norm(x) * g.astype(F32) + b.astype(F32)).astype(x.dtype)

def rms_norm(x, g):
    xf = x.astype(F32)
    return (xf * lax.rsqrt(jnp.mean(xf * xf, axis=-1, keepdims=True) + EPS) * g.astype(F32)).astype(x.dtype)

def axial_rope_tables(n_tokens):
    rows = n_tokens // GRID_W
    row = jnp.repeat(jnp.arange(rows, dtype=F32), GRID_W)
    col = jnp.tile(jnp.arange(GRID_W, dtype=F32), rows)
    n_freq = MLA_ROPE // 4
    inv_freq = ROPE_BASE ** (-jnp.arange(n_freq, dtype=F32) / n_freq)
    ang = jnp.stack([row[:, None] * inv_freq, col[:, None] * inv_freq], axis=1)
    return jnp.cos(ang), jnp.sin(ang)

def apply_axial_rope(x, cos, sin):
    xr = x.astype(F32).reshape(x.shape[:-1] + (2, 2, MLA_ROPE // 4))
    x1, x2 = xr[..., 0, :], xr[..., 1, :]
    out = jnp.stack([x1 * cos - x2 * sin, x2 * cos + x1 * sin], axis=-2)
    return out.reshape(x.shape).astype(x.dtype)

def multi_scale_pool(u, w_pool, scale):
    n = u.shape[1]
    uf = u.astype(F32)
    cs = jnp.concatenate([jnp.zeros_like(uf[:, :1]), jnp.cumsum(uf, axis=1)], axis=1)
    t = jnp.arange(n)
    outs = []
    for gi, w in enumerate(POOL_WINDOWS):
        lo = jnp.clip(t - w // 2, 0, n)
        hi = jnp.clip(t + w // 2, 0, n)
        sl = slice(gi * POOL_GROUP_DIM, (gi + 1) * POOL_GROUP_DIM)
        csg = cs[:, :, sl]
        mean = (csg[:, hi] - csg[:, lo]) / (hi - lo).astype(F32)[None, :, None]
        outs.append(mean - uf[:, :, sl])
    pooled = jnp.stack(outs, axis=2)
    y = jnp.einsum("bngc,gcd->bngd", pooled, w_pool.astype(F32))
    return (y.reshape(u.shape) * scale.astype(F32)).astype(u.dtype)

def log_forget(z, lb):
    return jnp.logaddexp(jnp.log(lb), jnp.log1p(-lb) + jax.nn.log_sigmoid(z.astype(F32)))

def gla_chunk_scan(q, k, v, logf, s0):
    bsz, n, h, dk = q.shape
    dv = v.shape[-1]
    nc = n // HG_CHUNK

    def to_chunks(a):
        return a.reshape(bsz, nc, HG_CHUNK, h, a.shape[-1]).transpose(1, 0, 3, 2, 4)

    mask = jnp.tril(jnp.ones((HG_CHUNK, HG_CHUNK), dtype=bool))

    def step(S, inp):
        qc, kc, vc, gc = inp
        b = jnp.cumsum(gc, axis=2)
        o_inter = jnp.einsum("bhtd,bhde->bhte", qc * jnp.exp(b), S)
        diff = b[:, :, :, None, :] - b[:, :, None, :, :]
        decay = jnp.exp(jnp.where(mask[:, :, None], diff, -jnp.inf))
        attn = jnp.einsum("bhtd,bhsd,bhtsd->bhts", qc, kc, decay)
        o = o_inter + jnp.einsum("bhts,bhse->bhte", attn, vc)
        b_last = b[:, :, -1, :]
        S = jnp.exp(b_last)[..., None] * S + jnp.einsum(
            "bhsd,bhse->bhde", kc * jnp.exp(b_last[:, :, None, :] - b), vc)
        return S, o

    S, o = lax.scan(step, s0, (to_chunks(q), to_chunks(k), to_chunks(v), to_chunks(logf)))
    o = o.transpose(1, 0, 3, 2, 4).reshape(bsz, n, h, dv)
    return o, S

def hgrn2_prepare(q_pre, z_f, z_b, i_in, lb_f, lb_b):
    bsz, n = q_pre.shape[:2]

    def heads(a, d):
        return a.astype(F32).reshape(bsz, n, HG_HEADS, d)

    q = heads(jax.nn.silu(q_pre.astype(F32)), HG_DK)
    g_f = heads(log_forget(z_f, lb_f), HG_DK)
    g_b = heads(log_forget(z_b, lb_b), HG_DK)
    return q, -jnp.expm1(g_f), g_f, -jnp.expm1(g_b), g_b, heads(i_in, HG_DV)

def hgrn2_bidirectional(q, kf, gf, kb, gb, v, s_fwd, s_bwd):
    def flip(a):
        return a[:, ::-1]

    o_f, s_f = gla_chunk_scan(q, kf, v, gf, s_fwd)
    o_b, s_b = gla_chunk_scan(flip(q), flip(kb), flip(v), flip(gb), s_bwd)
    return o_f + flip(o_b), s_f, s_b

def hgrn2_readout(o, gate, norm_g, dtype):
    o = o * lax.rsqrt(jnp.mean(o * o, axis=-1, keepdims=True) + EPS)
    o = o.reshape(o.shape[0], o.shape[1], HG_V) * norm_g.astype(F32) * jax.nn.silu(gate.astype(F32))
    return o.astype(dtype)

def mla_queries(cq, q_norm_g, w_uq, cos, sin):
    bsz, n = cq.shape[:2]
    q = (rms_norm(cq, q_norm_g) @ w_uq).reshape(bsz, n, MLA_HEADS, MLA_QK)
    q_nope, q_rope = q[..., :MLA_NOPE], q[..., MLA_NOPE:]
    if cos is not None:
        q_rope = apply_axial_rope(q_rope, cos[:, None], sin[:, None])
    return jnp.concatenate([q_nope, q_rope], axis=-1).transpose(0, 2, 1, 3)

def mla_keys_values(ckv, k_rope, kv_norm_g, w_ukv, cos, sin):
    bsz, n = ckv.shape[:2]
    kv = (rms_norm(ckv, kv_norm_g) @ w_ukv).reshape(bsz, n, MLA_HEADS, MLA_NOPE + MLA_V)
    k_nope, v = kv[..., :MLA_NOPE], kv[..., MLA_NOPE:]
    if cos is not None:
        k_rope = apply_axial_rope(k_rope, cos, sin)
    k_rope = jnp.broadcast_to(k_rope[:, :, None, :], (bsz, n, MLA_HEADS, MLA_ROPE))
    k = jnp.concatenate([k_nope, k_rope], axis=-1)
    return k.transpose(0, 2, 1, 3), v.transpose(0, 2, 1, 3)

def softmax_attend(q, k, v):
    s = jnp.einsum("bhqd,bhkd->bhqk", q, k, preferred_element_type=F32) * MLA_SCALE
    p = jax.nn.softmax(s, axis=-1)
    return jnp.einsum("bhqk,bhkd->bhqd", p.astype(v.dtype), v)

def block_attention(q, k, v):
    bsz, h, n, d = q.shape
    nb = n // Q_BLOCK
    qb = jnp.moveaxis(q.reshape(bsz, h, nb, Q_BLOCK, d), 2, 0)
    o = lax.map(lambda blk: softmax_attend(blk, k, v), qb)
    return jnp.moveaxis(o, 0, 2).reshape(bsz, h, n, v.shape[-1])

def merge_heads(o):
    bsz, h, n, d = o.shape
    return o.transpose(0, 2, 1, 3).reshape(bsz, n, h * d)

def token_mixer(h, hc, w_in, pool_w, pool_scale, lb_f, lb_b, hg_norm_g,
                q_norm_g, w_uq, kv_norm_g, w_ukv, w_out, cos, sin, with_ctx):
    bsz = h.shape[0]
    (p_in, hq, hzf, hzb, hin, hg, cq, ckv, kr) = jnp.split(h @ w_in, COL_SPLITS, axis=-1)
    (p_in_c, hq_c, hzf_c, hzb_c, hin_c, hg_c, cq_c, ckv_c, kr_c) = jnp.split(hc @ w_in, COL_SPLITS, axis=-1)

    a_lat = multi_scale_pool(p_in, pool_w, pool_scale)

    lat_in = hgrn2_prepare(hq, hzf, hzb, hin, lb_f, lb_b)
    ctx_in = hgrn2_prepare(hq_c, hzf_c, hzb_c, hin_c, lb_f, lb_b)
    zero = jnp.zeros((bsz, HG_HEADS, HG_DK, HG_DV), F32)
    o_c, s_f, s_b = hgrn2_bidirectional(*ctx_in, zero, zero)
    o_l, _, _ = hgrn2_bidirectional(*lat_in, s_f, s_b)
    b_lat = hgrn2_readout(o_l, hg, hg_norm_g, h.dtype)

    q_l = mla_queries(cq, q_norm_g, w_uq, cos, sin)
    k_l, v_l = mla_keys_values(ckv, kr, kv_norm_g, w_ukv, cos, sin)
    k_c, v_c = mla_keys_values(ckv_c, kr_c, kv_norm_g, w_ukv, None, None)
    k_all = jnp.concatenate([k_l, k_c], axis=2)
    v_all = jnp.concatenate([v_l, v_c], axis=2)
    c_lat = merge_heads(block_attention(q_l, k_all, v_all))

    out_lat = jnp.concatenate([a_lat, b_lat, c_lat], axis=-1) @ w_out
    if not with_ctx:
        return out_lat, None

    a_ctx = multi_scale_pool(p_in_c, pool_w, pool_scale)
    b_ctx = hgrn2_readout(o_c, hg_c, hg_norm_g, hc.dtype)
    q_c = mla_queries(cq_c, q_norm_g, w_uq, None, None)
    c_ctx_out = merge_heads(softmax_attend(q_c, k_c, v_c))
    out_ctx = jnp.concatenate([a_ctx, b_ctx, c_ctx_out], axis=-1) @ w_out
    return out_lat, out_ctx

def hier_moe(h, w_rg, b_rg, w_re, b_re, w1, w3, w2):
    n, d = h.shape
    lg = (h @ w_rg).astype(F32) + b_rg.astype(F32)
    pg = jax.nn.softmax(lg, axis=-1)
    g_sel = jnp.argmax(lg, axis=-1)
    w_g = jnp.take_along_axis(pg, g_sel[:, None], axis=-1)[:, 0]
    le = ((h @ w_re).astype(F32) + b_re.astype(F32)).reshape(n, N_GROUPS, EXPERTS_PER_GROUP)
    le_sel = jnp.take_along_axis(le, g_sel[:, None, None], axis=1)[:, 0]
    top_v, top_i = lax.top_k(le_sel, TOP_K)
    gate = jax.nn.softmax(top_v, axis=-1) * w_g[:, None]
    expert = g_sel[:, None] * EXPERTS_PER_GROUP + top_i

    n_assign = n * TOP_K
    e_flat = expert.reshape(-1).astype(jnp.int32)
    tok = jnp.repeat(jnp.arange(n, dtype=jnp.int32), TOP_K)
    wt = gate.reshape(-1)
    order = jnp.argsort(e_flat)
    e_s, tok_s, w_s = e_flat[order], tok[order], wt[order]
    counts = jnp.bincount(e_flat, length=N_EXPERTS)
    starts = jnp.cumsum(counts) - counts
    pcounts = (counts + MOE_BLOCK - 1) // MOE_BLOCK * MOE_BLOCK
    pends = jnp.cumsum(pcounts)
    pstarts = pends - pcounts
    dest = pstarts[e_s] + jnp.arange(n_assign) - starts[e_s]
    n_rows = (n_assign + N_EXPERTS * (MOE_BLOCK - 1) + MOE_BLOCK - 1) // MOE_BLOCK * MOE_BLOCK
    n_blocks = n_rows // MOE_BLOCK
    row_tok = jnp.full((n_rows,), n, dtype=jnp.int32).at[dest].set(tok_s)
    row_w = jnp.zeros((n_rows,), F32).at[dest].set(w_s)
    block_e = jnp.clip(jnp.searchsorted(pends, jnp.arange(n_blocks) * MOE_BLOCK, side="right"),
                       0, N_EXPERTS - 1)
    hp = jnp.concatenate([h, jnp.zeros((1, d), h.dtype)], axis=0)
    xr = hp[row_tok].reshape(n_blocks, MOE_BLOCK, d)

    def expert_block(args):
        xb, e = args
        return (jax.nn.silu(xb @ w1[e]) * (xb @ w3[e])) @ w2[e]

    y = lax.map(expert_block, (xr, block_e)).reshape(n_rows, d)
    out = jnp.zeros((n + 1, d), F32).at[row_tok].add(y.astype(F32) * row_w[:, None])[:n]
    return out.astype(h.dtype)

def setup_inputs(seed: int = 0) -> dict:
    key = jax.random.key(seed)
    ks = jax.random.split(key, 28)
    D = D_MODEL

    def nrm(k, shape, s):
        return jax.random.normal(k, shape, F32) * s

    return {
        "x": nrm(ks[0], (BATCH, SEQ, D), 1.0),
        "c": nrm(ks[1], (BATCH, D), 1.0),
        "ctx": nrm(ks[2], (BATCH, CTX_LEN, D), 1.0),
        "c_ctx": nrm(ks[3], (D,), 1.0),
        "w_mod": nrm(ks[4], (DEPTH, D, 6 * D), 0.5 * D ** -0.5),
        "b_mod": nrm(ks[5], (DEPTH, 6 * D), 0.01),
        "w_in": nrm(ks[6], (DEPTH, D, IN_DIM), D ** -0.5),
        "pool_w": nrm(ks[7], (DEPTH, POOL_GROUPS, POOL_GROUP_DIM, POOL_GROUP_DIM), POOL_GROUP_DIM ** -0.5),
        "pool_scale": 1.0 + nrm(ks[8], (DEPTH, POOL_DIM), 0.05),
        "hg_lb_logits": nrm(ks[9], (DEPTH, 2, HG_QK), 0.5),
        "hg_norm_g": 1.0 + nrm(ks[10], (DEPTH, HG_V), 0.05),
        "mla_q_norm_g": 1.0 + nrm(ks[11], (DEPTH, MLA_Q_LORA), 0.05),
        "mla_w_uq": nrm(ks[12], (DEPTH, MLA_Q_LORA, MLA_HEADS * MLA_QK), MLA_Q_LORA ** -0.5),
        "mla_kv_norm_g": 1.0 + nrm(ks[13], (DEPTH, MLA_KV_LORA), 0.05),
        "mla_w_ukv": nrm(ks[14], (DEPTH, MLA_KV_LORA, MLA_HEADS * (MLA_NOPE + MLA_V)), MLA_KV_LORA ** -0.5),
        "w_out": nrm(ks[15], (DEPTH, MIX_DIM, D), MIX_DIM ** -0.5 * BETA),
        "ln1_g": 1.0 + nrm(ks[16], (DEPTH, D), 0.05),
        "ln1_b": nrm(ks[17], (DEPTH, D), 0.01),
        "ln2_g": 1.0 + nrm(ks[18], (DEPTH, D), 0.05),
        "ln2_b": nrm(ks[19], (DEPTH, D), 0.01),
        "router_group_w": nrm(ks[20], (DEPTH, D, N_GROUPS), D ** -0.5),
        "router_group_b": nrm(ks[21], (DEPTH, N_GROUPS), 0.01),
        "router_expert_w": nrm(ks[22], (DEPTH, D, N_EXPERTS), D ** -0.5),
        "router_expert_b": nrm(ks[23], (DEPTH, N_EXPERTS), 0.01),
        "expert_w1": nrm(ks[24], (DEPTH, N_EXPERTS, D, D_EXPERT), D ** -0.5),
        "expert_w3": nrm(ks[25], (DEPTH, N_EXPERTS, D, D_EXPERT), D ** -0.5),
        "expert_w2": nrm(ks[26], (DEPTH, N_EXPERTS, D_EXPERT, D), D_EXPERT ** -0.5 * BETA),
    }

def reference(x, c, ctx, c_ctx, w_mod, b_mod, w_in, pool_w, pool_scale, hg_lb_logits, hg_norm_g,
              mla_q_norm_g, mla_w_uq, mla_kv_norm_g, mla_w_ukv, w_out, ln1_g, ln1_b, ln2_g, ln2_b,
              router_group_w, router_group_b, router_expert_w, router_expert_b,
              expert_w1, expert_w3, expert_w2):
    bsz, n_lat, d = x.shape
    n_ctx = ctx.shape[1]
    cos, sin = axial_rope_tables(n_lat)
    lb_all = jnp.cumsum(jax.nn.softmax(hg_lb_logits.astype(F32), axis=0), axis=0)
    lb_all = lb_all - lb_all[0:1]
    c_act = jax.nn.silu(c)
    cc_act = jax.nn.silu(c_ctx)
    xc = ctx
    for l in range(DEPTH):
        with_ctx = l < DEPTH - 1
        mod = c_act @ w_mod[l] + b_mod[l]
        mod_c = cc_act @ w_mod[l] + b_mod[l]
        sh1, sc1, g1, sh2, sc2, g2 = jnp.split(mod[:, None, :], 6, axis=-1)
        sh1c, sc1c, g1c, sh2c, sc2c, g2c = jnp.split(mod_c, 6, axis=-1)

        h = modulate(x, sh1, sc1)
        hc = modulate(xc, sh1c, sc1c)
        m_lat, m_ctx = token_mixer(h, hc, w_in[l], pool_w[l], pool_scale[l], lb_all[l, 0], lb_all[l, 1],
                                   hg_norm_g[l], mla_q_norm_g[l], mla_w_uq[l], mla_kv_norm_g[l],
                                   mla_w_ukv[l], w_out[l], cos, sin, with_ctx)
        x = post_norm(ALPHA * x + g1 * m_lat, ln1_g[l], ln1_b[l])
        h = modulate(x, sh2, sc2)
        if with_ctx:
            xc = post_norm(ALPHA * xc + g1c * m_ctx, ln1_g[l], ln1_b[l])
            hc = modulate(xc, sh2c, sc2c)
            tokens = jnp.concatenate([h.reshape(-1, d), hc.reshape(-1, d)], axis=0)
            y = hier_moe(tokens, router_group_w[l], router_group_b[l], router_expert_w[l],
                         router_expert_b[l], expert_w1[l], expert_w3[l], expert_w2[l])
            y_lat = y[:bsz * n_lat].reshape(bsz, n_lat, d)
            y_ctx = y[bsz * n_lat:].reshape(bsz, n_ctx, d)
            xc = post_norm(ALPHA * xc + g2c * y_ctx, ln2_g[l], ln2_b[l])
        else:
            y_lat = hier_moe(h.reshape(-1, d), router_group_w[l], router_group_b[l], router_expert_w[l],
                             router_expert_b[l], expert_w1[l], expert_w3[l],
                             expert_w2[l]).reshape(bsz, n_lat, d)
        x = post_norm(ALPHA * x + g2 * y_lat, ln2_g[l], ln2_b[l])
    return x


_drawn_inputs = setup_inputs


def setup_inputs(seed=0):
    import zlib

    import numpy as np

    out = dict(_drawn_inputs(seed))
    spreads = {}
    factors = {'ctx': 8.0,
     'c_ctx': 5.44,
     'b_mod': 8.0,
     'pool_scale': 8.0,
     'hg_lb_logits': 8.0,
     'hg_norm_g': 8.0,
     'mla_q_norm_g': 8.0,
     'mla_w_uq': 5.51,
     'mla_kv_norm_g': 8.0,
     'ln1_b': 3.839,
     'ln2_b': 4.056,
     'router_group_b': 8.0,
     'router_expert_b': 8.0}
    for name, (base, spread) in spreads.items():
        noise = np.random.default_rng([zlib.crc32(name.encode()), seed]).standard_normal(out[name].shape)
        drawn = base * np.exp(spread * noise) if base else spread * noise
        out[name] = jnp.asarray(drawn.astype(out[name].dtype))
    for name, factor in factors.items():
        out[name] = (out[name] * factor).astype(out[name].dtype)
    return out
```

```python
from contextlib import ExitStack

import numpy as np
import concourse.bass as bass
from concourse import mybir

F32 = mybir.dt.float32
U8 = mybir.dt.uint8
U32 = mybir.dt.uint32
I32 = mybir.dt.int32
ALU = mybir.AluOpType
ACT = mybir.ActivationFunctionType
AX = mybir.AxisListType

P = 128
D = 1024
DC = D // P
SEQ, CTX, DEPTH = 512, 256, 2
LT, CT = SEQ // P, CTX // P
NT = LT + CT
WINDOWS = (2, 4, 8, 16)
HEADS_G, DV_G = 4, 64
HEADS_A, NOPE, ROPE, DV_A = 8, 64, 32, 64
QK = NOPE + ROPE
SCALE = QK ** -0.5
GRID_W, ROPE_BASE = 64, 10000.0
NG, EPG, NE = 4, 8, 32
DE = D // 2
EC = DE // P
ALPHA = (2 * DEPTH) ** 0.25
EPS = 1e-6
LEVELS = (64, 32, 16, 8, 4, 2, 1)
MAXB = 44
SURE_BLOCKS = 2 * LT
ROWS_PER_LAYER = (NT, LT)
Z_MIN = -41.0

C_P, C_V, C_G, C_CQ, C_CKV, C_KR, TOKW = 0, 256, 512, 768, 1024, 1152, 1184
I_P, I_Q, I_ZF, I_ZB, I_V, I_CQ, IN_DIM = 0, 256, 768, 1280, 1792, 2304, 2720
SH1, SC1, G1, SH2, SC2, G2 = range(6)

CONST = {}
for _name, _n in (("ident", 128), ("before", 128), ("ones", 128), ("cos", LT * ROPE), ("sin", LT * ROPE),
                  ("iota", 128), ("multiples", 8), ("pairs", 24), ("block", MAXB), ("begin", MAXB), ("token", NT), ("eps", 1)):
    CONST[_name] = (sum(n for _, n in CONST.values()), _n)
CONSTW = sum(n for _, n in CONST.values())


def shape_constants():
    c = np.zeros((P, CONSTW), np.float32)

    def put(name, a):
        o, n = CONST[name]
        c[:, o:o + n] = a

    i = np.arange(P)
    put("ident", np.eye(P))
    put("before", (i[:, None] < i[None, :]))
    put("ones", 1.0)
    t = np.arange(SEQ)
    inv = ROPE_BASE ** (-np.arange(ROPE // 4, dtype=np.float32) / np.float32(ROPE // 4))
    ang = np.stack([(t // GRID_W).astype(np.float32)[:, None] * inv, (t % GRID_W).astype(np.float32)[:, None] * inv], 1)
    cos, sin = np.cos(ang, dtype=np.float32), np.sin(ang, dtype=np.float32)
    cos = np.stack([cos, cos], 2).reshape(LT, P, ROPE)
    sin = np.stack([-sin, sin], 2).reshape(LT, P, ROPE)
    put("cos", cos.transpose(1, 0, 2).reshape(P, -1))
    put("sin", sin.transpose(1, 0, 2).reshape(P, -1))
    put("iota", np.arange(P))
    put("multiples", 128.0 * np.arange(8))
    put("pairs", 2.0 * np.arange(24))
    put("block", np.arange(MAXB))
    put("begin", P * np.arange(MAXB))
    put("token", i[:, None] + P * np.arange(NT)[None, :])
    put("eps", EPS)
    s, u = i[:, None], i[None, :]
    m = [(s // (2 * h) == u // (2 * h)) & (s % (2 * h) < h) & (u % (2 * h) >= h) for h in LEVELS]
    masks = np.stack([a for x in m for a in (x, x.T)], 1).astype(np.float32).reshape(P, -1)
    bands = []
    for w in WINDOWS:
        n = 3 * P
        tt, ss = np.arange(n), np.arange(n)
        lo, hi = np.clip(tt - w // 2, 0, n), np.clip(tt + w // 2, 0, n)
        a = ((ss[:, None] >= lo) & (ss[:, None] < hi)) / (hi - lo).astype(np.float32)
        a = a - np.eye(n)
        b = a.reshape(3, P, 3, P)
        bands += [b[0, :, 0], b[1, :, 1], b[2, :, 2], b[0, :, 1], b[1, :, 0]]
    bands = np.stack(bands, 1).astype(np.float32).reshape(P, -1)
    return c, np.ascontiguousarray(masks), np.ascontiguousarray(bands)


class Signal:

    def __init__(self, sem, name, book, scope=None):
        self.sem, self.name, self.book, self.count = sem, name, book, 0

    def tick(self, key=None, by=1):
        self.count += by
        self.book[self.name, key] = self.count
        return self.sem, by

    def at(self, key=None):
        return self.sem, self.book.get((self.name, key), 1)

    def last(self):
        return self.sem, self.count


class LoopSignal(Signal):

    def per(self):
        return self.book.get((self.name, "per turn"), 16)

    def close(self):
        self.book[self.name, "per turn"] = self.count

    def now(self, key, i):
        return self.sem, i * self.per() + (self.per() + self.book.get((self.name, key), 1))

    def before(self, key, i):
        return self.sem, i * self.per() + self.book.get((self.name, key), 1)

    def latest(self, i):
        return self.sem, i * self.per() + (self.per() + self.count)


class GatherSignal(LoopSignal):

    def now(self, key, i):
        return self.sem, i * self.per() + self.book.get((self.name, key), 1)


class Kernel:

    def __init__(self, nc, io, book, ctx):
        self.nc, self.io, self.book = nc, io, book
        sb = lambda name, n, dt=F32: ctx.enter_context(nc.sbuf_tensor(name, [P, n], dt))
        self.x = sb("x", NT * D)[:, :].rearrange("p (t d) -> p t d", t=NT)
        self.feat = sb("feat", DC * NT * P)
        self.w = sb("w", 24576)
        self.tok = sb("tok", NT * TOKW)
        self.scr = sb("scr", 6144)
        self.const = sb("const", CONSTW)
        self.masks = sb("masks", 2 * len(LEVELS) * P, U8)
        self.cvec = sb("cvec", DC * 2)
        self.modc = sb("modc", 48 * 2 * DEPTH)
        self.bmod = sb("bmod", 48 * DEPTH)
        self.cols = sb("cols", 32 * DEPTH)
        self.stats = sb("stats", 64)
        self.small = sb("small", 160)
        self.logits = sb("logits", NT * 36)
        self.gates = sb("gates", 2 * NT)
        self.routei = sb("routei", 256, U32)
        self.psum = ctx.enter_context(nc.psum_tensor("psum", [P, 4096], F32))
        self.h_dram = [nc.dram_tensor(f"h_rows{l}", (ROWS_PER_LAYER[l] * P, D), F32, kind="Internal").ap() for l in range(DEPTH)]
        self.y_dram = nc.dram_tensor("y_rows", (MAXB * P, D), F32, kind="Internal").ap()
        self.signals = {}
        self.ctx = ctx
        self.slots = []

    def sig(self, name, kind=Signal):
        if name not in self.signals:
            self.signals[name] = kind(self.ctx.enter_context(self.nc.semaphore(name)), name, self.book)
        return self.signals[name]

    def c(self, name):
        o, n = CONST[name]
        return self.const[:, o:o + n]

    def open_slot(self, pe, key):
        n = len(self.slots)
        self.slots.append(key)
        self.book["slot", key] = n % 4
        if n >= 4:
            self.wait_read(pe, self.slots[n - 4])
        return self.slot(key)

    def wait_read(self, pe, key):
        for who in ("psum_read_by_scalar", "psum_read_by_vector"):
            if (who, key) in self.book:
                pe.wait_ge(*self.sig(who).at(key))

    def slot(self, key):
        s = self.book.get(("slot", key), 0)
        return self.psum[:, s * 1024:(s + 1) * 1024]

    def full(self, key):
        return self.sig("psum_full").at(key)

    def ring(self, n, cols=512):
        return self.w[:, (n % 2) * 4096:(n % 2) * 4096 + DC * cols].rearrange("p (c n) -> p c n", c=DC)

    def feat_c(self, c, a, b):
        return self.feat[:, c * NT * P + a:c * NT * P + b]

    def hg(self, which):
        o = 8192 + 3072 * which
        return self.w[:, o:o + 3072].rearrange("p (h t) -> p h t", h=HEADS_G)

    def prefix(self, which):
        o = 8192 + 9216 + which * 3096
        return self.w[:, o:o + 3096].rearrange("p (h c t) -> p h c t", h=HEADS_G, c=NT)

    def tokv(self, a, b):
        return self.tok[:, :].rearrange("p (t n) -> p t n", t=NT)[:, :, a:b]

    def row(self, n):
        return self.scr[:, n * D:(n + 1) * D] if n < 6 else self.tok[:, (n - 6) * D:(n - 5) * D]

    def mla(self, which):
        o = 8192 + 6144 * which
        return self.w[0:QK, o:o + 6144].rearrange("p (h t) -> p h t", h=HEADS_A)

    def poolw(self):
        return self.w[0:64, 23680:23936]

    def router_w(self):
        return self.tok[:, 6144:6432].rearrange("p (c n) -> p c n", c=DC)

    def router_b(self):
        return self.tok[:, 6432:6468]

    def choices(self, n):
        return self.feat[:, n * 192:(n + 1) * 192].rearrange("p (t e) -> p t e", t=NT)

    def mod(self, l):
        return self.modc[:, 96 * l:96 * l + 96].rearrange("p (j s) -> p j s", s=2)

    def mod_row(self, n):
        return self.scr[0:2, 5632:6144] if n % 2 else self.feat[0:2, 2304:2816]

    def gate_exp(self, t):
        return self.scr[:, 5632 + 256 * (t % 2):5888 + 256 * (t % 2)]

    def latent(self):
        return self.w[:, 20480:22784].rearrange("p (c t) -> p c t", c=3)


R_G1L, R_LN1G, R_LN1B, R_G1C, R_SC2L, R_SH2L, R_SC2C, R_SH2C, R_G2L, R_G2C, R_LN2G, R_LN2B = range(12)
MOD_ROWS = ((R_G1L, G1, 0), (R_G1C, G1, 1), (R_SC2L, SC2, 0), (R_SH2L, SH2, 0), (R_SC2C, SC2, 1), (R_SH2C, SH2, 1),
            (R_G2L, G2, 0), (R_G2C, G2, 1))
K_PS, K_HN, K_QN, K_KN, K_LB, K_OML, K_IND = 0, 2, 4, 6, 8, 16, 24
TURNS = ((4, 5, 0, 1, 2, 3), (5, 4, 3, 2, 1, 0))


RING_MOD, RING_IN, RING_OUT, RING_N = 0, 12, 18, 20
RING_ORDER = [(0, n) for n in range(RING_IN)]
for _l in range(DEPTH):
    RING_ORDER += [(_l, n) for n in range(RING_IN, RING_OUT)]
    RING_ORDER += [(_l + 1, n) for n in range(RING_IN) if _l + 1 < DEPTH]
    RING_ORDER += [(_l, n) for n in range(RING_OUT, RING_N)]
MOD_LEVELS = (2, 7, 12)
RING_D = 4
IN_SLICES = ((I_Q, 512), (I_ZF, 512), (I_ZB, 512), (I_P, 256), (I_V, 512), (I_CQ, 416))


def last_reader(l, n):
    if n < RING_IN:
        return ("mod", l, n)
    if n < RING_OUT:
        s = n - RING_IN
        if s < 3:
            return ("proj", l, s, 3)
        return ("proj", l, s, (ROWS_PER_LAYER[l] if s == 3 else NT) - 1)
    return ("out", l, ROWS_PER_LAYER[l] - 1)


def sync_program(k, sp):
    io, nc = k.io, k.nc
    first = k.sig("first_loads")
    sp.dma_start(k.const[:, :], io["shape_const"]).then_inc(*first.tick("const", 16))
    for s, name in enumerate(("c", "c_ctx")):
        src = io[name] if s else io[name][0, :]
        sp.dma_start(k.cvec[:, :].rearrange("p (c s) -> p c s", s=2)[:, :, s], src.rearrange("(c p) -> p c", p=P),
                     allow_slow_non_contiguous=True).then_inc(*first.tick("c", 16))
    sp.dma_start(k.scr[:, 3072:3072 + 2 * len(LEVELS) * P], io["shape_masks"]).then_inc(*first.tick("masks", 16))
    ring_in = [k.sig("ring0_loaded"), k.sig("ring1_loaded")]
    x_in = k.sig("x_loaded")

    def load_ring(l, n):
        place = RING_ORDER.index((l, n))
        if l and n in (RING_IN, RING_IN + 1):
            sp.wait_ge(*k.sig("moe_done").at(l - 1))
        elif place >= 2:
            sp.wait_ge(*k.full(last_reader(*RING_ORDER[place - 2])))
        if n < RING_IN:
            src, a, w = io["w_mod"][l], 512 * n, 512
        elif n < RING_OUT:
            src, (a, w) = io["w_in"][l], IN_SLICES[n - RING_IN]
        else:
            src, a, w = io["w_out"][l], 512 * (n - RING_OUT), 512
        sp.dma_start(k.ring(n, w), src.rearrange("(c p) n -> p c n", p=P)[:, :, a:a + w]) \
          .then_inc(*ring_in[n % 2].tick((l, n), 16))

    for l in range(DEPTH):
        if l == 0:
            for n in range(2):
                load_ring(l, n)
            sp.dma_start(k.x[:, 0:LT, :], io["x"][0].rearrange("(t p) d -> p t d", p=P)).then_inc(*x_in.tick(None, 16))
            sp.dma_start(k.x[:, LT:NT, :], io["ctx"][0].rearrange("(t p) d -> p t d", p=P)).then_inc(*x_in.tick(None, 16))
            for n in range(2, RING_IN):
                load_ring(l, n)
        for n in range(RING_IN, RING_IN + 2):
            load_ring(l, n)
        sp.wait_ge(*k.sig("psum_read_by_vector").at(("h", l, 0)))
        sp.dma_start(k.scr[:, 3072:3072 + 20 * P], io["shape_bands"]).then_inc(*k.sig("bands_loaded").tick(l, 16))
        for n in range(RING_IN + 2, RING_OUT):
            load_ring(l, n)
        sp.wait_ge(*k.full(("pool", l, 3)))
        mla_w = k.sig("mla_weights_loaded")
        sp.dma_start(k.scr[:, 3072:4608].rearrange("p (c n) -> p c n", c=2),
                     io["mla_w_uq"][l].rearrange("(c p) n -> p c n", p=P)).then_inc(*mla_w.tick(l, 16))
        sp.dma_start(k.scr[:, 4608:5632], io["mla_w_ukv"][l]).then_inc(*mla_w.tick(l, 16))
        if l + 1 < DEPTH:
            for n in range(RING_IN):
                load_ring(l + 1, n)
        for n in range(RING_OUT, RING_N):
            load_ring(l, n)
        rows = k.sig("norm_rows_loaded")
        sp.wait_ge(*k.sig("psum_read_by_scalar").at(("mixed", l, ROWS_PER_LAYER[l] - 1)))
        for r, name in ((R_LN1G, "ln1_g"), (R_LN1B, "ln1_b"), (R_LN2G, "ln2_g"), (R_LN2B, "ln2_b")):
            sp.dma_start(k.row(r), io[name][l].partition_broadcast(P)).then_inc(*rows.tick(l, 16))
        for name, n, o in (("router_group_w", NG, 0), ("router_expert_w", NE, NG)):
            sp.dma_start(k.router_w()[:, :, o:o + n], io[name][l].rearrange("(c p) n -> p c n", p=P)).then_inc(*rows.tick(l, 16))
        for name, n, o in (("router_group_b", NG, 0), ("router_expert_b", NE, NG)):
            sp.dma_start(k.router_b()[:, o:o + n], io[name][l].partition_broadcast(P)).then_inc(*rows.tick(l, 16))
        for t in range(ROWS_PER_LAYER[l]):
            sp.wait_ge(*k.sig("h2_ready").at((l, t)))
            sp.dma_start(k.h_dram[l][t * P:(t + 1) * P, :], k.w[:, 20480 + (t % 2) * D:20480 + (t % 2 + 1) * D]) \
              .then_inc(*k.sig("h2_stored%d" % (t % 2)).tick((l, t), 16))
        moe_sync(k, sp, l)
    for s in ("out_stored",):
        sp.wait_ge(*k.sig(s).at("all"))


def matmuls(pe, out, pairs):
    for n, (a, b) in enumerate(pairs):
        ins = pe.matmul(out, a, b, start=(n == 0), stop=(n == len(pairs) - 1))
    return ins


def tensor_program(k, pe):
    full = k.sig("psum_full")
    ident = k.c("ident")
    ring_in = [k.sig("ring0_loaded"), k.sig("ring1_loaded")]
    pe.wait_ge(*k.sig("first_loads").at("masks"))
    for l in range(DEPTH):
        T = ROWS_PER_LAYER[l]
        if l == 0:
            pe.wait_ge(*k.sig("c_ready").at())
            for n in range(RING_IN + 1):
                if n < RING_IN:
                    tensor_mod(k, pe, l, n)
                if n:
                    tensor_mod_columns(k, pe, l, n - 1)
        for t in range(NT):
            ps = k.open_slot(pe, ("h", l, t))
            pe.wait_ge(*k.sig("z_ready").at((l, t)))
            z = k.scr[:, (t % 2) * D:(t % 2 + 1) * D]
            for c in range(DC):
                ins = pe.transpose(ps[:, c * P:(c + 1) * P], z[:, c * P:(c + 1) * P], ident)
            ins.then_inc(*full.tick(("h", l, t)))
        for s in range(3):
            n = RING_IN + s
            pe.wait_ge(*ring_in[n % 2].at((l, n)))
            w = k.ring(n)
            cuts = ((0, 512), (512, 768)) if s or T == NT else ((0, 512),)
            for hd in range(HEADS_G):
                ps = k.open_slot(pe, ("proj", l, s, hd))
                if s == 0 and hd == 0:
                    k.wait_read(pe, ("h", l, NT - 1))
                for a, b in cuts:
                    ins = matmuls(pe, ps[:, a:b], [(w[:, c, hd * P:(hd + 1) * P], k.feat_c(c, a, b)) for c in range(DC)])
                ins.then_inc(*full.tick(("proj", l, s, hd)))
        for s in range(3, 6):
            n = RING_IN + s
            pe.wait_ge(*ring_in[n % 2].at((l, n)))
            width = IN_SLICES[s][1]
            w = k.ring(n, width)
            for t in range(T if s == 3 else NT):
                ps = k.open_slot(pe, ("proj", l, s, t))
                a, b = token_cut(l, s, t)
                ins = matmuls(pe, ps[:, a:b], [(k.feat_c(c, t * P, (t + 1) * P), w[:, c, a:b]) for c in range(DC)])
                ins.then_inc(*full.tick(("proj", l, s, t)))
        pe.wait_ge(*k.sig("bands_loaded").at(l))
        band = k.scr[:, 3072:3072 + 20 * P].rearrange("p (b t) -> p b t", t=P)
        for g in range(4):
            ps = k.open_slot(pe, ("pool", l, g))
            if g == 0:
                k.wait_read(pe, ("proj", l, 3, T - 1))
            for t in range(T):
                lo, hi = (0, LT - 1) if t < LT else (LT, NT - 1)
                blocks = [(t, 0 if t == lo else 2 if t == hi else 1)]
                blocks += [(t - 1, 3)] if t > lo else []
                blocks += [(t + 1, 4)] if t < hi else []
                ins = matmuls(pe, ps[0:64, t * P:(t + 1) * P],
                              [(k.tokv(64 * g, 64 * g + 64)[:, s, :], band[:, 5 * g + b, :]) for s, b in blocks])
            ins.then_inc(*full.tick(("pool", l, g)))
        pooled = k.feat[0:64, 3072:6144].rearrange("p (g t) -> p g t", g=4)
        for j in range(2):
            ps = k.open_slot(pe, ("poolout", l, j))
            if j == 0:
                k.wait_read(pe, ("pool", l, 3))
                pe.wait_ge(*k.sig("columns_loaded").at(l))
            for g in (2 * j, 2 * j + 1):
                for a, b in ((0, 512), (512, 768))[:1 + (T == NT)]:
                    ins = matmuls(pe, ps[64 * (g % 2):64 * (g % 2) + 64, a:b], [(k.poolw()[:, 64 * g:64 * g + 64], pooled[:, g, a:b])])
            ins.then_inc(*full.tick(("poolout", l, j)))
        tensor_hgrn(k, pe, l)
        tensor_attention(k, pe, l)
        m = k.mod(l)
        for r, v, s in MOD_ROWS:
            ps = k.open_slot(pe, ("row", l, r))
            for c in range(DC):
                ins = pe.matmul(ps[:, c * P:(c + 1) * P], m[:, v * DC + c, s:s + 1].to_broadcast([P, P]), ident, start=True, stop=True)
            ins.then_inc(*full.tick(("row", l, r)))
        for n in (RING_OUT, RING_OUT + 1):
            pe.wait_ge(*ring_in[n % 2].at((l, n)))
        for n in range(T + 2):
            if n < T:
                ps = k.open_slot(pe, ("out", l, n))
                if n == 0:
                    k.wait_read(pe, ("mixed", l, T - 1))
                for half in range(2):
                    w = k.ring(RING_OUT + half)
                    ins = matmuls(pe, ps[:, half * 512:half * 512 + 512],
                                  [(k.feat_c(c, n * P, (n + 1) * P), w[:, c, :]) for c in range(DC)])
                ins.then_inc(*full.tick(("out", l, n)))
            if n >= 2:
                t = n - 2
                ps = k.open_slot(pe, ("h2", l, t))
                pe.wait_ge(*k.sig("h2_ready").at((l, t)))
                z = k.w[:, 20480 + (t % 2) * D:20480 + (t % 2 + 1) * D]
                for c in range(DC):
                    ins = pe.transpose(ps[:, c * P:(c + 1) * P], z[:, c * P:(c + 1) * P], ident)
                ins.then_inc(*full.tick(("h2", l, t)))
                ps = k.open_slot(pe, ("logit", l, t))
                k.wait_read(pe, ("h2", l, t))
                h2t = k.w[:, 22528 + (t % 2) * D:22528 + (t % 2 + 1) * D].rearrange("p (c t) -> p c t", c=DC)
                rw = k.router_w()
                ins = matmuls(pe, ps[:, 0:36], [(h2t[:, c, :], rw[:, c, :]) for c in range(DC)])
                ins.then_inc(*full.tick(("logit", l, t)))
        ps = k.open_slot(pe, ("rank", l))
        pe.wait_ge(*k.sig("choices_ready").at(l))
        ch = k.choices(2)
        for t in range(T):
            ins = matmuls(pe, ps[:, t * 32:t * 32 + 32], [(k.c("ones"), ch[:, s, :]) for s in range(t)] + [(k.c("before"), ch[:, t, :])])
        ins = matmuls(pe, ps[:, 512:544], [(k.c("ones"), ch[:, s, :]) for s in range(T)])
        ins.then_inc(*full.tick(("rank", l)))
        ps = k.open_slot(pe, ("rows", l))
        pe.wait_ge(*k.sig("row_hots_ready").at(l))
        hot, own = (k.scr[:, o:o + 2 * NT * w].rearrange("p (n r) -> p n r", r=w) for o, w in ((0, P), (2688, MAXB)))
        ins = matmuls(pe, ps[:, 0:MAXB], [(hot[:, NT * j + t, :], own[:, NT * j + t, :]) for j in range(2) for t in range(T)])
        ins.then_inc(*full.tick(("rows", l)))
        moe_tensor(k, pe, l)


def tensor_mod(k, pe, l, n):
    pe.wait_ge(*k.sig("ring%d_loaded" % (n % 2)).at((l, n)))
    w, ps = k.ring(n), k.open_slot(pe, ("mod", l, n))
    cv = k.cvec[:, :].rearrange("p (c s) -> p c s", s=2)
    matmuls(pe, ps[0:2, 0:512], [(cv[:, c, :], w[:, c, :]) for c in range(DC)]).then_inc(*k.sig("psum_full").tick(("mod", l, n)))


def tensor_mod_columns(k, pe, l, n):
    ps = k.open_slot(pe, ("modcol", l, n))
    k.wait_read(pe, ("mod", l, n))
    for j in range(4):
        ins = pe.transpose(ps[:, 2 * j:2 * j + 2], k.mod_row(n)[:, j * P:(j + 1) * P], k.c("ident")[0:2, 0:2])
    ins.then_inc(*k.sig("psum_full").tick(("modcol", l, n)))


def token_cut(l, s, t):
    a, b = 0, IN_SLICES[s][1]
    if ROWS_PER_LAYER[l] <= t:
        a, b = {4: (0, 256), 5: (256, 416)}[s]
    return a, b


def tensor_hgrn(k, pe, l):
    full, ident, T = k.sig("psum_full"), k.c("ident"), ROWS_PER_LAYER[l]
    dring = lambda n: k.scr[:, (n % RING_D) * 768:(n % RING_D + 1) * 768].rearrange("p (c t) -> p c t", c=NT)
    kt = k.feat[:, 3072:3840].rearrange("p (c t) -> p c t", c=NT)
    st = k.feat[:, 3840:4608].rearrange("p (d c e) -> p d c e", d=2, c=NT)
    qd = k.feat[:, 4608:6144].rearrange("p (d c t) -> p d c t", d=2, c=NT)
    at = k.feat[:, 1536:2304].rearrange("p (c t) -> p c t", c=NT)
    q, kf, kb = (k.hg(n).rearrange("p h (c t) -> p h c t", c=NT) for n in range(3))
    v = k.tokv(C_V, C_V + 256)
    for hd in range(HEADS_G):
        for dr in range(2):
            ps = k.open_slot(pe, ("keys", l, hd, dr))
            pe.wait_ge(*k.sig("decayed").at((l, hd, dr)))
            for c in range(NT):
                ins = pe.transpose(ps[:, c * P:(c + 1) * P], dring(hd * 18 + dr)[:, c, :], ident)
            ins.then_inc(*full.tick(("keys", l, hd, dr)))
            ps = k.open_slot(pe, ("adds", l, hd, dr))
            k.wait_read(pe, ("keys", l, hd, dr))
            for c in range(NT):
                ins = matmuls(pe, ps[:, c * 64:(c + 1) * 64], [(kt[:, c, :], v[:, c, 64 * hd:64 * hd + 64])])
            ins.then_inc(*full.tick(("adds", l, hd, dr)))
        ps = k.open_slot(pe, ("diag", l, hd))
        for c in range(T):
            ins = matmuls(pe, ps[:, c * P:(c + 1) * P], [(kf[:, hd, c, :], q[:, hd, c, :]), (kb[:, hd, c, :], q[:, hd, c, :])])
        ins.then_inc(*full.tick(("diag", l, hd)))
        for m in range(2 * len(LEVELS)):
            ps = k.open_slot(pe, ("level", l, hd, m))
            pe.wait_ge(*k.sig("decayed").at((l, hd, 4 + m)))
            dz = dring(hd * 18 + 4 + m)
            for c in range(T):
                ins = pe.matmul(ps[:, c * P:(c + 1) * P], dz[:, c, :], dz[:, c, :], start=True, stop=True)
            ins.then_inc(*full.tick(("level", l, hd, m)))
            if m in MOD_LEVELS and l + 1 < DEPTH:
                n = 3 * hd + MOD_LEVELS.index(m)
                if n:
                    tensor_mod_columns(k, pe, l + 1, n - 1)
                tensor_mod(k, pe, l + 1, n)
        ps = k.open_slot(pe, ("hgout", l, hd))
        k.wait_read(pe, ("adds", l, hd, 1))
        k.wait_read(pe, ("level", l, hd, 2 * len(LEVELS) - 1))
        for c in range(T):
            terms = [(at[:, c, :], v[:, c, 64 * hd:64 * hd + 64])]
            for dr in range(2):
                n = TURNS[dr].index(c)
                terms += [(qd[:, dr, c, :], st[:, dr, n, :])] if n else []
            ins = matmuls(pe, ps[:, c * 64:(c + 1) * 64], terms)
        ins.then_inc(*full.tick(("hgout", l, hd)))
    if l + 1 < DEPTH:
        tensor_mod_columns(k, pe, l + 1, RING_IN - 1)
    for t in range(T):
        ps = k.open_slot(pe, ("readout", l, t))
        if t == 0:
            pe.wait_ge(*k.sig("readout_ready").at(l))
        for j in range(2):
            ins = pe.transpose(ps[:, j * P:(j + 1) * P], k.tokv(C_P, C_P + 256)[:, t, j * P:(j + 1) * P], ident)
        ins.then_inc(*full.tick(("readout", l, t)))


def tensor_attention(k, pe, l):
    full, ident, T = k.sig("psum_full"), k.c("ident"), ROWS_PER_LAYER[l]
    lat = k.latent()
    uq = k.scr[:, 3072:4608].rearrange("p (c n) -> p c n", c=2)
    ukv = k.scr[:, 4608:5632]
    cq, ckv = k.tokv(C_CQ, C_CQ + 256), k.tokv(C_CKV, C_CKV + 128)
    for t in range(NT):
        ps = k.open_slot(pe, ("latent", l, t))
        if t == 0:
            pe.wait_ge(*k.sig("latents_normed").at(l))
        if t < T:
            for c in range(2):
                pe.transpose(ps[:, c * P:(c + 1) * P], cq[:, t, c * P:(c + 1) * P], ident)
        pe.transpose(ps[:, 2 * P:3 * P], ckv[:, t, :], ident).then_inc(*full.tick(("latent", l, t)))
    pe.wait_ge(*k.sig("mla_weights_loaded").at(l))
    qt = k.scr[:, 0:768].rearrange("p (h n) -> p h n", h=HEADS_A)
    kt = k.scr[:, 768:1536].rearrange("p (h n) -> p h n", h=HEADS_A)
    for t in range(NT):
        if t < T:
            ps = k.open_slot(pe, ("q", l, t))
            k.wait_read(pe, ("latent", l, t))
            for half in range(2):
                ins = matmuls(pe, ps[:, half * 512:half * 512 + 384],
                              [(lat[:, c, t * P:(t + 1) * P], uq[:, c, half * 384:half * 384 + 384]) for c in range(2)])
            ins.then_inc(*full.tick(("q", l, t)))
        ps = k.open_slot(pe, ("kv", l, t))
        k.wait_read(pe, ("latent", l, t))
        for half in range(2):
            ins = matmuls(pe, ps[:, half * 512:half * 512 + 512], [(lat[:, 2, t * P:(t + 1) * P], ukv[:, half * 512:half * 512 + 512])])
        ins.then_inc(*full.tick(("kv", l, t)))
        for name, src, ok in (("qT", qt, t < T), ("kT", kt, True)):
            if ok:
                ps = k.open_slot(pe, (name, l, t))
                k.wait_read(pe, ("q" if name == "qT" else "kv", l, t))
                if name == "kT" or t < LT:
                    pe.wait_ge(*k.sig(name[0] + "_roped").at((l, t)))
                for hd in range(HEADS_A):
                    ins = pe.transpose(ps[0:QK, hd * P:(hd + 1) * P], src[:, hd, :], ident)
                ins.then_inc(*full.tick((name, l, t)))
    turns = [(hd, t) for hd in range(HEADS_A) for t in range(T)]
    qm, km, v = k.mla(0), k.mla(1), k.tokv(0, 512)
    for n in range(len(turns) + 2):
        if n < len(turns):
            hd, t = turns[n]
            ps = k.open_slot(pe, ("score", l, hd, t))
            if n == 0:
                k.wait_read(pe, ("qT", l, T - 1))
                k.wait_read(pe, ("kT", l, NT - 1))
                k.wait_read(pe, ("kv", l, NT - 1))
            for a, b in key_cuts(t):
                ins = pe.matmul(ps[:, a:b], qm[:, hd, t * P:(t + 1) * P], km[:, hd, a:b], start=True, stop=True)
            ins.then_inc(*full.tick(("score", l, hd, t)))
        if 1 <= n <= len(turns):
            hd, t = turns[n - 1]
            prob = k.scr[:, ((n - 1) % 2) * 768:((n - 1) % 2) * 768 + 768]
            ps = k.open_slot(pe, ("probT", l, hd, t))
            k.wait_read(pe, ("score", l, hd, t))
            for kt_ in key_tiles(t):
                ins = pe.transpose(ps[:, kt_ * P:(kt_ + 1) * P], prob[:, kt_ * P:(kt_ + 1) * P], ident)
            ins.then_inc(*full.tick(("probT", l, hd, t)))
        if n >= 2:
            hd, t = turns[n - 2]
            pt = k.scr[:, 1536 + ((n - 2) % 2) * 768:1536 + ((n - 2) % 2) * 768 + 768]
            ps = k.open_slot(pe, ("pv", l, hd, t))
            k.wait_read(pe, ("probT", l, hd, t))
            ins = matmuls(pe, ps[:, 0:64], [(pt[:, kt_ * P:(kt_ + 1) * P], v[:, kt_, hd * 64:hd * 64 + 64]) for kt_ in key_tiles(t)])
            ins.then_inc(*full.tick(("pv", l, hd, t)))
    for t in range(T):
        ps = k.open_slot(pe, ("mixed", l, t))
        if t == 0:
            k.wait_read(pe, ("pv", l, HEADS_A - 1, T - 1))
        for c in range(4):
            ins = pe.transpose(ps[:, c * P:(c + 1) * P], k.tokv(512, 1024)[:, t, c * P:(c + 1) * P], ident)
        ins.then_inc(*full.tick(("mixed", l, t)))


def key_tiles(t):
    return range(NT) if t < LT else range(LT, NT)


def key_cuts(t):
    return ((0, 512), (512, 768)) if t < LT else ((512, 768),)


def mv(k):
    return k.stats[:, 0:12].rearrange("p (t s) -> p t s", s=2)


ST_BN, ST_RSTD, ST_LOG = 12, 36, 42
SM_END, SM_SS, SM_RS, SM_LS, SM_QS, SM_MAX, SM_SUM, SM_INV = 0, 48, 72, 96, 120, 134, 138, 142


def scalar_program(k, act):
    nc = k.nc
    step = k.sig("scalar_step")
    read = k.sig("psum_read_by_scalar")

    def link(ins):
        ins.then_inc(*step.tick())
        act.wait_ge(*step.last())

    eps = k.c("eps")

    def rstd(key, out, log, src, scale=1.0):
        act.wait_ge(*k.sig("variance_ready").at(key))
        link(act.activation(log, src, ACT.Ln, bias=eps, scale=scale))
        act.activation(out, log, ACT.Exp, scale=-0.5).then_inc(*k.sig("rstd_ready").tick(key))

    act.wait_ge(*k.sig("first_loads").at("masks"))
    act.activation(k.small[:, 0:16], k.cvec[:, :], ACT.Exp, scale=-1.0).then_inc(*k.sig("c_exp").tick())
    act.wait_ge(*k.sig("bound_gap").at())
    act.activation(k.logits[:, 24:40], k.logits[:, 24:40], ACT.Exp).then_inc(*k.sig("bound_exp").tick())
    for l in range(DEPTH):
        T = ROWS_PER_LAYER[l]
        m = k.mod(l)
        col = lambda n: k.cols[:, 32 * l + n:32 * l + n + 1]
        tcols = T * P
        if l == 0:
            for n in range(RING_IN):
                scalar_mod(k, act, l, n)
        rstd(("h", l, NT - 1), k.stats[:, ST_RSTD:ST_RSTD + NT], k.stats[:, ST_LOG:ST_LOG + NT], mv(k)[:, :, 1])
        act.wait_ge(*k.sig("mod_ready").at(l))
        for t in range(NT):
            s = 0 if t < LT else 1
            act.wait_ge(*k.full(("h", l, t)))
            ps = k.slot(("h", l, t))
            for c in range(4):
                ins = act.activation(k.feat_c(c, t * P, (t + 1) * P), ps[:, c * P:(c + 1) * P], ACT.Identity,
                                     scale=m[:, SC1 * DC + c, s:s + 1], bias=m[:, SH1 * DC + c, s:s + 1])
            ins.then_inc(*read.tick(("h", l, t)))
        tmp = lambda n, w: k.scr[:, n * 768:n * 768 + w]
        for s in range(3):
            w = tcols if s == 0 else NT * P
            for hd in range(HEADS_G):
                key = ("proj", l, s, hd)
                if s == 0:
                    act.wait_ge(*k.full(key))
                    if hd:
                        act.wait_ge(*k.sig("psum_read_by_vector").at(("proj", l, s, hd - 1)))
                    act.activation(tmp(0, w), k.slot(key)[:, 0:w], ACT.Exp, scale=-1.0).then_inc(*k.sig("q_exp").tick((l, hd)))
                else:
                    act.wait_ge(*k.sig("psum_read_by_vector").at(key))
                    link(act.activation(tmp(0, w), tmp(0, w), ACT.Exp, scale=-1.0))
                    act.activation(tmp(2, w), tmp(0, w), ACT.Ln, scale=col(K_LB + 4 * (s - 1) + hd), bias=1.0)
                    act.activation(tmp(3, w), tmp(0, w), ACT.Ln, bias=1.0).then_inc(*k.sig("logs_ready").tick(key))
        act.wait_ge(*k.sig("y_cleared").at())
        for s, o in ((3, C_P), (4, C_V), (5, C_CQ)):
            for t in range(T if s == 3 else NT):
                key = ("proj", l, s, t)
                a, b = token_cut(l, s, t)
                act.wait_ge(*k.full(key))
                if s == 4 and t < T:
                    if t >= 2:
                        act.wait_ge(*k.sig("gate_silu").at((l, t - 2)))
                    act.activation(k.gate_exp(t), k.slot(key)[:, 256:512], ACT.Exp, scale=-1.0).then_inc(*k.sig("gate_exp").tick((l, t)))
                act.copy(k.tokv(o + a, o + b)[:, t, :], k.slot(key)[:, a:b]).then_inc(*read.tick(key))
        pooled = k.feat[0:64, 3072:6144].rearrange("p (g t) -> p g t", g=4)
        for g in range(4):
            act.wait_ge(*k.full(("pool", l, g)))
            act.copy(pooled[:, g, 0:tcols], k.slot(("pool", l, g))[0:64, 0:tcols]).then_inc(*read.tick(("pool", l, g)))
        act.wait_ge(*k.sig("columns_loaded").at(l))
        for j in range(2):
            act.wait_ge(*k.full(("poolout", l, j)))
            act.activation(k.feat_c(j, 0, tcols), k.slot(("poolout", l, j))[:, 0:tcols], ACT.Identity, scale=col(K_PS + j)) \
               .then_inc(*read.tick(("poolout", l, j)))
        scalar_hgrn(k, act, l, link)
        n = 4 * T
        rstd(("hg", l), k.small[:, SM_RS:SM_RS + n], k.small[:, SM_LS:SM_LS + n], k.small[:, SM_SS:SM_SS + n], 1.0 / DV_G)
        for t in range(T):
            key = ("readout", l, t)
            act.wait_ge(*k.full(key))
            for j in range(2):
                ins = act.activation(k.feat_c(2 + j, t * P, (t + 1) * P), k.slot(key)[:, j * P:(j + 1) * P], ACT.Identity, scale=col(K_HN + j))
            ins.then_inc(*read.tick(key))
        scalar_attention(k, act, l, rstd)
        for r, _, _ in MOD_ROWS:
            act.wait_ge(*k.full(("row", l, r)))
            act.copy(k.row(r), k.slot(("row", l, r))).then_inc(*read.tick(("row", l, r)))
        for n in range(T + 2):
            if n >= 2:
                h2_copy(k, act, l, n - 2, read)
            for which, t in (("post1", n), ("h2", n - 1)):
                if 0 <= t < T:
                    rstd((which, l, t), k.stats[:, ST_RSTD + t:ST_RSTD + t + 1], k.stats[:, ST_LOG + t:ST_LOG + t + 1], mv(k)[:, t, 1:2])
        act.wait_ge(*k.sig("group_logits_ready").at(l))
        act.activation(k.feat[:, 672:672 + 4 * T], k.feat[:, 672:672 + 4 * T], ACT.Exp).then_inc(*k.sig("group_exp").tick(l))
        act.wait_ge(*k.sig("second_minus_first").at(l))
        act.activation(k.feat[:, 1160:1160 + T], k.feat[:, 1160:1160 + T], ACT.Exp).then_inc(*k.sig("second_exp").tick(l))
        moe_scalar(k, act, l)
        for t in range(T):
            one = lambda o: k.stats[:, o + t:o + t + 1]
            rstd(("post2", l, t), one(ST_RSTD), one(ST_LOG), mv(k)[:, t, 1:2])


def scalar_mod(k, act, l, n):
    act.wait_ge(*k.full(("mod", l, n)))
    if l and n == 1:
        act.wait_ge(*k.sig("gate_silu").at((l - 1, ROWS_PER_LAYER[l - 1] - 1)))
    if n >= 2:
        act.wait_ge(*k.full(("modcol", l, n - 2)))
    act.copy(k.mod_row(n), k.slot(("mod", l, n))[0:2, 0:512]).then_inc(*k.sig("psum_read_by_scalar").tick(("mod", l, n)))


def h2_copy(k, act, l, t, read):
    act.wait_ge(*k.full(("h2", l, t)))
    if t >= 2:
        act.wait_ge(*k.full(("logit", l, t - 2)))
    act.copy(k.w[:, 22528 + (t % 2) * D:22528 + (t % 2 + 1) * D], k.slot(("h2", l, t))).then_inc(*read.tick(("h2", l, t)))


def decay_end(k, l, n):
    hd, m = divmod(n, 18)
    if m < 2:
        return k.full(("keys", l, hd, m))
    if m < 4:
        return k.sig("decayed").at((l, hd, m))
    return k.full(("level", l, hd, m - 4))


def scalar_hgrn(k, act, l, link):
    T = ROWS_PER_LAYER[l]
    read = k.sig("psum_read_by_scalar")
    dring = lambda n: k.scr[:, (n % RING_D) * 768:(n % RING_D + 1) * 768].rearrange("p (c t) -> p c t", c=NT)
    xf, xb = k.prefix(0), k.prefix(1)
    kt = k.feat[:, 3072:3840]
    act.wait_ge(*k.sig("head_done").at((l, 2, HEADS_G - 1)))
    for dr, x in enumerate((xf, xb)):
        ins = act.activation(k.small[:, SM_END + 24 * dr:SM_END + 24 * dr + 24].rearrange("p (h c) -> p h c", h=HEADS_G), x[:, :, :, P], ACT.Exp)
    ins.then_inc(*k.sig("ends_ready").tick(l))

    def exp(hd, m):
        n = hd * 18 + m
        d = dring(n)
        c = NT if m < 2 else T
        if m in (1, 2):
            if n >= RING_D:
                act.wait_ge(*decay_end(k, l, n - RING_D))
            src = xb[:, hd, 0:c, 0:P] if m == 1 else xf[:, hd, 0:c, 1:P + 1]
        else:
            act.wait_ge(*k.sig("gap_ready").at((l, hd, m)))
            src = d[:, 0:c, :]
        act.activation(d[:, 0:c, :], src, ACT.Exp).then_inc(*k.sig("decay_ready").tick((l, hd, m)))

    def keys(hd, dr):
        act.wait_ge(*k.full(("keys", l, hd, dr)))
        if hd or dr:
            act.wait_ge(*k.full(("adds", l, hd - (dr == 0), 1 - dr)))
        act.copy(kt, k.slot(("keys", l, hd, dr))[:, 0:768]).then_inc(*read.tick(("keys", l, hd, dr)))

    for hd in range(HEADS_G):
        exp(hd, 0)
        exp(hd, 1)
        exp(hd, 2)
        keys(hd, 0)
        exp(hd, 3)
        keys(hd, 1)
        for m in range(4, 18):
            exp(hd, m)
            for i, level in enumerate(MOD_LEVELS):
                if l + 1 < DEPTH and m - 4 == min(level + 2, 13):
                    scalar_mod(k, act, l + 1, 3 * hd + i)
        act.wait_ge(*k.full(("hgout", l, hd)))
        act.copy(k.tokv(64 * hd, 64 * hd + 64)[:, 0:T, :], k.slot(("hgout", l, hd))[:, 0:T * 64].rearrange("p (t n) -> p t n", t=T)) \
           .then_inc(*read.tick(("hgout", l, hd)))


def scalar_attention(k, act, l, rstd):
    T = ROWS_PER_LAYER[l]
    read = k.sig("psum_read_by_scalar")
    col = lambda n: k.cols[:, 32 * l + n:32 * l + n + 1]
    lat = k.latent()
    rstd(("cq", l), k.small[:, SM_RS:SM_RS + T], k.small[:, SM_LS:SM_LS + T], k.small[:, SM_QS:SM_QS + T], 1.0 / 256)
    rstd(("ckv", l), k.small[:, SM_RS + 6:SM_RS + 12], k.small[:, SM_LS + 6:SM_LS + 12], k.small[:, SM_QS + 6:SM_QS + 12], 1.0 / 128)
    for t in range(NT):
        key = ("latent", l, t)
        act.wait_ge(*k.full(key))
        for c in range(0 if t < T else 2, 3):
            ins = act.activation(lat[:, c, t * P:(t + 1) * P], k.slot(key)[:, c * P:(c + 1) * P], ACT.Identity,
                                 scale=col(K_QN + c if c < 2 else K_KN))
        ins.then_inc(*read.tick(key))
    for t in range(NT):
        if t < T:
            key = ("q", l, t)
            act.wait_ge(*k.full(key))
            if t:
                act.wait_ge(*k.full(("qT", l, t - 1)))
            act.copy(k.scr[:, 0:768].rearrange("p (a n) -> p a n", a=2), k.slot(key).rearrange("p (a n) -> p a n", a=2)[:, :, 0:384]) \
               .then_inc(*read.tick(key))
        key = ("kv", l, t)
        act.wait_ge(*k.full(key))
        if t:
            act.wait_ge(*k.full(("kT", l, t - 1)))
        act.copy(k.scr[:, 768:1536].rearrange("p (h n) -> p h n", h=HEADS_A)[:, :, 0:NOPE],
                 k.slot(key).rearrange("p (h n) -> p h n", h=HEADS_A)[:, :, 0:NOPE])
        act.copy(k.tokv(0, 512)[:, t, :].rearrange("p (h n) -> p h n", h=HEADS_A),
                 k.slot(key).rearrange("p (h n) -> p h n", h=HEADS_A)[:, :, NOPE:]).then_inc(*read.tick(key))
        key = ("kT", l, t)
        act.wait_ge(*k.full(key))
        act.copy(k.mla(1)[:, :, t * P:(t + 1) * P], k.slot(key)[0:QK, :].rearrange("p (h t) -> p h t", h=HEADS_A)).then_inc(*read.tick(key))
    turns = [(hd, t) for hd in range(HEADS_A) for t in range(T)]
    for n in range(len(turns) + 2):
        if n < len(turns):
            hd, t = turns[n]
            key = ("score", l, hd, t)
            a, b = (0, 768) if t < LT else (512, 768)
            act.wait_ge(*k.sig("max_ready").at(key))
            if n >= 2:
                act.wait_ge(*k.full(("probT", l) + turns[n - 2]))
            act.activation(k.scr[:, (n % 2) * 768 + a:(n % 2) * 768 + b], k.slot(key)[:, a:b], ACT.Exp, scale=SCALE,
                           bias=k.small[:, SM_MAX + n % 4:SM_MAX + n % 4 + 1],
                           accum_out=k.small[:, SM_SUM + n % 4:SM_SUM + n % 4 + 1]).then_inc(*read.tick(key))
        if n >= 2:
            hd, t = turns[n - 2]
            key = ("pv", l, hd, t)
            act.wait_ge(*k.full(key))
            act.wait_ge(*k.sig("sum_inverted").at(("score", l, hd, t)))
            act.activation(k.tokv(512 + 64 * hd, 576 + 64 * hd)[:, t, :], k.slot(key)[:, 0:64], ACT.Identity,
                           scale=k.small[:, SM_INV + (n - 2) % 4:SM_INV + (n - 2) % 4 + 1]).then_inc(*read.tick(key))
    for t in range(T):
        key = ("mixed", l, t)
        act.wait_ge(*k.full(key))
        act.copy(k.feat[:, :].rearrange("p (c t) -> p c t", c=DC)[:, 4:8, t * P:(t + 1) * P],
                 k.slot(key)[:, 0:512].rearrange("p (c t) -> p c t", c=4)).then_inc(*read.tick(key))


def vector_program(k, dve):
    step = k.sig("vector_step")
    read = k.sig("psum_read_by_vector")

    def link(ins):
        ins.then_inc(*step.tick())
        dve.wait_ge(*step.last())

    def statistics(key, t):
        bn = k.stats[:, ST_BN + (t % 2) * 12:ST_BN + (t % 2) * 12 + 12].rearrange("p (a s) -> p a s", a=2)
        for a in range(2):
            ins = dve.bn_stats(bn[:, a, :], k.x[:, t, a * 512:(a + 1) * 512])
        link(ins)
        dve.bn_aggr(mv(k)[:, t, :], bn).then_inc(*k.sig("variance_ready").tick(key))

    def normalise(out, key, t):
        dve.wait_ge(*k.sig("variance_ready").at(key))
        dve.wait_ge(*k.sig("rstd_ready").at(key))
        return dve.tensor_scalar(out, k.x[:, t, :], mv(k)[:, t, 0:1], k.stats[:, ST_RSTD + t:ST_RSTD + t + 1], ALU.subtract, ALU.mult)

    dve.wait_ge(*k.sig("c_exp").at())
    e = k.small[:, 0:16]
    link(dve.tensor_scalar(e, e, 1.0, None, ALU.add))
    link(dve.reciprocal(e, e))
    dve.tensor_tensor(k.cvec[:, :], k.cvec[:, :], e, ALU.mult).then_inc(*k.sig("c_ready").tick())
    dve.wait_ge(*k.sig("first_loads").at("masks"))
    link(dve.tensor_copy(k.masks[:, :], k.scr[:, 3072:3072 + 2 * len(LEVELS) * P]))
    dve.wait_ge(*k.sig("x_loaded").at())
    for l in range(DEPTH):
        T = ROWS_PER_LAYER[l]
        tcols = T * P
        m = k.mod(l)
        col = lambda n: k.cols[:, 32 * l + n:32 * l + n + 1]
        for t in range(NT):
            statistics(("h", l, t), t)
        if l:
            dve.wait_ge(*k.sig("moe_done").at(l - 1))
        for dr in range(2):
            dve.memset(k.prefix(dr)[:, :, :, 0:1], 0.0)
        lower_bound(k, dve, l, link)
        dve.wait_ge(*k.sig("columns_loaded").at(l))
        if l == 0:
            for n in range(RING_IN):
                vector_mod(k, dve, l, n)
        dve.wait_ge(*k.sig("mod_ready").at(l))
        for t in range(NT + 1):
            if t < NT:
                if t >= 2:
                    dve.wait_ge(*k.full(("h", l, t - 2)))
                dve.wait_ge(*k.sig("rstd_ready").at(("h", l, NT - 1)))
                dve.tensor_scalar(k.scr[:, (t % 2) * D:(t % 2 + 1) * D], k.x[:, t, :], mv(k)[:, t, 0:1],
                                  k.stats[:, ST_RSTD + t:ST_RSTD + t + 1], ALU.subtract, ALU.mult).then_inc(*k.sig("z_ready").tick((l, t)))
            if t:
                u = t - 1
                s = 0 if u < LT else 1
                dve.wait_ge(*k.full(("h", l, u)))
                ps = k.slot(("h", l, u))
                for c in range(4, 8):
                    ins = dve.tensor_scalar(k.feat_c(c, u * P, (u + 1) * P), ps[:, c * P:(c + 1) * P],
                                            m[:, SC1 * DC + c, s:s + 1], m[:, SH1 * DC + c, s:s + 1], ALU.mult, ALU.add)
                ins.then_inc(*read.tick(("h", l, u)))
        tmp = lambda n, w: k.scr[:, n * 768:n * 768 + w]
        for s in range(3):
            w = tcols if s == 0 else NT * P
            for hd in range(HEADS_G):
                key = ("proj", l, s, hd)
                ps = k.slot(key)[:, 0:w]
                if s == 0:
                    dve.wait_ge(*k.sig("q_exp").at((l, hd)))
                    link(dve.tensor_scalar(tmp(0, w), tmp(0, w), 1.0, None, ALU.add))
                    link(dve.reciprocal(tmp(0, w), tmp(0, w)))
                    dve.tensor_tensor(k.hg(0)[:, hd, 0:w], ps, tmp(0, w), ALU.mult).then_inc(*read.tick(key))
                    continue
                dve.wait_ge(*k.full(key))
                dve.wait_ge(*(read.at(("proj", l, 0, HEADS_G - 1)) if (s, hd) == (1, 0) else k.sig("head_done").at((l, s - (hd == 0), (hd - 1) % 4))))
                dve.tensor_scalar(tmp(0, w), ps, Z_MIN, None, ALU.max)
                dve.tensor_scalar(tmp(1, w), ps, -Z_MIN, 0.0, ALU.add, ALU.min).then_inc(*read.tick(key))
                dve.wait_ge(*read.at(key))
                dve.wait_ge(*k.sig("logs_ready").at(key))
                link(dve.tensor_tensor(tmp(2, w), tmp(2, w), tmp(3, w), ALU.subtract))
                dve.scalar_tensor_tensor(tmp(2, w), tmp(1, w), col(K_IND + 4 * (s - 1) + hd), tmp(2, w), ALU.mult, ALU.add)
                link(dve.tensor_scalar(tmp(3, w), tmp(0, w), 1.0, None, ALU.add))
                link(dve.reciprocal(tmp(3, w), tmp(3, w)))
                dve.scalar_tensor_tensor(k.hg(s)[:, hd, 0:w], tmp(0, w), col(K_OML + 4 * (s - 1) + hd), tmp(3, w), ALU.mult, ALU.mult)
                for c in range(NT):
                    ins = dve.tensor_tensor_scan(k.prefix(s - 1)[:, hd, c, 1:P + 1], k.c("ones"), tmp(2, w)[:, c * P:(c + 1) * P], 0.0, ALU.mult, ALU.add)
                ins.then_inc(*k.sig("head_done").tick((l, s, hd)))
        dve.wait_ge(*k.sig("head_done").at((l, 2, HEADS_G - 1)))
        for t in range(T):
            e, g = k.gate_exp(t), k.tokv(C_G, C_G + 256)[:, t, :]
            dve.wait_ge(*k.sig("gate_exp").at((l, t)))
            link(dve.tensor_scalar(e, e, 1.0, None, ALU.add))
            link(dve.reciprocal(e, e))
            dve.wait_ge(*k.sig("psum_read_by_scalar").at(("proj", l, 4, t)))
            dve.tensor_tensor(g, g, e, ALU.mult).then_inc(*k.sig("gate_silu").tick((l, t)))
        vector_hgrn(k, dve, l, link)
        o, g = (k.tokv(a, a + 256)[:, 0:T, :] for a in (C_P, C_G))
        n = 4 * T
        sq = k.scr[:, 0:T * 256].rearrange("p (t n) -> p t n", t=T)
        dve.wait_ge(*k.sig("psum_read_by_scalar").at(("hgout", l, HEADS_G - 1)))
        link(dve.tensor_tensor(sq, o, o, ALU.mult))
        dve.tensor_reduce(k.small[:, SM_SS:SM_SS + n], k.scr[:, 0:T * 256].rearrange("p (n e) -> p n e", e=DV_G), AX.X, ALU.add) \
           .then_inc(*k.sig("variance_ready").tick(("hg", l)))
        link(dve.tensor_tensor(o, o, g, ALU.mult))
        dve.wait_ge(*k.sig("rstd_ready").at(("hg", l)))
        o4, rs = o.rearrange("p t (h e) -> p t h e", e=DV_G), k.small[:, SM_RS:SM_RS + n].rearrange("p (t h) -> p t h", t=T)
        dve.tensor_tensor(o4, o4, rs.unsqueeze(3).to_broadcast([P, T, HEADS_G, DV_G]), ALU.mult).then_inc(*k.sig("readout_ready").tick(l))
        if l + 1 < DEPTH:
            vector_mod(k, dve, l + 1, RING_IN - 1)
        vector_attention(k, dve, l, link)
        vector_post_mixer(k, dve, l, link, statistics, normalise)
        vector_route(k, dve, l, link)
        moe_vector(k, dve, l)
        for n in range(T + 1):
            if n < T:
                xa, xb = (k.feat[:, i * D:(i + 1) * D] for i in (2 * (n % 2), 2 * (n % 2) + 1))
                dve.wait_ge(*k.sig("y_gathered%d" % (n % 2)).at((l, n)))
                link(dve.tensor_scalar(xb, xb, k.gates[:, NT + n:NT + n + 1], None, ALU.mult))
                link(dve.scalar_tensor_tensor(xa, xa, k.gates[:, n:n + 1], xb, ALU.mult, ALU.add))
                link(dve.tensor_tensor(xa, xa, k.row(R_G2L if n < LT else R_G2C), ALU.mult))
                dve.scalar_tensor_tensor(k.x[:, n, :], k.x[:, n, :], ALPHA, xa, ALU.mult, ALU.add).then_inc(*k.sig("y_used").tick((l, n)))
                dve.wait_ge(*k.sig("y_used").at((l, n)))
                statistics(("post2", l, n), n)
            if n:
                t = n - 1
                link(normalise(k.x[:, t, :], ("post2", l, t), t))
                link(dve.tensor_tensor(k.x[:, t, :], k.x[:, t, :], k.row(R_LN2G), ALU.mult))
                dve.tensor_tensor(k.x[:, t, :], k.x[:, t, :], k.row(R_LN2B), ALU.add).then_inc(*k.sig("x_ready").tick((l, t)))
        dve.wait_ge(*k.sig("x_ready").at((l, T - 1)))


def vector_mod(k, dve, l, n):
    key, m, read = ("modcol", l, n), k.mod(l), k.sig("psum_read_by_vector")
    dve.wait_ge(*k.full(key))
    b = k.bmod[:, 48 * l + 4 * n:48 * l + 4 * n + 4].unsqueeze(2).to_broadcast([P, 4, 2])
    dve.tensor_tensor(m[:, 4 * n:4 * n + 4, :], k.slot(key)[:, 0:8].rearrange("p (j s) -> p j s", s=2), b, ALU.add) \
       .then_inc(*read.tick(key))
    if n == RING_IN - 1:
        dve.wait_ge(*read.at(key))
        for v in (SC1, SC2):
            ins = dve.tensor_scalar(m[:, v * DC:(v + 1) * DC, :], m[:, v * DC:(v + 1) * DC, :], 1.0, None, ALU.add)
        ins.then_inc(*k.sig("mod_ready").tick(l))


def lower_bound(k, dve, l, link):
    if l == 0:
        dve.wait_ge(*k.sig("columns_loaded").at(0))
        lg = k.logits[:, 0:16].rearrange("p (l n) -> p l n", l=DEPTH)
        mx, e0, e1, p0 = (k.logits[:, 16 + 8 * n:24 + 8 * n] for n in range(4))
        link(dve.tensor_tensor(mx, lg[:, 0, :], lg[:, 1, :], ALU.max))
        dve.tensor_tensor(e0, lg[:, 0, :], mx, ALU.subtract)
        dve.tensor_tensor(e1, lg[:, 1, :], mx, ALU.subtract).then_inc(*k.sig("bound_gap").tick())
        dve.wait_ge(*k.sig("bound_exp").at())
        link(dve.tensor_tensor(mx, e0, e1, ALU.add))
        link(dve.reciprocal(mx, mx))
        dve.tensor_tensor(p0, e0, mx, ALU.mult)
        link(dve.tensor_tensor(e1, e1, mx, ALU.mult))
        link(dve.tensor_tensor(e1, p0, e1, ALU.add))
        dve.tensor_tensor(k.cols[:, K_LB:K_LB + 8], p0, p0, ALU.subtract)
        link(dve.tensor_tensor(k.cols[:, 32 + K_LB:32 + K_LB + 8], e1, p0, ALU.subtract))
    c = k.cols[:, 32 * l:32 * l + 32]
    dve.tensor_scalar(c[:, K_OML:K_OML + 8], c[:, K_LB:K_LB + 8], -1.0, 1.0, ALU.mult, ALU.add)
    link(dve.tensor_scalar(c[:, K_IND:K_IND + 8], c[:, K_LB:K_LB + 8], 0.0, None, ALU.is_equal))


def halves(ap, h):
    return ap.rearrange("p c (b t) -> p c b t", t=2 * h)


def vector_hgrn(k, dve, l, link):
    T = ROWS_PER_LAYER[l]
    read = k.sig("psum_read_by_vector")
    dring = lambda n: k.scr[:, (n % RING_D) * 768:(n % RING_D + 1) * 768].rearrange("p (c t) -> p c t", c=NT)
    st = k.feat[:, 3840:4608].rearrange("p (d c e) -> p d c e", d=2, c=NT)
    qd = k.feat[:, 4608:6144].rearrange("p (d c t) -> p d c t", d=2, c=NT)
    at = k.feat[:, 1536:2304].rearrange("p (c t) -> p c t", c=NT)
    arrays = [k.hg(n).rearrange("p h (c t) -> p h c t", c=NT) for n in range(3)]
    ends = k.small[:, SM_END:SM_END + 48].rearrange("p (d h c) -> p d h c", d=2, h=HEADS_G)
    masks = k.masks[:, :].rearrange("p (m t) -> p m t", t=P)
    decayed = k.sig("decayed")
    dve.wait_ge(*k.sig("ends_ready").at(l))
    for hd in range(HEADS_G):
        q, kf, kb = (a[:, hd] for a in arrays)
        for m, (src, out) in enumerate(((kf, None), (kb, None), (q, qd[:, 0]), (q, qd[:, 1]))):
            d = dring(hd * 18 + m)
            c = NT if m < 2 else T
            dve.wait_ge(*k.sig("decay_ready").at((l, hd, m)))
            if m == 2:
                dve.wait_ge(*k.full(("hgout", l, hd - 1) if hd else ("poolout", l, 1)))
            dve.tensor_tensor((d if out is None else out)[:, 0:c, :], d[:, 0:c, :], src[:, 0:c, :], ALU.mult).then_inc(*decayed.tick((l, hd, m)))
        for dr in range(2):
            key = ("adds", l, hd, dr)
            dve.wait_ge(*k.full(key))
            for n in range(NT - 1):
                c = TURNS[dr][n]
                add = k.slot(key)[:, c * 64:(c + 1) * 64]
                if n == 0:
                    ins = dve.tensor_copy(st[:, dr, 1, :], add)
                else:
                    ins = dve.scalar_tensor_tensor(st[:, dr, n + 1, :], st[:, dr, n, :], ends[:, dr, hd, c:c + 1], add, ALU.mult, ALU.add)
                if n < NT - 2:
                    link(ins)
            ins.then_inc(*read.tick(key))
        key = ("diag", l, hd)
        dve.wait_ge(*k.full(key))
        dve.tensor_copy(at[:, 0:T, :], k.slot(key)[:, 0:T * P].rearrange("p (c t) -> p c t", c=T)).then_inc(*read.tick(key))
        for m in range(2 * len(LEVELS) + 1):
            if m < 2 * len(LEVELS):
                h, dr = LEVELS[m // 2], m % 2
                d = halves(dring(hd * 18 + 4 + m)[:, 0:T, :], h)
                first, second = (kf, q) if dr == 0 else (q, kb)
                dve.wait_ge(*k.sig("decay_ready").at((l, hd, 4 + m)))
                dve.tensor_tensor(d[:, :, :, 0:h], d[:, :, :, 0:h], halves(first[:, 0:T, :], h)[:, :, :, 0:h], ALU.mult)
                dve.tensor_tensor(d[:, :, :, h:2 * h], d[:, :, :, h:2 * h], halves(second[:, 0:T, :], h)[:, :, :, h:2 * h], ALU.mult) \
                   .then_inc(*decayed.tick((l, hd, 4 + m)))
            if m:
                key = ("level", l, hd, m - 1)
                dve.wait_ge(*k.full(key))
                dve.wait_ge(*read.at(("level", l, hd, m - 2) if m > 1 else ("diag", l, hd)))
                dve.copy_predicated(at[:, 0:T, :], masks[:, m - 1, :].unsqueeze(1).to_broadcast([P, T, P]),
                                    k.slot(key)[:, 0:T * P].rearrange("p (c t) -> p c t", c=T)).then_inc(*read.tick(key))
                n = 3 * hd + (MOD_LEVELS.index(m - 1) if m - 1 in MOD_LEVELS else 0)
                if l + 1 < DEPTH and m - 1 in MOD_LEVELS and n:
                    vector_mod(k, dve, l + 1, n - 1)


def vector_attention(k, dve, l, link):
    T = ROWS_PER_LAYER[l]
    read = k.sig("psum_read_by_vector")
    small = k.small
    dve.wait_ge(*k.sig("readout_ready").at(l))
    for o, w, n, key in ((C_CQ, 256, T, "cq"), (C_CKV, 128, NT, "ckv")):
        sq = (k.scr[:, 0:n * w] if key == "cq" else k.scr[:, 1536:1536 + n * w]).rearrange("p (t n) -> p t n", t=n)
        v = k.tokv(o, o + w)[:, 0:n, :]
        s = SM_QS + (0 if key == "cq" else 6)
        link(dve.tensor_tensor(sq, v, v, ALU.mult))
        dve.tensor_reduce(small[:, s:s + n], sq, AX.X, ALU.add).then_inc(*k.sig("variance_ready").tick((key, l)))
    for o, w, n, key in ((C_CQ, 256, T, "cq"), (C_CKV, 128, NT, "ckv")):
        v = k.tokv(o, o + w)[:, 0:n, :]
        r = SM_RS + (0 if key == "cq" else 6)
        dve.wait_ge(*k.sig("rstd_ready").at((key, l)))
        ins = dve.tensor_tensor(v, v, small[:, r:r + n].unsqueeze(2).to_broadcast([P, n, w]), ALU.mult)
    ins.then_inc(*k.sig("latents_normed").tick(l))

    def rope(x, heads, a, b, t):
        cos = k.c("cos")[:, t * ROPE:(t + 1) * ROPE].unsqueeze(1).to_broadcast([P, heads, ROPE])
        sin = k.c("sin")[:, t * ROPE:(t + 1) * ROPE].rearrange("p (a s f) -> p a s f", a=2, s=2)
        av, bv = (y.rearrange("p (h n) -> p h n", h=heads) for y in (a, b))
        b5, x5 = (y.rearrange("p h (a s f) -> p h a s f", a=2, s=2) for y in (bv, x))
        dve.tensor_tensor(av, x, cos, ALU.mult)
        for s in range(2):
            for ax in range(2):
                ins = dve.tensor_tensor(b5[:, :, ax, s, :], x5[:, :, ax, 1 - s, :],
                                        sin[:, ax, s, :].unsqueeze(1).to_broadcast([P, heads, ROPE // 4]), ALU.mult)
        link(ins)
        return dve.tensor_tensor(x, av, bv, ALU.add)

    qt, kt = (k.scr[:, o:o + 768].rearrange("p (h n) -> p h n", h=HEADS_A) for o in (0, 768))
    for t in range(NT):
        if t < T:
            if t < LT:
                dve.wait_ge(*k.sig("psum_read_by_scalar").at(("q", l, t)))
                rope(qt[:, :, NOPE:QK], HEADS_A, k.scr[:, 1536:1792], k.scr[:, 1792:2048], t).then_inc(*k.sig("q_roped").tick((l, t)))
        kr = k.tokv(C_KR, C_KR + ROPE)[:, t:t + 1, :]
        if t < LT:
            link(rope(kr, 1, k.scr[:, 2048:2080], k.scr[:, 2080:2112], t))
        if t:
            dve.wait_ge(*k.full(("kT", l, t - 1)))
        dve.tensor_copy(kt[:, :, NOPE:QK], kr.to_broadcast([P, HEADS_A, ROPE])).then_inc(*k.sig("k_roped").tick((l, t)))
        if t < T:
            key = ("qT", l, t)
            dve.wait_ge(*k.full(key))
            dve.tensor_copy(k.mla(0)[:, :, t * P:(t + 1) * P], k.slot(key)[0:QK, :].rearrange("p (h t) -> p h t", h=HEADS_A)).then_inc(*read.tick(key))
    turns = [(hd, t) for hd in range(HEADS_A) for t in range(T)]
    for n in range(len(turns) + 1):
        if n < len(turns):
            hd, t = turns[n]
            key = ("score", l, hd, t)
            a, b = (0, 768) if t < LT else (512, 768)
            mx = small[:, SM_MAX + n % 4:SM_MAX + n % 4 + 1]
            dve.wait_ge(*k.full(key))
            if n >= 4:
                dve.wait_ge(*k.sig("psum_read_by_scalar").at(("score", l) + turns[n - 4]))
            dve.tensor_reduce(mx, k.slot(key)[:, a:b], AX.X, ALU.max, negate=True).then_inc(*read.tick(key))
            dve.wait_ge(*read.at(key))
            dve.tensor_scalar(mx, mx, SCALE, None, ALU.mult).then_inc(*k.sig("max_ready").tick(key))
        if n:
            hd, t = turns[n - 1]
            i = (n - 1) % 4
            a, b = (0, 768) if t < LT else (512, 768)
            dve.wait_ge(*k.sig("psum_read_by_scalar").at(("score", l, hd, t)))
            if n >= 5:
                dve.wait_ge(*k.sig("psum_read_by_scalar").at(("pv", l) + turns[n - 5]))
            dve.reciprocal(small[:, SM_INV + i:SM_INV + i + 1], small[:, SM_SUM + i:SM_SUM + i + 1]).then_inc(*k.sig("sum_inverted").tick(("score", l, hd, t)))
            key = ("probT", l, hd, t)
            dve.wait_ge(*k.full(key))
            if n >= 3:
                dve.wait_ge(*k.full(("pv", l) + turns[n - 3]))
            o = 1536 + ((n - 1) % 2) * 768
            dve.tensor_copy(k.scr[:, o + a:o + b], k.slot(key)[:, a:b]).then_inc(*read.tick(key))


def vector_post_mixer(k, dve, l, link, statistics, normalise):
    T = ROWS_PER_LAYER[l]
    read = k.sig("psum_read_by_vector")
    dve.wait_ge(*k.sig("norm_rows_loaded").at(l))
    dve.wait_ge(*k.sig("psum_read_by_scalar").at(("row", l, R_G2C)))

    def logits(t):
        key = ("logit", l, t)
        dve.wait_ge(*k.full(key))
        dve.tensor_tensor(k.logits[:, 36 * t:36 * t + 36], k.slot(key)[:, 0:36], k.router_b(), ALU.add).then_inc(*read.tick(key))

    ctx = lambda t: t >= LT
    z = lambda t: k.w[:, 20480 + (t % 2) * D:20480 + (t % 2 + 1) * D]

    def gated(t):
        key = ("out", l, t)
        g = k.w[:, 18432 + (t % 2) * D:18432 + (t % 2 + 1) * D]
        dve.wait_ge(*k.full(key))
        dve.tensor_tensor(g, k.slot(key), k.row(R_G1C if ctx(t) else R_G1L), ALU.mult).then_inc(*read.tick(key))
        dve.wait_ge(*read.at(key))
        link(dve.scalar_tensor_tensor(k.x[:, t, :], k.x[:, t, :], ALPHA, g, ALU.mult, ALU.add))
        statistics(("post1", l, t), t)

    def normed(t):
        x = k.x[:, t, :]
        link(normalise(x, ("post1", l, t), t))
        link(dve.tensor_tensor(x, x, k.row(R_LN1G), ALU.mult))
        link(dve.tensor_tensor(x, x, k.row(R_LN1B), ALU.add))
        statistics(("h2", l, t), t)

    def modulated(t):
        if t >= 2:
            dve.wait_ge(*k.full(("h2", l, t - 2)))
            dve.wait_ge(*k.sig("h2_stored%d" % (t % 2)).at((l, t - 2)))
        link(normalise(z(t), ("h2", l, t), t))
        link(dve.tensor_tensor(z(t), z(t), k.row(R_SC2C if ctx(t) else R_SC2L), ALU.mult))
        dve.tensor_tensor(z(t), z(t), k.row(R_SH2C if ctx(t) else R_SH2L), ALU.add).then_inc(*k.sig("h2_ready").tick((l, t)))

    for n in range(T + 2):
        if n >= 2:
            modulated(n - 2)
        if n < T:
            gated(n)
        if 1 <= n <= T:
            normed(n - 1)
        if n >= 2:
            logits(n - 2)


RI_SLOT, RI_TABLE, RI_TURNS, RI_ROWS, RI_NOW = 96, 112, 156, 160, 208
BIG = 1e30


def vector_route(k, dve, l, link):
    T = ROWS_PER_LAYER[l]
    read = k.sig("psum_read_by_vector")
    f, ri = k.feat, k.routei
    gl, gm = (f[:, o:o + 48].rearrange("p (t n) -> p t n", t=NT)[:, 0:T, :] for o in (576, 624))
    eg = f[:, 672:672 + 4 * T].rearrange("p (t n) -> p t n", t=T)
    le = f[:, 704:896].rearrange("p (t n) -> p t n", t=NT)[:, 0:T, :]
    ev = f[:, 896:944].rearrange("p (t n) -> p t n", t=NT)[:, 0:T, :]
    gi, ei = (ri[:, o:o + 48].rearrange("p (t n) -> p t n", t=NT)[:, 0:T, :] for o in (0, 48))
    gf = f[:, 944:944 + T]
    ef = f[:, 952:952 + 2 * T].rearrange("p (t j) -> p t j", j=2)
    mg, ng = (f[:, o:o + 4 * T].rearrange("p (t n) -> p t n", t=T) for o in (968, 992))
    total, e2, inv = f[:, 1152:1152 + T], f[:, 1160:1160 + T], f[:, 1168:1168 + T]
    nb, pend, base = f[:, 1184:1216], f[:, 1216:1248], f[:, 1248:1280]
    place, prod = (f[:, o:o + 192].rearrange("p (t e) -> p t e", t=NT)[:, 0:T, :] for o in (1280, 1472))
    rows = f[:, 1664:1664 + 2 * NT]
    lg = k.logits[:, :].rearrange("p (t n) -> p t n", t=NT)[:, 0:T, :]
    iota = k.c("iota")[:, 0:NE]
    dve.wait_ge(*read.at(("logit", l, T - 1)))
    dve.memset(gl[:, :, NG:8], -BIG)
    link(dve.tensor_copy(gl[:, :, 0:NG], lg[:, :, 0:NG]))
    for t in range(T):
        ins = dve.max(gm[:, t, :], gl[:, t, :])
    link(ins)
    dve.tensor_tensor(eg, lg[:, :, 0:NG], gm[:, :, 0:1].to_broadcast([P, T, NG]), ALU.subtract).then_inc(*k.sig("group_logits_ready").tick(l))
    for t in range(T):
        ins = dve.max_index(gi[:, t, :], gm[:, t, :], gl[:, t, :])
    link(ins)
    link(dve.tensor_copy(gf, gi[:, :, 0]))
    link(dve.tensor_tensor(mg, iota[:, 0:NG].unsqueeze(1).to_broadcast([P, T, NG]), gf.unsqueeze(2).to_broadcast([P, T, NG]), ALU.is_equal))
    dve.tensor_scalar(ng, mg, BIG, -BIG, ALU.mult, ALU.add)
    le4, shape = le.rearrange("p t (g e) -> p t g e", g=NG), [P, T, NG, EPG]
    link(dve.tensor_tensor(le4, lg[:, :, NG:].rearrange("p t (g e) -> p t g e", g=NG), mg.unsqueeze(3).to_broadcast(shape), ALU.mult))
    link(dve.tensor_tensor(le4, le4, ng.unsqueeze(3).to_broadcast(shape), ALU.add))
    for t in range(T):
        ins = dve.max(ev[:, t, :], le[:, t, :])
    link(ins)
    dve.tensor_tensor(e2, ev[:, :, 1], ev[:, :, 0], ALU.subtract).then_inc(*k.sig("second_minus_first").tick(l))
    for t in range(T):
        ins = dve.max_index(ei[:, t, :], ev[:, t, :], le[:, t, :])
    link(ins)
    link(dve.tensor_copy(ef, ei[:, :, 0:2]))
    for j in range(2):
        ins = dve.tensor_tensor(k.choices(j)[:, 0:T, :], iota.unsqueeze(1).to_broadcast([P, T, NE]), ef[:, :, j:j + 1].to_broadcast([P, T, NE]), ALU.is_equal)
    link(ins)
    dve.tensor_tensor(k.choices(2)[:, 0:T, :], k.choices(0)[:, 0:T, :], k.choices(1)[:, 0:T, :], ALU.add).then_inc(*k.sig("choices_ready").tick(l))
    dve.wait_ge(*k.sig("group_exp").at(l))
    link(dve.tensor_reduce(total, eg, AX.X, ALU.add))
    dve.wait_ge(*k.sig("second_exp").at(l))
    link(dve.tensor_scalar(inv, e2, 1.0, None, ALU.add))
    link(dve.tensor_tensor(inv, inv, total, ALU.mult))
    link(dve.reciprocal(k.gates[:, 0:T], inv))
    dve.tensor_tensor(k.gates[:, NT:NT + T], k.gates[:, 0:T], e2, ALU.mult)
    key = ("rank", l)
    dve.wait_ge(*k.full(key))
    rank, count = k.slot(key)[:, 0:T * 32].rearrange("p (t e) -> p t e", t=T), k.slot(key)[:, 512:544]
    link(dve.tensor_scalar(nb, count, 0.0, None, ALU.is_gt))
    for n in range(1, T):
        link(dve.scalar_tensor_tensor(nb, count, float(P * n), nb, ALU.is_gt, ALU.add))
    link(dve.tensor_tensor_scan(pend, k.c("ones")[:, 0:NE], nb, 0.0, ALU.mult, ALU.add))
    link(dve.tensor_tensor(base, pend, nb, ALU.subtract))
    link(dve.tensor_scalar(base, base, float(P), None, ALU.mult))
    dve.tensor_tensor(place, rank, base.unsqueeze(1).to_broadcast([P, T, NE]), ALU.add).then_inc(*read.tick(key))
    dve.wait_ge(*read.at(key))
    for j in range(2):
        link(dve.tensor_tensor(prod, k.choices(j)[:, 0:T, :], place, ALU.mult))
        link(dve.tensor_reduce(rows[:, NT * j:NT * j + T], prod, AX.X, ALU.add))
        ins = dve.tensor_copy(ri[:, RI_SLOT + NT * j:RI_SLOT + NT * j + T], rows[:, NT * j:NT * j + T])
    link(ins)
    cmp = f[:, 2048:2048 + MAXB * NE].rearrange("p (b e) -> p b e", b=MAXB)
    by, tn, tc = f[:, 1700:1700 + MAXB], f[:, 1760:1784], f[:, 1784:1785]
    link(dve.tensor_tensor(cmp, pend.unsqueeze(1).to_broadcast([P, MAXB, NE]), k.c("block").unsqueeze(2).to_broadcast([P, MAXB, NE]), ALU.is_le))
    link(dve.tensor_reduce(by, cmp, AX.X, ALU.add))
    link(dve.tensor_scalar(by, by, float(NE - 1), None, ALU.min))
    dve.tensor_copy(ri[:, RI_TABLE:RI_TABLE + MAXB], by)
    link(dve.tensor_scalar(tn, k.c("pairs"), pend[:, NE - 1:NE], None, ALU.is_lt))
    link(dve.tensor_reduce(tc, tn, AX.X, ALU.add))
    dve.tensor_copy(ri[:, RI_TURNS:RI_TURNS + 1], tc).then_inc(*k.sig("table_ready").tick(l))
    s = k.scr
    hot = s[:, 0:2 * NT * P].rearrange("p (n r) -> p n r", r=P)
    past, inside, own = (s[:, o:o + 2 * NT * MAXB].rearrange("p (n b) -> p n b", b=MAXB) for o in (1536, 2112, 2688))
    row = s[:, 3264:3264 + 2 * NT]
    for j in range(2):
        a = slice(NT * j, NT * j + T)
        link(dve.tensor_tensor(past[:, a, :], rows[:, a].unsqueeze(2).to_broadcast([P, T, MAXB]),
                               k.c("begin").unsqueeze(1).to_broadcast([P, T, MAXB]), ALU.subtract))
        link(dve.tensor_scalar(own[:, a, :], past[:, a, :], -0.5, None, ALU.is_gt))
        link(dve.scalar_tensor_tensor(inside[:, a, :], past[:, a, :], float(P), own[:, a, :], ALU.is_lt, ALU.mult))
        dve.tensor_tensor(own[:, a, :], inside[:, a, :], k.c("token")[:, 0:T].unsqueeze(2).to_broadcast([P, T, MAXB]), ALU.mult)
        link(dve.tensor_tensor(past[:, a, :], inside[:, a, :], past[:, a, :], ALU.mult))
        link(dve.tensor_reduce(row[:, a], past[:, a, :], AX.X, ALU.add))
        ins = dve.tensor_tensor(hot[:, a, :], k.c("iota").unsqueeze(1).to_broadcast([P, T, P]), row[:, a].unsqueeze(2).to_broadcast([P, T, P]), ALU.is_equal)
    ins.then_inc(*k.sig("row_hots_ready").tick(l))
    dve.wait_ge(*k.full(("rows", l)))
    dve.tensor_copy(ri[:, RI_ROWS:RI_ROWS + MAXB], k.slot(("rows", l))[:, 0:MAXB]).then_inc(*read.tick(("rows", l)))


def pool_program(k, pool):
    io = k.io
    step = k.sig("pool_step")
    cols_in = k.sig("columns_loaded")

    def link(ins):
        ins.then_inc(*step.tick())
        pool.wait_ge(*step.last())

    def col(dst, src):
        pool.dma_start(dst, src, allow_slow_non_contiguous=True)

    def pool_weights(l):
        pool.dma_start(k.poolw().rearrange("p (g d) -> p g d", g=4), io["pool_w"][l].rearrange("g c d -> c g d")).then_inc(*cols_in.tick(l, 16))

    for l in range(DEPTH):
        c = lambda o, n: k.cols[:, 32 * l + o:32 * l + o + n]
        for dst, src in ((k.bmod[:, 48 * l:48 * l + 48], io["b_mod"][l].rearrange("(j p) -> p j", p=P)),
                         (c(K_PS, 2), io["pool_scale"][l].rearrange("(j p) -> p j", p=P)),
                         (c(K_HN, 2), io["hg_norm_g"][l].rearrange("(j p) -> p j", p=P)),
                         (c(K_QN, 2), io["mla_q_norm_g"][l].rearrange("(j p) -> p j", p=P)),
                         (c(K_KN, 1), io["mla_kv_norm_g"][l].rearrange("(j p) -> p j", p=P)),
                         (k.logits[:, 8 * l:8 * l + 8], io["hg_lb_logits"][l].rearrange("r (h p) -> p (r h)", p=P))):
            pool.dma_start(dst, src, allow_slow_non_contiguous=True).then_inc(*cols_in.tick(0, 16))
    pool.memset(k.tok[:, 0:D], 0.0).then_inc(*k.sig("rows_zero").tick())
    pool.wait_ge(*k.sig("rows_zero").at())
    pool_weights(0)
    pool.wait_ge(*k.full(("mod", 0, RING_IN - 1)))
    pool.dma_start(k.y_dram.rearrange("(b p) d -> p b d", p=P)[:, SURE_BLOCKS:MAXB, :],
                   k.tok[:, 0:D].unsqueeze(1).to_broadcast([P, MAXB - SURE_BLOCKS, D])).then_inc(*k.sig("y_cleared").tick(None, 16))
    for l in range(DEPTH):
        T = ROWS_PER_LAYER[l]
        if l:
            pool.wait_ge(*k.sig("moe_done").at(l - 1))
            pool_weights(l)
        gap = k.sig("gap_ready")
        dring = lambda n: k.scr[:, (n % RING_D) * 768:(n % RING_D + 1) * 768].rearrange("p (c t) -> p c t", c=NT)
        pool.wait_ge(*k.sig("head_done").at((l, 2, HEADS_G - 1)))
        for hd in range(HEADS_G):
            xf, xb = (k.prefix(dr)[:, hd] for dr in range(2))
            for m in (0, 3) + tuple(range(4, 18)):
                n = hd * 18 + m
                if n >= RING_D:
                    pool.wait_ge(*decay_end(k, l, n - RING_D))
                d = dring(n)
                if m == 0:
                    ins = pool.tensor_tensor(d, xf[:, :, P:P + 1].to_broadcast([P, NT, P]), xf[:, :, 1:P + 1], ALU.subtract)
                elif m == 3:
                    ins = pool.tensor_tensor(d[:, 0:T, :], xb[:, 0:T, P:P + 1].to_broadcast([P, T, P]), xb[:, 0:T, 0:P], ALU.subtract)
                else:
                    h, dr = LEVELS[(m - 4) // 2], m % 2
                    x = halves(xb[:, 0:T, 0:P] if dr else xf[:, 0:T, 1:P + 1], h)
                    e = halves(d[:, 0:T, :], h)
                    mid = x[:, :, :, h - 1 + dr:h + dr]
                    mid = mid.to_broadcast([P, T, P // (2 * h), h])
                    if dr == 0:
                        pool.tensor_tensor(e[:, :, :, 0:h], mid, x[:, :, :, 0:h], ALU.subtract)
                        ins = pool.tensor_tensor(e[:, :, :, h:2 * h], x[:, :, :, h:2 * h], mid, ALU.subtract)
                    else:
                        pool.tensor_tensor(e[:, :, :, 0:h], mid, x[:, :, :, 0:h], ALU.subtract)
                        ins = pool.tensor_tensor(e[:, :, :, h:2 * h], x[:, :, :, h:2 * h], mid, ALU.subtract)
                ins.then_inc(*gap.tick((l, hd, m)))
        pool.wait_ge(*k.sig("psum_read_by_vector").at(("rows", l)))
        for p in range(2):
            pool.wait_ge(*k.sig("h2_stored%d" % p).at((l, T - 2 + (T + p) % 2)))
        moe_pool(k, pool, l)


def block_turns(k, eng, l):
    return eng.value_load(k.routei[0:1, RI_TURNS:RI_TURNS + 1], min_val=1, max_val=MAXB // 2)


def lsig(k, name, l):
    return k.sig("%s%d" % (name, l), GatherSignal if name.startswith("rows_gathered") else LoopSignal)


def wbuf(k, p, which):
    o = p * 12288 + which * 4096
    return k.w[:, o:o + 4096]


X_ROWS = (0, 1024)
X_T = (2048, 5120)
Y_ROWS = (3072, 4096)
X_SLOT, Y_SLOT = (0, 3), (3, 1)
HID, GATE_EXP, HID_T = (0, 512), (1024, 1536), (2048, 2560)


def moe_sync(k, sp, l):
    io = k.io
    T = ROWS_PER_LAYER[l]
    pe = lsig(k, "moe_tensor", l)
    gu, dn = ([lsig(k, "%s_loaded%d_" % (n, p), l) for p in range(2)] for n in ("gate_up", "down"))
    sp.wait_ge(*k.sig("table_ready").at(l))
    sp.wait_ge(*k.full(("rank", l)))
    for p in range(2):
        sp.wait_ge(*k.sig("h2_stored%d" % p).at((l, T - 2 + (T + p) % 2)))
        sp.sem_inc(gu[p].sem, gu[p].per())
        sp.sem_inc(dn[p].sem, dn[p].per())
    turns = block_turns(k, sp, l)
    with sp.Fori(0, turns) as i:
        expert = [sp.value_load(k.routei[0:1, bass.ds(i * 2 + (RI_TABLE + p), 1)], min_val=0, max_val=NE - 1) for p in range(2)]
        for p, e in enumerate(expert):
            sp.wait_ge(*pe.before(("gate_up", p), i))
            for which, name in ((0, "expert_w1"), (1, "expert_w3")):
                sp.dma_start(wbuf(k, p, which), io[name][l, bass.ds(e, 1)].rearrange("e (p c) n -> p (e c n)", p=P)).then_inc(*gu[p].tick(None, 16))
        for p, e in enumerate(expert):
            sp.wait_ge(*pe.before(("down", p), i))
            sp.dma_start(wbuf(k, p, 2), io["expert_w2"][l, bass.ds(e, 1)].rearrange("e (p c) n -> p (e c n)", p=P)).then_inc(*dn[p].tick(None, 16))
    for s in gu + dn:
        s.close()
    if l == DEPTH - 1:
        for t in range(LT):
            sp.wait_ge(*k.sig("x_ready").at((l, t)))
            sp.dma_start(io["out"][0, t * P:(t + 1) * P, :], k.x[:, t, :]).then_inc(*k.sig("out_stored").tick("all", 16))


def moe_pool(k, pool, l):
    T = ROWS_PER_LAYER[l]
    pe = lsig(k, "moe_tensor", l)
    xin = [lsig(k, "rows_gathered%d_" % p, l) for p in range(2)]
    now = lsig(k, "moe_pool", l)
    pool.sem_inc(now.sem, now.per())
    turns = block_turns(k, pool, l)
    with pool.Fori(0, turns) as i:
        for p in range(2):
            idx = k.routei[:, RI_NOW + p:RI_NOW + p + 1]
            pool.wait_ge(*pe.before(("x", p), i))
            pool.tensor_copy(idx, k.routei[:, bass.ds(i * 2 + (RI_ROWS + p), 1)]).then_inc(*now.tick(p))
            pool.wait_ge(*now.now(p, i))
            pool.sem_inc(*k.sig("gather_turn").tick())
            pool.indirect_dma_start(k.feat[:, X_ROWS[p]:X_ROWS[p] + D], None, k.h_dram[l], bass.IndirectOffsetOnAxis(ap=idx, axis=0)) \
                .then_inc(*xin[p].tick(None, 16))
    for s in xin + [now]:
        s.close()
    for p in range(2):
        s = lsig(k, "y_stored%d_" % p, l)
        pool.wait_ge(s.sem, turns * s.per() + s.per())
    pool.wait_ge(*k.sig("moe_done").at(l))
    pool.sem_inc(*k.sig("gather_turn").tick())
    for t in range(T):
        if t >= 2:
            pool.wait_ge(*k.sig("y_used").at((l, t - 2)))
        for j in range(2):
            i = RI_SLOT + NT * j + t
            n = 2 * (t % 2) + j
            pool.indirect_dma_start(k.feat[:, n * D:(n + 1) * D], None, k.y_dram,
                                    bass.IndirectOffsetOnAxis(ap=k.routei[:, i:i + 1], axis=0)).then_inc(*k.sig("y_gathered%d" % (t % 2)).tick((l, t), 16))


def moe_tensor(k, pe, l):
    ident = k.c("ident")
    sig, act, dve = (lsig(k, n, l) for n in ("moe_tensor", "moe_scalar", "moe_vector"))
    gu, dn = ([lsig(k, "%s_loaded%d_" % (n, p), l) for p in range(2)] for n in ("gate_up", "down"))
    xin = [lsig(k, "rows_gathered%d_" % p, l) for p in range(2)]
    slot = lambda n: k.psum[:, n * 1024:(n + 1) * 1024]
    for key in k.slots[-4:]:
        k.wait_read(pe, key)
    pe.wait_ge(*k.sig("table_ready").at(l))
    pe.sem_inc(sig.sem, sig.per())
    turns = block_turns(k, pe, l)
    with pe.Fori(0, turns) as i:
        for p in range(2):
            pe.wait_ge(*xin[p].now(None, i))
            if p == 0:
                pe.wait_ge(*dve.before(("hid_t", 1), i))
            else:
                for who in (act, dve):
                    pe.wait_ge(*who.before(("y", 0), i))
            x = k.feat[:, X_ROWS[p]:X_ROWS[p] + D].rearrange("p (q c) -> p c q", c=DC)
            for c in range(DC):
                ins = pe.transpose(slot(X_SLOT[p])[:, c * P:(c + 1) * P], x[:, c, :], ident)
            ins.then_inc(*sig.tick(("x", p)))
        for p in range(2):
            pe.wait_ge(*act.now(("x_t", p), i))
            pe.wait_ge(*gu[p].now(None, i))
            pe.wait_ge(*dve.before(("hidden", p), i))
            if p == 0:
                for who in (act, dve):
                    pe.wait_ge(*who.before(("y", 1), i))
            xt = k.feat[:, X_T[p]:X_T[p] + D].rearrange("p (c t) -> p c t", c=DC)
            for which in range(2):
                w = wbuf(k, p, which).rearrange("p (c n) -> p c n", c=DC)
                ins = matmuls(pe, slot(1 + p)[:, which * 512:which * 512 + 512], [(xt[:, c, :], w[:, c, :]) for c in range(DC)])
            ins.then_inc(*sig.tick(("gate_up", p)))

        def hidden_transposed(p):
            pe.wait_ge(*dve.now(("hidden", p), i))
            hid = k.scr[:, HID[p]:HID[p] + DE].rearrange("p (q c) -> p c q", c=EC)
            for c in range(EC):
                ins = pe.transpose(slot(0)[:, p * 512 + c * P:p * 512 + (c + 1) * P], hid[:, c, :], ident)
            ins.then_inc(*sig.tick(("hid_t", p)))

        hidden_transposed(0)
        for p in range(2):
            pe.wait_ge(*dve.now(("hid_t", p), i))
            pe.wait_ge(*dn[p].now(None, i))
            ht = k.scr[:, HID_T[p]:HID_T[p] + DE].rearrange("p (c t) -> p c t", c=EC)
            w = wbuf(k, p, 2).rearrange("p (c n) -> p c n", c=EC)
            for half in range(2):
                for c in range(EC):
                    ins = pe.matmul(slot(Y_SLOT[p])[:, half * 512:half * 512 + 512], ht[:, c, :], w[:, c, half * 512:half * 512 + 512],
                                    start=(c == 0), stop=(c == EC - 1))
                    if (p, half, c) == (0, 1, 1):
                        hidden_transposed(1)
            ins.then_inc(*sig.tick(("down", p)))
    sig.close()
    pe.wait_ge(sig.sem, turns * sig.per() + sig.per())
    pe.sem_inc(*k.sig("moe_done").tick(l))
    for who in (act, dve):
        pe.wait_ge(who.sem, turns * who.per() + who.per())


def moe_scalar(k, act, l):
    sig, pe, dve = (lsig(k, n, l) for n in ("moe_scalar", "moe_tensor", "moe_vector"))
    stored = [lsig(k, "y_stored%d_" % p, l) for p in range(2)]
    slot = lambda n: k.psum[:, n * 1024:(n + 1) * 1024]
    act.wait_ge(*k.sig("table_ready").at(l))
    act.sem_inc(sig.sem, sig.per())
    for p in range(2):
        act.sem_inc(stored[p].sem, stored[p].per())
    turns = block_turns(k, act, l)
    with act.Fori(0, turns) as i:
        for p in range(2):
            act.wait_ge(*pe.now(("x", p), i))
            act.wait_ge(*pe.before(("gate_up", p), i))
            act.copy(k.feat[:, X_T[p]:X_T[p] + D], slot(X_SLOT[p])).then_inc(*sig.tick(("x_t", p)))
        for p in range(2):
            act.wait_ge(*pe.now(("gate_up", p), i))
            act.wait_ge(*dve.before(("hidden", p), i))
            act.activation(k.scr[:, GATE_EXP[p]:GATE_EXP[p] + DE], slot(1 + p)[:, 0:DE], ACT.Exp, scale=-1.0).then_inc(*sig.tick(("exp", p)))
        for p in range(2):
            act.wait_ge(*pe.now(("down", p), i))
            act.wait_ge(*stored[p].before(None, i))
            act.copy(k.feat[:, Y_ROWS[p]:Y_ROWS[p] + 512], slot(Y_SLOT[p])[:, 0:512]).then_inc(*sig.tick(("y", p)))
            act.wait_ge(*sig.now(("y", p), i))
            act.wait_ge(*dve.now(("y", p), i))
            act.dma_start(k.y_dram.rearrange("(b p) d -> p b d", p=P)[:, bass.ds(i * 2 + p, 1), :],
                          k.feat[:, Y_ROWS[p]:Y_ROWS[p] + D].unsqueeze(1)).then_inc(*stored[p].tick(None, 16))
    for s in [sig] + stored:
        s.close()


def moe_vector(k, dve, l):
    sig, pe, act = (lsig(k, n, l) for n in ("moe_vector", "moe_tensor", "moe_scalar"))
    stored = [lsig(k, "y_stored%d_" % p, l) for p in range(2)]
    slot = lambda n: k.psum[:, n * 1024:(n + 1) * 1024]
    dve.sem_inc(sig.sem, sig.per())
    turns = block_turns(k, dve, l)
    with dve.Fori(0, turns) as i:
        for p in range(2):
            g, u = slot(1 + p)[:, 0:DE], slot(1 + p)[:, 512:512 + DE]
            e, h = k.scr[:, GATE_EXP[p]:GATE_EXP[p] + DE], k.scr[:, HID[p]:HID[p] + DE]

            def silu():
                dve.wait_ge(*act.now(("exp", p), i))
                dve.tensor_scalar(e, e, 1.0, None, ALU.add).then_inc(*sig.tick(("one", p)))
                dve.wait_ge(*sig.now(("one", p), i))
                dve.reciprocal(e, e).then_inc(*sig.tick(("inv", p)))
                dve.wait_ge(*sig.now(("inv", p), i))
                dve.wait_ge(*pe.before(("hid_t", p), i))
                dve.tensor_tensor(h, g, e, ALU.mult).then_inc(*sig.tick(("silu", p)))
                dve.wait_ge(*sig.now(("silu", p), i))
                dve.tensor_tensor(h, u, h, ALU.mult).then_inc(*sig.tick(("hidden", p)))

            silu()
            dve.wait_ge(*pe.now(("hid_t", p), i))
            dve.wait_ge(*pe.before(("down", p), i))
            dve.tensor_copy(k.scr[:, HID_T[p]:HID_T[p] + DE], slot(0)[:, p * 512:p * 512 + 512]).then_inc(*sig.tick(("hid_t", p)))
            if p:
                y_copy(k, dve, sig, pe, stored, slot, 0, i)
        y_copy(k, dve, sig, pe, stored, slot, 1, i)
    sig.close()


def y_copy(k, dve, sig, pe, stored, slot, p, i):
    dve.wait_ge(*pe.now(("down", p), i))
    dve.wait_ge(*stored[p].before(None, i))
    dve.tensor_copy(k.feat[:, Y_ROWS[p] + 512:Y_ROWS[p] + D], slot(Y_SLOT[p])[:, 512:1024]).then_inc(*sig.tick(("y", p)))


def build(nc, io, book):
    with ExitStack() as ctx:
        ctx.enter_context(nc.allow_non_contiguous_dma("columns of vectors"))
        k = Kernel(nc, io, book, ctx)
        block = ctx.enter_context(nc.Block())

        @block.tensor
        def _(pe):
            tensor_program(k, pe)

        @block.scalar
        def _(act):
            scalar_program(k, act)

        @block.vector
        def _(dve):
            vector_program(k, dve)

        @block.gpsimd
        def _(pool):
            pool_program(k, pool)

        @block.sync
        def _(sp):
            sync_program(k, sp)


_INS = ["x", "c", "ctx", "c_ctx", "w_mod", "b_mod", "w_in", "pool_w", "pool_scale", "hg_lb_logits", "hg_norm_g",
        "mla_q_norm_g", "mla_w_uq", "mla_kv_norm_g", "mla_w_ukv", "w_out", "ln1_g", "ln1_b", "ln2_g", "ln2_b",
        "router_group_w", "router_group_b", "router_expert_w", "router_expert_b", "expert_w1", "expert_w3", "expert_w2"]


def kernel(**inputs):
    import concourse.bacc as bacc
    from concourse.bass_utils import run_bass_kernel_spmd

    const, masks, bands = shape_constants()
    arrays = {"in_" + n: np.ascontiguousarray(inputs[n]) for n in _INS}
    arrays.update(shape_const=const, shape_masks=masks, shape_bands=bands)
    book = {}
    for _ in range(2):
        nc = bacc.Bacc("TRN2", target_bir_lowering=False, num_devices=1)
        io = {n.removeprefix("in_"): nc.dram_tensor(n, a.shape, mybir.dt.from_np(a.dtype), kind="ExternalInput").ap()
              for n, a in arrays.items()}
        io["out"] = nc.dram_tensor("out", (1, SEQ, D), F32, kind="ExternalOutput").ap()
        build(nc, io, book)
    r = run_bass_kernel_spmd(nc, [arrays], core_ids=[0])
    return r.results[0]["out"]
```

```python
from contextlib import ExitStack

import numpy as np
import concourse.bass as bass
from concourse import mybir

F32 = mybir.dt.float32
U8 = mybir.dt.uint8
U32 = mybir.dt.uint32
I32 = mybir.dt.int32
ALU = mybir.AluOpType
ACT = mybir.ActivationFunctionType
AX = mybir.AxisListType

P = 128
D = 1024
DC = D // P
SEQ, CTX, DEPTH = 512, 256, 2
LT, CT = SEQ // P, CTX // P
NT = LT + CT
WINDOWS = (2, 4, 8, 16)
HEADS_G, DV_G = 4, 64
HEADS_A, NOPE, ROPE, DV_A = 8, 64, 32, 64
QK = NOPE + ROPE
SCALE = QK ** -0.5
GRID_W, ROPE_BASE = 64, 10000.0
NG, EPG, NE = 4, 8, 32
DE = D // 2
EC = DE // P
ALPHA = (2 * DEPTH) ** 0.25
EPS = 1e-6
LEVELS = (64, 32, 16, 8, 4, 2, 1)
MAXB = 44
SURE_BLOCKS = 2 * LT
ROWS_PER_LAYER = (NT, LT)
Z_MIN = -41.0

C_P, C_V, C_G, C_CQ, C_CKV, C_KR, TOKW = 0, 256, 512, 768, 1024, 1152, 1184
I_P, I_Q, I_ZF, I_ZB, I_V, I_CQ, IN_DIM = 0, 256, 768, 1280, 1792, 2304, 2720
SH1, SC1, G1, SH2, SC2, G2 = range(6)

CONST = {}
for _name, _n in (("ident", 128), ("before", 128), ("ones", 128), ("cos", LT * ROPE), ("sin", LT * ROPE),
                  ("iota", 128), ("pairs", 24), ("block", MAXB), ("begin", MAXB), ("token", NT), ("eps", 1)):
    CONST[_name] = (sum(n for _, n in CONST.values()), _n)
CONSTW = sum(n for _, n in CONST.values())


def shape_constants():
    c = np.zeros((P, CONSTW), np.float32)

    def put(name, a):
        o, n = CONST[name]
        c[:, o:o + n] = a

    i = np.arange(P)
    put("ident", np.eye(P))
    put("before", (i[:, None] < i[None, :]))
    put("ones", 1.0)
    t = np.arange(SEQ)
    inv = ROPE_BASE ** (-np.arange(ROPE // 4, dtype=np.float32) / np.float32(ROPE // 4))
    ang = np.stack([(t // GRID_W).astype(np.float32)[:, None] * inv, (t % GRID_W).astype(np.float32)[:, None] * inv], 1)
    cos, sin = np.cos(ang, dtype=np.float32), np.sin(ang, dtype=np.float32)
    cos = np.stack([cos, cos], 2).reshape(LT, P, ROPE)
    sin = np.stack([-sin, sin], 2).reshape(LT, P, ROPE)
    put("cos", cos.transpose(1, 0, 2).reshape(P, -1))
    put("sin", sin.transpose(1, 0, 2).reshape(P, -1))
    put("iota", np.arange(P))
    put("pairs", 2.0 * np.arange(24))
    put("block", np.arange(MAXB))
    put("begin", P * np.arange(MAXB))
    put("token", i[:, None] + P * np.arange(NT)[None, :])
    put("eps", EPS)
    s, u = i[:, None], i[None, :]
    m = [(s // (2 * h) == u // (2 * h)) & (s % (2 * h) < h) & (u % (2 * h) >= h) for h in LEVELS]
    masks = np.stack([a for x in m for a in (x, x.T)], 1).astype(np.float32).reshape(P, -1)
    bands = []
    for w in WINDOWS:
        n = 3 * P
        tt, ss = np.arange(n), np.arange(n)
        lo, hi = np.clip(tt - w // 2, 0, n), np.clip(tt + w // 2, 0, n)
        a = ((ss[:, None] >= lo) & (ss[:, None] < hi)) / (hi - lo).astype(np.float32)
        a = a - np.eye(n)
        b = a.reshape(3, P, 3, P)
        bands += [b[0, :, 0], b[1, :, 1], b[2, :, 2], b[0, :, 1], b[1, :, 0]]
    bands = np.stack(bands, 1).astype(np.float32).reshape(P, -1)
    return c, np.ascontiguousarray(masks), np.ascontiguousarray(bands)


class Signal:

    def __init__(self, sem, name, book, scope=None):
        self.sem, self.name, self.book, self.count = sem, name, book, 0

    def tick(self, key=None, by=1):
        self.count += by
        self.book[self.name, key] = self.count
        return self.sem, by

    def at(self, key=None):
        return self.sem, self.book.get((self.name, key), 1)

    def last(self):
        return self.sem, self.count


class LoopSignal(Signal):

    def per(self):
        return self.book.get((self.name, "per turn"), 16)

    def close(self):
        self.book[self.name, "per turn"] = self.count

    def now(self, key, i):
        return self.sem, i * self.per() + (self.per() + self.book.get((self.name, key), 1))

    def before(self, key, i):
        return self.sem, i * self.per() + self.book.get((self.name, key), 1)

    def latest(self, i):
        return self.sem, i * self.per() + (self.per() + self.count)


class GatherSignal(LoopSignal):

    def now(self, key, i):
        return self.sem, i * self.per() + self.book.get((self.name, key), 1)


class Kernel:

    def __init__(self, nc, io, book, ctx):
        self.nc, self.io, self.book = nc, io, book
        sb = lambda name, n, dt=F32: ctx.enter_context(nc.sbuf_tensor(name, [P, n], dt))
        self.x = sb("x", NT * D)[:, :].rearrange("p (t d) -> p t d", t=NT)
        self.feat = sb("feat", DC * NT * P)
        self.w = sb("w", 24576)
        self.tok = sb("tok", NT * TOKW)
        self.scr = sb("scr", 6144)
        self.const = sb("const", CONSTW)
        self.masks = sb("masks", 2 * len(LEVELS) * P, U8)
        self.cvec = sb("cvec", DC * 2)
        self.modc = sb("modc", 48 * 2 * DEPTH)
        self.bmod = sb("bmod", 48 * DEPTH)
        self.cols = sb("cols", 32 * DEPTH)
        self.stats = sb("stats", 64)
        self.small = sb("small", 160)
        self.logits = sb("logits", NT * 36)
        self.gates = sb("gates", 2 * NT)
        self.routei = sb("routei", 256, U32)
        self.psum = ctx.enter_context(nc.psum_tensor("psum", [P, 4096], F32))
        self.h_dram = [nc.dram_tensor(f"h_rows{l}", (ROWS_PER_LAYER[l] * P, D), F32, kind="Internal").ap() for l in range(DEPTH)]
        self.y_dram = nc.dram_tensor("y_rows", (MAXB * P, D), F32, kind="Internal").ap()
        self.signals = {}
        self.ctx = ctx
        self.slots = []

    def sig(self, name, kind=Signal):
        if name not in self.signals:
            self.signals[name] = kind(self.ctx.enter_context(self.nc.semaphore(name)), name, self.book)
        return self.signals[name]

    def c(self, name):
        o, n = CONST[name]
        return self.const[:, o:o + n]

    def open_slot(self, pe, key):
        n = len(self.slots)
        self.slots.append(key)
        self.book["slot", key] = n % 4
        if n >= 4:
            self.wait_read(pe, self.slots[n - 4])
        return self.slot(key)

    def wait_read(self, pe, key):
        for who in ("psum_read_by_scalar", "psum_read_by_vector"):
            if (who, key) in self.book:
                pe.wait_ge(*self.sig(who).at(key))

    def slot(self, key):
        s = self.book.get(("slot", key), 0)
        return self.psum[:, s * 1024:(s + 1) * 1024]

    def full(self, key):
        return self.sig("psum_full").at(key)

    def ring(self, n, cols=512):
        return self.w[:, (n % 2) * 4096:(n % 2) * 4096 + DC * cols].rearrange("p (c n) -> p c n", c=DC)

    def feat_c(self, c, a, b):
        return self.feat[:, c * NT * P + a:c * NT * P + b]

    def hg(self, which):
        o = 8192 + 3072 * which
        return self.w[:, o:o + 3072].rearrange("p (h t) -> p h t", h=HEADS_G)

    def prefix(self, which):
        o = 8192 + 9216 + which * 3096
        return self.w[:, o:o + 3096].rearrange("p (h c t) -> p h c t", h=HEADS_G, c=NT)

    def tokv(self, a, b):
        return self.tok[:, :].rearrange("p (t n) -> p t n", t=NT)[:, :, a:b]

    def row(self, n):
        return self.scr[:, n * D:(n + 1) * D] if n < 6 else self.tok[:, (n - 6) * D:(n - 5) * D]

    def mla(self, which):
        o = 8192 + 6144 * which
        return self.w[0:QK, o:o + 6144].rearrange("p (h t) -> p h t", h=HEADS_A)

    def poolw(self):
        return self.w[0:64, 23680:23936]

    def router_w(self):
        return self.tok[:, 6144:6432].rearrange("p (c n) -> p c n", c=DC)

    def router_b(self):
        return self.tok[:, 6432:6468]

    def choices(self, n):
        return self.feat[:, n * 192:(n + 1) * 192].rearrange("p (t e) -> p t e", t=NT)

    def mod(self, l):
        return self.modc[:, 96 * l:96 * l + 96].rearrange("p (j s) -> p j s", s=2)

    def mod_row(self, n):
        return self.scr[0:2, 5632:6144] if n % 2 else self.feat[0:2, 2304:2816]

    def gate_exp(self, t):
        return self.scr[:, 5632 + 256 * (t % 2):5888 + 256 * (t % 2)]

    def expert_rows(self, t, j):
        o = 12288 + (2 * (t % 2) + j) * D
        return self.w[:, o:o + D]

    def latent(self):
        return self.w[:, 20480:22784].rearrange("p (c t) -> p c t", c=3)


R_G1L, R_LN1G, R_LN1B, R_G1C, R_SC2L, R_SH2L, R_SC2C, R_SH2C, R_G2L, R_G2C, R_LN2G, R_LN2B = range(12)
MOD_ROWS = ((R_G1L, G1, 0), (R_G1C, G1, 1), (R_SC2L, SC2, 0), (R_SH2L, SH2, 0), (R_SC2C, SC2, 1), (R_SH2C, SH2, 1),
            (R_G2L, G2, 0), (R_G2C, G2, 1))


def mod_rows(l):
    return [r for r in MOD_ROWS if r[2] == 0 or ROWS_PER_LAYER[l] == NT]


K_PS, K_HN, K_QN, K_KN, K_LB, K_OML, K_IND = 0, 2, 4, 6, 8, 16, 24
TURNS = ((4, 5, 0, 1, 2, 3), (5, 4, 3, 2, 1, 0))


RING_MOD, RING_IN, RING_OUT, RING_N = 0, 12, 18, 20
RING_EARLY = 4
MOD_DURING = [[(_l, n) for n in range(RING_EARLY, RING_IN)] + [(_l + 1, n) for n in range(RING_EARLY) if _l + 1 < DEPTH]
              for _l in range(DEPTH)]
MOD_ORDER = [(0, n) for n in range(RING_EARLY)] + sum(MOD_DURING, [])
RING_ORDER = [(0, n) for n in range(RING_EARLY)]
for _l in range(DEPTH):
    RING_ORDER += [(_l, n) for n in range(RING_IN, RING_OUT)] + MOD_DURING[_l] + [(_l, n) for n in range(RING_OUT, RING_N)]
MOD_LEVELS = ((2, 7, 12), (3, 10))
RING_PAST_BANDS = 4
HG_ORDER = (4, 5, 6, 0, 7, 1, 8, 2, 9, 3) + tuple(range(10, 18))
HG_ITEMS = [(_h, _m) for _h in range(HEADS_G) for _m in HG_ORDER]
LEVEL_LAG = 2
KEY_LAG = 3
HG_LATE = 1
RING_D = 7


def mod_item(l, hd, level):
    if level in MOD_LEVELS[l]:
        return MOD_DURING[l][len(MOD_LEVELS[l]) * hd + MOD_LEVELS[l].index(level)]
    return None


def mod_before(item, n=1):
    place = MOD_ORDER.index(item) - n
    return MOD_ORDER[place] if place >= 0 else None
IN_SLICES = ((I_Q, 512), (I_ZF, 512), (I_ZB, 512), (I_P, 256), (I_V, 512), (I_CQ, 416))


def last_reader(l, n):
    if n < RING_IN:
        return ("mod", l, n)
    if n < RING_OUT:
        s = n - RING_IN
        if s < 3:
            return ("proj", l, s, 3)
        return ("proj", l, s, (ROWS_PER_LAYER[l] if s == 3 else NT) - 1)
    return ("out", l, ROWS_PER_LAYER[l] - 1)


def sync_program(k, sp):
    io, nc = k.io, k.nc
    first = k.sig("first_loads")
    sp.dma_start(k.const[:, :], io["shape_const"]).then_inc(*first.tick("const", 16))
    for s, name in enumerate(("c", "c_ctx")):
        src = io[name] if s else io[name][0, :]
        sp.dma_start(k.cvec[:, :].rearrange("p (c s) -> p c s", s=2)[:, :, s], src.rearrange("(c p) -> p c", p=P),
                     allow_slow_non_contiguous=True).then_inc(*first.tick("c", 16))
    sp.dma_start(k.scr[:, 3072:3072 + 2 * len(LEVELS) * P], io["shape_masks"]).then_inc(*first.tick("masks", 16))
    ring_in = [k.sig("ring0_loaded"), k.sig("ring1_loaded")]
    x_in = k.sig("x_loaded")

    def load_ring(l, n):
        place = RING_ORDER.index((l, n))
        if l and n in (RING_IN, RING_IN + 1):
            sp.wait_ge(*k.sig("moe_done").at(l - 1))
            sp.wait_ge(*k.sig("y_gathered0").at((l - 1, 2)))
        elif place >= 2:
            sp.wait_ge(*k.full(last_reader(*RING_ORDER[place - 2])))
        if n < RING_IN:
            src, a, w = io["w_mod"][l], 512 * n, 512
        elif n < RING_OUT:
            src, (a, w) = io["w_in"][l], IN_SLICES[n - RING_IN]
        else:
            src, a, w = io["w_out"][l], 512 * (n - RING_OUT), 512
        sp.dma_start(k.ring(n, w), src.rearrange("(c p) n -> p c n", p=P)[:, :, a:a + w]) \
          .then_inc(*ring_in[n % 2].tick((l, n), 16))

    for l in range(DEPTH):
        if l == 0:
            for n in range(2):
                load_ring(l, n)
            sp.dma_start(k.x[:, 0:LT, :], io["x"][0].rearrange("(t p) d -> p t d", p=P)).then_inc(*x_in.tick(None, 16))
            sp.dma_start(k.x[:, LT:NT, :], io["ctx"][0].rearrange("(t p) d -> p t d", p=P)).then_inc(*x_in.tick(None, 16))
            for n in range(2, RING_EARLY):
                load_ring(l, n)
        for n in range(RING_IN, RING_IN + 2):
            load_ring(l, n)
        sp.wait_ge(*k.sig("psum_read_by_scalar").at(("h", l, 0)))
        sp.dma_start(k.scr[:, 3072:3072 + 20 * P], io["shape_bands"]).then_inc(*k.sig("bands_loaded").tick(l, 16))
        for n in range(RING_IN + 2, RING_OUT):
            load_ring(l, n)
        for item in MOD_DURING[l]:
            load_ring(*item)
        sp.wait_ge(*k.full(("level", l, HEADS_G - 1, 2 * len(LEVELS) - 1)))
        mla_w = k.sig("mla_weights_loaded")
        sp.dma_start(k.scr[:, 3072:4608].rearrange("p (c n) -> p c n", c=2),
                     io["mla_w_uq"][l].rearrange("(c p) n -> p c n", p=P)).then_inc(*mla_w.tick(l, 16))
        sp.dma_start(k.scr[:, 4608:5632], io["mla_w_ukv"][l]).then_inc(*mla_w.tick(l, 16))
        for n in range(RING_OUT, RING_N):
            load_ring(l, n)
        rows = k.sig("norm_rows_loaded")
        sp.wait_ge(*k.sig("psum_read_by_scalar").at(("mixed", l, ROWS_PER_LAYER[l] - 1)))
        for r, name in ((R_LN1G, "ln1_g"), (R_LN1B, "ln1_b"), (R_LN2G, "ln2_g"), (R_LN2B, "ln2_b")):
            sp.dma_start(k.row(r), io[name][l].partition_broadcast(P)).then_inc(*rows.tick(l, 16))
        for name, n, o in (("router_group_w", NG, 0), ("router_expert_w", NE, NG)):
            sp.dma_start(k.router_w()[:, :, o:o + n], io[name][l].rearrange("(c p) n -> p c n", p=P)).then_inc(*rows.tick(l, 16))
        for name, n, o in (("router_group_b", NG, 0), ("router_expert_b", NE, NG)):
            sp.dma_start(k.router_b()[:, o:o + n], io[name][l].partition_broadcast(P)).then_inc(*rows.tick(l, 16))
        for t in range(ROWS_PER_LAYER[l]):
            sp.wait_ge(*k.sig("h2_ready").at((l, t)))
            sp.dma_start(k.h_dram[l][t * P:(t + 1) * P, :], k.w[:, 20480 + (t % 2) * D:20480 + (t % 2 + 1) * D]) \
              .then_inc(*k.sig("h2_stored%d" % (t % 2)).tick((l, t), 16))
        moe_sync(k, sp, l)
    for s in ("out_stored",):
        sp.wait_ge(*k.sig(s).at("all"))


def matmuls(pe, out, pairs):
    for n, (a, b) in enumerate(pairs):
        ins = pe.matmul(out, a, b, start=(n == 0), stop=(n == len(pairs) - 1))
    return ins


def tensor_program(k, pe):
    full = k.sig("psum_full")
    ident = k.c("ident")
    ring_in = [k.sig("ring0_loaded"), k.sig("ring1_loaded")]
    pe.wait_ge(*k.sig("first_loads").at("masks"))
    for l in range(DEPTH):
        T = ROWS_PER_LAYER[l]
        if l == 0:
            pe.wait_ge(*k.sig("c_ready").at())
            for n in range(RING_EARLY + 1):
                if n < RING_EARLY:
                    tensor_mod(k, pe, l, n)
                if n:
                    tensor_mod_columns(k, pe, l, n - 1)
        def transposed(t):
            ps = k.open_slot(pe, ("h", l, t))
            pe.wait_ge(*k.sig("z_ready").at((l, t)))
            z = k.scr[:, (t % 2) * D:(t % 2 + 1) * D]
            for c in range(DC):
                ins = pe.transpose(ps[:, c * P:(c + 1) * P], z[:, c * P:(c + 1) * P], ident)
            ins.then_inc(*full.tick(("h", l, t)))

        ahead = LT if T == LT else NT
        for t in range(ahead):
            transposed(t)
        for s in range(3):
            n = RING_IN + s
            pe.wait_ge(*ring_in[n % 2].at((l, n)))
            w = k.ring(n)
            cuts = ((0, 512), (512, 768)) if s or T == NT else ((0, 512),)
            for hd in range(HEADS_G):
                ps = k.open_slot(pe, ("proj", l, s, hd))
                if s == 0 and hd == 0:
                    k.wait_read(pe, ("h", l, ahead - 1))
                if s == 1 and hd == 0:
                    k.wait_read(pe, ("h", l, NT - 1))
                for a, b in cuts:
                    ins = matmuls(pe, ps[:, a:b], [(w[:, c, hd * P:(hd + 1) * P], k.feat_c(c, a, b)) for c in range(DC)])
                ins.then_inc(*full.tick(("proj", l, s, hd)))
                if s == 0 and ahead + hd < NT:
                    transposed(ahead + hd)
        for s in range(3, 6):
            n = RING_IN + s
            pe.wait_ge(*ring_in[n % 2].at((l, n)))
            width = IN_SLICES[s][1]
            w = k.ring(n, width)
            for t in range(T if s == 3 else NT):
                ps = k.open_slot(pe, ("proj", l, s, t))
                a, b = token_cut(l, s, t)
                ins = matmuls(pe, ps[:, a:b], [(k.feat_c(c, t * P, (t + 1) * P), w[:, c, a:b]) for c in range(DC)])
                ins.then_inc(*full.tick(("proj", l, s, t)))
        pe.wait_ge(*k.sig("bands_loaded").at(l))
        band = k.scr[:, 3072:3072 + 20 * P].rearrange("p (b t) -> p b t", t=P)
        for g in range(4):
            ps = k.open_slot(pe, ("pool", l, g))
            if g == 0:
                k.wait_read(pe, ("proj", l, 3, T - 1))
            for t in range(T):
                lo, hi = (0, LT - 1) if t < LT else (LT, NT - 1)
                blocks = [(t, 0 if t == lo else 2 if t == hi else 1)]
                blocks += [(t - 1, 3)] if t > lo else []
                blocks += [(t + 1, 4)] if t < hi else []
                ins = matmuls(pe, ps[0:64, t * P:(t + 1) * P],
                              [(k.tokv(64 * g, 64 * g + 64)[:, s, :], band[:, 5 * g + b, :]) for s, b in blocks])
            ins.then_inc(*full.tick(("pool", l, g)))
        pooled = k.feat[0:64, 3072:6144].rearrange("p (g t) -> p g t", g=4)
        for j in range(2):
            ps = k.open_slot(pe, ("poolout", l, j))
            if j == 0:
                k.wait_read(pe, ("pool", l, 3))
                pe.wait_ge(*k.sig("columns_loaded").at(l))
            for g in (2 * j, 2 * j + 1):
                for a, b in ((0, 512), (512, 768))[:1 + (T == NT)]:
                    ins = matmuls(pe, ps[64 * (g % 2):64 * (g % 2) + 64, a:b], [(k.poolw()[:, 64 * g:64 * g + 64], pooled[:, g, a:b])])
            ins.then_inc(*full.tick(("poolout", l, j)))
        tensor_hgrn(k, pe, l)
        tensor_attention(k, pe, l)
        pe.wait_ge(*k.sig("mod_ready").at((l, "late")))
        m = k.mod(l)
        for r, v, s in mod_rows(l):
            ps = k.open_slot(pe, ("row", l, r))
            for c in range(DC):
                ins = pe.matmul(ps[:, c * P:(c + 1) * P], m[:, v * DC + c, s:s + 1].to_broadcast([P, P]), ident, start=True, stop=True)
            ins.then_inc(*full.tick(("row", l, r)))
        for n in (RING_OUT, RING_OUT + 1):
            pe.wait_ge(*ring_in[n % 2].at((l, n)))
        for n in range(T + 2):
            if n < T:
                ps = k.open_slot(pe, ("out", l, n))
                if n == 0:
                    k.wait_read(pe, ("mixed", l, T - 1))
                for half in range(2):
                    w = k.ring(RING_OUT + half)
                    ins = matmuls(pe, ps[:, half * 512:half * 512 + 512],
                                  [(k.feat_c(c, n * P, (n + 1) * P), w[:, c, :]) for c in range(DC)])
                ins.then_inc(*full.tick(("out", l, n)))
            if n >= 2:
                t = n - 2
                ps = k.open_slot(pe, ("logit", l, t))
                k.wait_read(pe, ("h2", l, t))
                h2t = k.w[:, 22528 + (t % 2) * D:22528 + (t % 2 + 1) * D].rearrange("p (c t) -> p c t", c=DC)
                rw = k.router_w()
                ins = matmuls(pe, ps[:, 0:36], [(h2t[:, c, :], rw[:, c, :]) for c in range(DC)])
                ins.then_inc(*full.tick(("logit", l, t)))
            if 1 <= n <= T:
                t = n - 1
                ps = k.open_slot(pe, ("h2", l, t))
                pe.wait_ge(*k.sig("h2_ready").at((l, t)))
                z = k.w[:, 20480 + (t % 2) * D:20480 + (t % 2 + 1) * D]
                for c in range(DC):
                    ins = pe.transpose(ps[:, c * P:(c + 1) * P], z[:, c * P:(c + 1) * P], ident)
                ins.then_inc(*full.tick(("h2", l, t)))
        ps = k.open_slot(pe, ("rank", l))
        pe.wait_ge(*k.sig("choices_ready").at(l))
        both = k.feat[:, 384:384 + T * NE]
        pe.matmul(ps[:, 0:T * NE], k.c("before"), both, start=True, stop=True)
        ins = pe.matmul(ps[:, 512:512 + T * NE], k.c("ones"), both, start=True, stop=True)
        ins.then_inc(*full.tick(("rank", l)))
        s = lsig(k, "moe_tensor", l)
        pe.sem_inc(s.sem, s.per())
        ps = k.open_slot(pe, ("rows", l))
        pe.wait_ge(*k.sig("row_hots_ready").at(l))
        hot, own = (k.scr[:, o:o + 2 * NT * w].rearrange("p (n r) -> p n r", r=w) for o, w in ((0, P), (2688, MAXB)))
        ins = matmuls(pe, ps[:, 0:MAXB], [(hot[:, NT * j + t, :], own[:, NT * j + t, :]) for j in range(2) for t in range(T)])
        ins.then_inc(*full.tick(("rows", l)))
        moe_tensor(k, pe, l)


def tensor_mod(k, pe, l, n):
    pe.wait_ge(*k.sig("ring%d_loaded" % (n % 2)).at((l, n)))
    w, ps = k.ring(n), k.open_slot(pe, ("mod", l, n))
    cv = k.cvec[:, :].rearrange("p (c s) -> p c s", s=2)
    matmuls(pe, ps[0:2, 0:512], [(cv[:, c, :], w[:, c, :]) for c in range(DC)]).then_inc(*k.sig("psum_full").tick(("mod", l, n)))


def tensor_mod_columns(k, pe, l, n):
    ps = k.open_slot(pe, ("modcol", l, n))
    k.wait_read(pe, ("mod", l, n))
    for j in range(4):
        ins = pe.transpose(ps[:, 2 * j:2 * j + 2], k.mod_row(n)[:, j * P:(j + 1) * P], k.c("ident")[0:2, 0:2])
    ins.then_inc(*k.sig("psum_full").tick(("modcol", l, n)))


def token_cut(l, s, t):
    a, b = 0, IN_SLICES[s][1]
    if ROWS_PER_LAYER[l] <= t:
        a, b = {4: (0, 256), 5: (256, 416)}[s]
    return a, b


def tensor_hgrn(k, pe, l):
    full, ident, T = k.sig("psum_full"), k.c("ident"), ROWS_PER_LAYER[l]
    dring = lambda n: k.scr[:, (n % RING_D) * 768:(n % RING_D + 1) * 768].rearrange("p (c t) -> p c t", c=NT)
    kt = k.feat[:, 3072:3840].rearrange("p (c t) -> p c t", c=NT)
    st = k.feat[:, 3840:4608].rearrange("p (d c e) -> p d c e", d=2, c=NT)
    qd = k.feat[:, 4608:6144].rearrange("p (d c t) -> p d c t", d=2, c=NT)
    at = k.feat[:, 1536:2304].rearrange("p (c t) -> p c t", c=NT)
    q, kf, kb = (k.hg(n).rearrange("p h (c t) -> p h c t", c=NT) for n in range(3))
    v = k.tokv(C_V, C_V + 256)

    def output(hd):
        ps = k.open_slot(pe, ("hgout", l, hd))
        k.wait_read(pe, ("adds", l, hd, 1))
        k.wait_read(pe, ("level", l, hd, 2 * len(LEVELS) - 1))
        for c in range(T):
            terms = [(at[:, c, :], v[:, c, 64 * hd:64 * hd + 64])]
            for dr in range(2):
                n = TURNS[dr].index(c)
                terms += [(qd[:, dr, c, :], st[:, dr, n, :])] if n else []
            ins = matmuls(pe, ps[:, c * 64:(c + 1) * 64], terms)
        ins.then_inc(*full.tick(("hgout", l, hd)))

    for n, (hd, m) in enumerate(HG_ITEMS):
        place = n % len(HG_ORDER)
        if place == 0:
            ps = k.open_slot(pe, ("diag", l, hd))
            for c in range(T):
                ins = matmuls(pe, ps[:, c * P:(c + 1) * P], [(kf[:, hd, c, :], q[:, hd, c, :]), (kb[:, hd, c, :], q[:, hd, c, :])])
            ins.then_inc(*full.tick(("diag", l, hd)))
        if m < 2:
            ps = k.open_slot(pe, ("keys", l, hd, m))
            pe.wait_ge(*k.sig("decayed").at((l, hd, m)))
            for c in range(NT):
                ins = pe.transpose(ps[:, c * P:(c + 1) * P], dring(n)[:, c, :], ident)
            ins.then_inc(*full.tick(("keys", l, hd, m)))
        elif m >= 4:
            level = m - 4
            ps = k.open_slot(pe, ("level", l, hd, level))
            pe.wait_ge(*k.sig("decayed").at((l, hd, m)))
            dz = dring(n)
            for c in range(T):
                ins = pe.matmul(ps[:, c * P:(c + 1) * P], dz[:, c, :], dz[:, c, :], start=True, stop=True)
            ins.then_inc(*full.tick(("level", l, hd, level)))
            item = mod_item(l, hd, level)
            if item:
                if item != MOD_DURING[l][0]:
                    tensor_mod_columns(k, pe, *mod_before(item))
                tensor_mod(k, pe, *item)
        if place >= KEY_LAG and HG_ORDER[place - KEY_LAG] < 2:
            dr = HG_ORDER[place - KEY_LAG]
            ps = k.open_slot(pe, ("adds", l, hd, dr))
            k.wait_read(pe, ("keys", l, hd, dr))
            for c in range(NT):
                ins = matmuls(pe, ps[:, c * 64:(c + 1) * 64], [(kt[:, c, :], v[:, c, 64 * hd:64 * hd + 64])])
            ins.then_inc(*full.tick(("adds", l, hd, dr)))
        if hd and place == HG_LATE:
            output(hd - 1)
    output(HEADS_G - 1)
    tensor_mod_columns(k, pe, *MOD_DURING[l][-1])
    for t in range(T):
        ps = k.open_slot(pe, ("readout", l, t))
        if t == 0:
            pe.wait_ge(*k.sig("readout_ready").at(l))
        for j in range(2):
            ins = pe.transpose(ps[:, j * P:(j + 1) * P], k.tokv(C_P, C_P + 256)[:, t, j * P:(j + 1) * P], ident)
        ins.then_inc(*full.tick(("readout", l, t)))


def tensor_attention(k, pe, l):
    full, ident, T = k.sig("psum_full"), k.c("ident"), ROWS_PER_LAYER[l]
    lat = k.latent()
    uq = k.scr[:, 3072:4608].rearrange("p (c n) -> p c n", c=2)
    ukv = k.scr[:, 4608:5632]
    cq, ckv = k.tokv(C_CQ, C_CQ + 256), k.tokv(C_CKV, C_CKV + 128)
    for t in range(NT):
        ps = k.open_slot(pe, ("latent", l, t))
        if t == 0:
            pe.wait_ge(*k.sig("latents_normed").at(l))
        if t < T:
            for c in range(2):
                pe.transpose(ps[:, c * P:(c + 1) * P], cq[:, t, c * P:(c + 1) * P], ident)
        pe.transpose(ps[:, 2 * P:3 * P], ckv[:, t, :], ident).then_inc(*full.tick(("latent", l, t)))
    pe.wait_ge(*k.sig("mla_weights_loaded").at(l))
    qt = k.scr[:, 0:768].rearrange("p (h n) -> p h n", h=HEADS_A)
    kt = k.scr[:, 768:1536].rearrange("p (h n) -> p h n", h=HEADS_A)
    for t in range(NT):
        if t < T:
            ps = k.open_slot(pe, ("q", l, t))
            k.wait_read(pe, ("latent", l, t))
            for half in range(2):
                ins = matmuls(pe, ps[:, half * 512:half * 512 + 384],
                              [(lat[:, c, t * P:(t + 1) * P], uq[:, c, half * 384:half * 384 + 384]) for c in range(2)])
            ins.then_inc(*full.tick(("q", l, t)))
        ps = k.open_slot(pe, ("kv", l, t))
        k.wait_read(pe, ("latent", l, t))
        for half in range(2):
            ins = matmuls(pe, ps[:, half * 512:half * 512 + 512], [(lat[:, 2, t * P:(t + 1) * P], ukv[:, half * 512:half * 512 + 512])])
        ins.then_inc(*full.tick(("kv", l, t)))
        for name, src, ok in (("qT", qt, t < T), ("kT", kt, True)):
            if ok:
                ps = k.open_slot(pe, (name, l, t))
                k.wait_read(pe, ("q" if name == "qT" else "kv", l, t))
                if name == "kT" or t < LT:
                    pe.wait_ge(*k.sig(name[0] + "_roped").at((l, t)))
                for hd in range(HEADS_A):
                    ins = pe.transpose(ps[0:QK, hd * P:(hd + 1) * P], src[:, hd, :], ident)
                ins.then_inc(*full.tick((name, l, t)))
    turns = [(hd, t) for hd in range(HEADS_A) for t in range(T)]
    qm, km, v = k.mla(0), k.mla(1), k.tokv(0, 512)
    for n in range(len(turns) + 2):
        if n < len(turns):
            hd, t = turns[n]
            ps = k.open_slot(pe, ("score", l, hd, t))
            if n == 0:
                k.wait_read(pe, ("qT", l, T - 1))
                k.wait_read(pe, ("kT", l, NT - 1))
                k.wait_read(pe, ("kv", l, NT - 1))
            for a, b in key_cuts(t):
                ins = pe.matmul(ps[:, a:b], qm[:, hd, t * P:(t + 1) * P], km[:, hd, a:b], start=True, stop=True)
            ins.then_inc(*full.tick(("score", l, hd, t)))
        if 1 <= n <= len(turns):
            hd, t = turns[n - 1]
            prob = k.scr[:, ((n - 1) % 2) * 768:((n - 1) % 2) * 768 + 768]
            ps = k.open_slot(pe, ("probT", l, hd, t))
            k.wait_read(pe, ("score", l, hd, t))
            for kt_ in key_tiles(t):
                ins = pe.transpose(ps[:, kt_ * P:(kt_ + 1) * P], prob[:, kt_ * P:(kt_ + 1) * P], ident)
            ins.then_inc(*full.tick(("probT", l, hd, t)))
        if n >= 2:
            hd, t = turns[n - 2]
            pt = k.scr[:, 1536 + ((n - 2) % 2) * 768:1536 + ((n - 2) % 2) * 768 + 768]
            ps = k.open_slot(pe, ("pv", l, hd, t))
            k.wait_read(pe, ("probT", l, hd, t))
            ins = matmuls(pe, ps[:, 0:64], [(pt[:, kt_ * P:(kt_ + 1) * P], v[:, kt_, hd * 64:hd * 64 + 64]) for kt_ in key_tiles(t)])
            ins.then_inc(*full.tick(("pv", l, hd, t)))
    for t in range(T):
        ps = k.open_slot(pe, ("mixed", l, t))
        if t == 0:
            k.wait_read(pe, ("pv", l, HEADS_A - 1, T - 1))
        for c in range(4):
            ins = pe.transpose(ps[:, c * P:(c + 1) * P], k.tokv(512, 1024)[:, t, c * P:(c + 1) * P], ident)
        ins.then_inc(*full.tick(("mixed", l, t)))


def key_tiles(t):
    return range(NT) if t < LT else range(LT, NT)


def key_cuts(t):
    return ((0, 512), (512, 768)) if t < LT else ((512, 768),)


def mv(k):
    return k.stats[:, 0:12].rearrange("p (t s) -> p t s", s=2)


ST_BN, ST_RSTD, ST_LOG = 12, 36, 42
SM_END, SM_SS, SM_RS, SM_LS, SM_QS, SM_MAX, SM_SUM, SM_INV = 0, 48, 72, 96, 120, 134, 138, 142


def scalar_program(k, act):
    nc = k.nc
    step = k.sig("scalar_step")
    read = k.sig("psum_read_by_scalar")

    def link(ins):
        ins.then_inc(*step.tick())
        act.wait_ge(*step.last())

    eps = k.c("eps")

    def rstd(key, out, log, src, scale=1.0):
        act.wait_ge(*k.sig("variance_ready").at(key))
        link(act.activation(log, src, ACT.Ln, bias=eps, scale=scale))
        act.activation(out, log, ACT.Exp, scale=-0.5).then_inc(*k.sig("rstd_ready").tick(key))

    def token_rstd(key, t):
        rstd(key, k.stats[:, ST_RSTD + t:ST_RSTD + t + 1], k.stats[:, ST_LOG + t:ST_LOG + t + 1], mv(k)[:, t, 1:2])

    def modulated(l, t):
        m, s = k.mod(l), 0 if t < LT else 1
        if t == 0:
            act.wait_ge(*k.sig("mod_ready").at((l, "early")))
        act.wait_ge(*k.full(("h", l, t)))
        ps = k.slot(("h", l, t))
        for c in range(DC if l else 4):
            ins = act.activation(k.feat_c(c, t * P, (t + 1) * P), ps[:, c * P:(c + 1) * P], ACT.Identity,
                                 scale=m[:, SC1 * DC + c, s:s + 1], bias=m[:, SH1 * DC + c, s:s + 1])
        ins.then_inc(*read.tick(("h", l, t)))

    act.wait_ge(*k.sig("first_loads").at("masks"))
    act.activation(k.small[:, 0:16], k.cvec[:, :], ACT.Exp, scale=-1.0).then_inc(*k.sig("c_exp").tick())
    act.wait_ge(*k.sig("bound_gap").at())
    act.activation(k.logits[:, 24:40], k.logits[:, 24:40], ACT.Exp).then_inc(*k.sig("bound_exp").tick())
    for l in range(DEPTH):
        T = ROWS_PER_LAYER[l]
        m = k.mod(l)
        col = lambda n: k.cols[:, 32 * l + n:32 * l + n + 1]
        tcols = T * P
        if l == 0:
            for n in range(RING_EARLY):
                scalar_mod(k, act, l, n)
        if l == 0:
            for t in range(NT):
                token_rstd(("h", l, t), t)
            for t in range(NT):
                modulated(l, t)
        tmp = lambda n, w: k.scr[:, n * 768:n * 768 + w]
        for s in range(3):
            w = tcols if s == 0 else NT * P
            for hd in range(HEADS_G):
                key = ("proj", l, s, hd)
                if s == 0:
                    act.wait_ge(*k.full(key))
                    if hd:
                        act.wait_ge(*k.sig("psum_read_by_vector").at(("proj", l, s, hd - 1)))
                    act.activation(tmp(0, w), k.slot(key)[:, 0:w], ACT.Exp, scale=-1.0).then_inc(*k.sig("q_exp").tick((l, hd)))
                else:
                    act.wait_ge(*k.sig("psum_read_by_vector").at(key))
                    link(act.activation(tmp(0, w), tmp(0, w), ACT.Exp, scale=-1.0))
                    act.activation(tmp(2, w), tmp(0, w), ACT.Ln, scale=col(K_LB + 4 * (s - 1) + hd), bias=1.0)
                    act.activation(tmp(3, w), tmp(0, w), ACT.Ln, bias=1.0).then_inc(*k.sig("logs_ready").tick(key))
        act.wait_ge(*k.sig("y_cleared").at())
        for s, o in ((3, C_P), (4, C_V), (5, C_CQ)):
            for t in range(T if s == 3 else NT):
                key = ("proj", l, s, t)
                a, b = token_cut(l, s, t)
                act.wait_ge(*k.full(key))
                if s == 4 and t < T:
                    if t >= 2:
                        act.wait_ge(*k.sig("gate_silu").at((l, t - 2)))
                    act.activation(k.gate_exp(t), k.slot(key)[:, 256:512], ACT.Exp, scale=-1.0).then_inc(*k.sig("gate_exp").tick((l, t)))
                act.copy(k.tokv(o + a, o + b)[:, t, :], k.slot(key)[:, a:b]).then_inc(*read.tick(key))
        pooled = k.feat[0:64, 3072:6144].rearrange("p (g t) -> p g t", g=4)
        for g in range(4):
            act.wait_ge(*k.full(("pool", l, g)))
            act.copy(pooled[:, g, 0:tcols], k.slot(("pool", l, g))[0:64, 0:tcols]).then_inc(*read.tick(("pool", l, g)))
        act.wait_ge(*k.sig("columns_loaded").at(l))
        for j in range(2):
            act.wait_ge(*k.full(("poolout", l, j)))
            act.activation(k.feat_c(j, 0, tcols), k.slot(("poolout", l, j))[:, 0:tcols], ACT.Identity, scale=col(K_PS + j)) \
               .then_inc(*read.tick(("poolout", l, j)))
        scalar_hgrn(k, act, l, link)
        n = 4 * T
        rstd(("hg", l), k.small[:, SM_RS:SM_RS + n], k.small[:, SM_LS:SM_LS + n], k.small[:, SM_SS:SM_SS + n], 1.0 / DV_G)
        for t in range(T):
            key = ("readout", l, t)
            act.wait_ge(*k.full(key))
            for j in range(2):
                ins = act.activation(k.feat_c(2 + j, t * P, (t + 1) * P), k.slot(key)[:, j * P:(j + 1) * P], ACT.Identity, scale=col(K_HN + j))
            ins.then_inc(*read.tick(key))
        scalar_attention(k, act, l, rstd)
        for r, _, _ in mod_rows(l):
            act.wait_ge(*k.full(("row", l, r)))
            act.copy(k.row(r), k.slot(("row", l, r))).then_inc(*read.tick(("row", l, r)))
        for n in range(T + 1):
            if n < T:
                token_rstd(("post1", l, n), n)
            if n:
                h2_copy(k, act, l, n - 1, read)
            if n < T:
                token_rstd(("h2", l, n), n)
        act.wait_ge(*k.sig("group_logits_ready").at(l))
        act.activation(k.feat[:, 672:672 + 4 * T], k.feat[:, 672:672 + 4 * T], ACT.Exp).then_inc(*k.sig("group_exp").tick(l))
        act.wait_ge(*k.sig("second_minus_first").at(l))
        act.activation(k.feat[:, 1160:1160 + T], k.feat[:, 1160:1160 + T], ACT.Exp).then_inc(*k.sig("second_exp").tick(l))
        moe_scalar(k, act, l)
        for n in range(-1, T + 2):
            if 0 <= n < T:
                token_rstd(("post2", l, n), n)
            if n + 1 < T:
                rows = k.expert_rows(n + 1, 1)
                act.wait_ge(*k.sig("y_gathered%d" % ((n + 1) % 2)).at((l, n + 1)))
                act.activation(rows, rows, ACT.Identity, scale=k.gates[:, NT + n + 1:NT + n + 2]).then_inc(*k.sig("second_gated").tick((l, n + 1)))
            if l + 1 < DEPTH:
                if 1 <= n <= T:
                    token_rstd(("h", l + 1, n - 1), n - 1)
                if n >= 2:
                    modulated(l + 1, n - 2)


def scalar_mod(k, act, l, n):
    act.wait_ge(*k.full(("mod", l, n)))
    if n % 2 and (l, n) in MOD_DURING[0][:2] + MOD_DURING[1][:2]:
        u = [(l, n) in items for items in MOD_DURING].index(True)
        act.wait_ge(*k.sig("gate_silu").at((u, ROWS_PER_LAYER[u] - 1)))
    if mod_before((l, n), 2):
        act.wait_ge(*k.full(("modcol",) + mod_before((l, n), 2)))
    act.copy(k.mod_row(n), k.slot(("mod", l, n))[0:2, 0:512]).then_inc(*k.sig("psum_read_by_scalar").tick(("mod", l, n)))


def h2_copy(k, act, l, t, read):
    act.wait_ge(*k.full(("h2", l, t)))
    if t >= 2:
        act.wait_ge(*k.full(("logit", l, t - 2)))
    act.copy(k.w[:, 22528 + (t % 2) * D:22528 + (t % 2 + 1) * D], k.slot(("h2", l, t))).then_inc(*read.tick(("h2", l, t)))


def decay_end(k, l, n):
    hd, m = HG_ITEMS[n]
    if m < 2:
        return k.full(("keys", l, hd, m))
    if m < 4:
        return k.sig("decayed").at((l, hd, m))
    return k.full(("level", l, hd, m - 4))


def wait_decay_room(k, eng, l, n):
    if n >= RING_D:
        eng.wait_ge(*decay_end(k, l, n - RING_D))
    elif n >= RING_PAST_BANDS:
        eng.wait_ge(*k.full(("pool", l, 3)))


def scalar_hgrn(k, act, l, link):
    T = ROWS_PER_LAYER[l]
    read = k.sig("psum_read_by_scalar")
    dring = lambda n: k.scr[:, (n % RING_D) * 768:(n % RING_D + 1) * 768].rearrange("p (c t) -> p c t", c=NT)
    xf, xb = k.prefix(0), k.prefix(1)
    kt = k.feat[:, 3072:3840]
    act.wait_ge(*k.sig("head_done").at((l, 2, HEADS_G - 1)))
    for dr, x in enumerate((xf, xb)):
        ins = act.activation(k.small[:, SM_END + 24 * dr:SM_END + 24 * dr + 24].rearrange("p (h c) -> p h c", h=HEADS_G), x[:, :, :, P], ACT.Exp)
    ins.then_inc(*k.sig("ends_ready").tick(l))

    def exp(n):
        hd, m = HG_ITEMS[n]
        d = dring(n)
        c = NT if m < 2 else T
        if m in (1, 2):
            wait_decay_room(k, act, l, n)
            src = xb[:, hd, 0:c, 0:P] if m == 1 else xf[:, hd, 0:c, 1:P + 1]
        else:
            act.wait_ge(*k.sig("gap_ready").at((l, hd, m)))
            src = d[:, 0:c, :]
        act.activation(d[:, 0:c, :], src, ACT.Exp).then_inc(*k.sig("decay_ready").tick((l, hd, m)))

    def keys(hd, dr):
        act.wait_ge(*k.full(("keys", l, hd, dr)))
        if hd or dr:
            act.wait_ge(*k.full(("adds", l, hd - (dr == 0), 1 - dr)))
        act.copy(kt, k.slot(("keys", l, hd, dr))[:, 0:768]).then_inc(*read.tick(("keys", l, hd, dr)))

    def output(hd):
        act.wait_ge(*k.full(("hgout", l, hd)))
        act.copy(k.tokv(64 * hd, 64 * hd + 64)[:, 0:T, :], k.slot(("hgout", l, hd))[:, 0:T * 64].rearrange("p (t n) -> p t n", t=T)) \
           .then_inc(*read.tick(("hgout", l, hd)))

    for n, (hd, m) in enumerate(HG_ITEMS):
        place = n % len(HG_ORDER)
        exp(n)
        for level in MOD_LEVELS[l]:
            if m - 4 == min(level + 1, 13):
                scalar_mod(k, act, *mod_item(l, hd, level))
        if place >= KEY_LAG and HG_ORDER[place - KEY_LAG] < 2:
            keys(hd, HG_ORDER[place - KEY_LAG])
        if hd and place == HG_LATE + 1:
            output(hd - 1)
    output(HEADS_G - 1)


def scalar_attention(k, act, l, rstd):
    T = ROWS_PER_LAYER[l]
    read = k.sig("psum_read_by_scalar")
    col = lambda n: k.cols[:, 32 * l + n:32 * l + n + 1]
    lat = k.latent()
    rstd(("cq", l), k.small[:, SM_RS:SM_RS + T], k.small[:, SM_LS:SM_LS + T], k.small[:, SM_QS:SM_QS + T], 1.0 / 256)
    rstd(("ckv", l), k.small[:, SM_RS + 6:SM_RS + 12], k.small[:, SM_LS + 6:SM_LS + 12], k.small[:, SM_QS + 6:SM_QS + 12], 1.0 / 128)
    for t in range(NT):
        key = ("latent", l, t)
        act.wait_ge(*k.full(key))
        for c in range(0 if t < T else 2, 3):
            ins = act.activation(lat[:, c, t * P:(t + 1) * P], k.slot(key)[:, c * P:(c + 1) * P], ACT.Identity,
                                 scale=col(K_QN + c if c < 2 else K_KN))
        ins.then_inc(*read.tick(key))
    for t in range(NT):
        if t < T:
            key = ("q", l, t)
            act.wait_ge(*k.full(key))
            if t:
                act.wait_ge(*k.full(("qT", l, t - 1)))
            act.copy(k.scr[:, 0:768].rearrange("p (a n) -> p a n", a=2), k.slot(key).rearrange("p (a n) -> p a n", a=2)[:, :, 0:384]) \
               .then_inc(*read.tick(key))
        key = ("kv", l, t)
        act.wait_ge(*k.full(key))
        if t:
            act.wait_ge(*k.full(("kT", l, t - 1)))
        act.copy(k.scr[:, 768:1536].rearrange("p (h n) -> p h n", h=HEADS_A)[:, :, 0:NOPE],
                 k.slot(key).rearrange("p (h n) -> p h n", h=HEADS_A)[:, :, 0:NOPE])
        act.copy(k.tokv(0, 512)[:, t, :].rearrange("p (h n) -> p h n", h=HEADS_A),
                 k.slot(key).rearrange("p (h n) -> p h n", h=HEADS_A)[:, :, NOPE:]).then_inc(*read.tick(key))
        key = ("kT", l, t)
        act.wait_ge(*k.full(key))
        act.copy(k.mla(1)[:, :, t * P:(t + 1) * P], k.slot(key)[0:QK, :].rearrange("p (h t) -> p h t", h=HEADS_A)).then_inc(*read.tick(key))
    turns = [(hd, t) for hd in range(HEADS_A) for t in range(T)]
    for n in range(len(turns) + 2):
        if n < len(turns):
            hd, t = turns[n]
            key = ("score", l, hd, t)
            a, b = (0, 768) if t < LT else (512, 768)
            act.wait_ge(*k.sig("max_ready").at(key))
            if n >= 2:
                act.wait_ge(*k.full(("probT", l) + turns[n - 2]))
            act.activation(k.scr[:, (n % 2) * 768 + a:(n % 2) * 768 + b], k.slot(key)[:, a:b], ACT.Exp, scale=SCALE,
                           bias=k.small[:, SM_MAX + n % 4:SM_MAX + n % 4 + 1],
                           accum_out=k.small[:, SM_SUM + n % 4:SM_SUM + n % 4 + 1]).then_inc(*read.tick(key))
        if n >= 2:
            hd, t = turns[n - 2]
            key = ("pv", l, hd, t)
            act.wait_ge(*k.full(key))
            act.wait_ge(*k.sig("sum_inverted").at(("score", l, hd, t)))
            act.activation(k.tokv(512 + 64 * hd, 576 + 64 * hd)[:, t, :], k.slot(key)[:, 0:64], ACT.Identity,
                           scale=k.small[:, SM_INV + (n - 2) % 4:SM_INV + (n - 2) % 4 + 1]).then_inc(*read.tick(key))
    for t in range(T):
        key = ("mixed", l, t)
        act.wait_ge(*k.full(key))
        act.copy(k.feat[:, :].rearrange("p (c t) -> p c t", c=DC)[:, 4:8, t * P:(t + 1) * P],
                 k.slot(key)[:, 0:512].rearrange("p (c t) -> p c t", c=4)).then_inc(*read.tick(key))


def vector_program(k, dve):
    step = k.sig("vector_step")
    read = k.sig("psum_read_by_vector")

    def link(ins):
        ins.then_inc(*step.tick())
        dve.wait_ge(*step.last())

    def statistics(key, t):
        bn = k.stats[:, ST_BN + (t % 2) * 12:ST_BN + (t % 2) * 12 + 12].rearrange("p (a s) -> p a s", a=2)
        for a in range(2):
            ins = dve.bn_stats(bn[:, a, :], k.x[:, t, a * 512:(a + 1) * 512])
        link(ins)
        dve.bn_aggr(mv(k)[:, t, :], bn).then_inc(*k.sig("variance_ready").tick(key))

    def normalise(out, key, t):
        dve.wait_ge(*k.sig("variance_ready").at(key))
        dve.wait_ge(*k.sig("rstd_ready").at(key))
        return dve.tensor_scalar(out, k.x[:, t, :], mv(k)[:, t, 0:1], k.stats[:, ST_RSTD + t:ST_RSTD + t + 1], ALU.subtract, ALU.mult)

    def h_normalised(l, t):
        if t >= 2:
            dve.wait_ge(*k.full(("h", l, t - 2)))
        normalise(k.scr[:, (t % 2) * D:(t % 2 + 1) * D], ("h", l, t), t).then_inc(*k.sig("z_ready").tick((l, t)))

    def h_modulated(l, t):
        m, s = k.mod(l), 0 if t < LT else 1
        if t == 0:
            dve.wait_ge(*k.sig("mod_ready").at((l, "early")))
        dve.wait_ge(*k.full(("h", l, t)))
        ps = k.slot(("h", l, t))
        for c in range(4, 8):
            ins = dve.tensor_scalar(k.feat_c(c, t * P, (t + 1) * P), ps[:, c * P:(c + 1) * P],
                                    m[:, SC1 * DC + c, s:s + 1], m[:, SH1 * DC + c, s:s + 1], ALU.mult, ALU.add)
        ins.then_inc(*read.tick(("h", l, t)))

    dve.wait_ge(*k.sig("c_exp").at())
    e = k.small[:, 0:16]
    link(dve.tensor_scalar(e, e, 1.0, None, ALU.add))
    link(dve.reciprocal(e, e))
    dve.tensor_tensor(k.cvec[:, :], k.cvec[:, :], e, ALU.mult).then_inc(*k.sig("c_ready").tick())
    dve.wait_ge(*k.sig("first_loads").at("masks"))
    link(dve.tensor_copy(k.masks[:, :], k.scr[:, 3072:3072 + 2 * len(LEVELS) * P]))
    dve.wait_ge(*k.sig("x_loaded").at())
    for l in range(DEPTH):
        T = ROWS_PER_LAYER[l]
        tcols = T * P
        m = k.mod(l)
        col = lambda n: k.cols[:, 32 * l + n:32 * l + n + 1]
        if l == 0:
            for t in range(NT):
                statistics(("h", l, t), t)
        else:
            dve.wait_ge(*k.sig("moe_done").at(l - 1))
        for dr in range(2):
            dve.memset(k.prefix(dr)[:, :, :, 0:1], 0.0)
        lower_bound(k, dve, l, link)
        dve.wait_ge(*k.sig("columns_loaded").at(l))
        if l == 0:
            for n in range(RING_EARLY):
                vector_mod(k, dve, l, n)
            for t in range(NT + 1):
                if t < NT:
                    h_normalised(l, t)
                if t:
                    h_modulated(l, t - 1)
        tmp = lambda n, w: k.scr[:, n * 768:n * 768 + w]
        for s in range(3):
            w = tcols if s == 0 else NT * P
            for hd in range(HEADS_G):
                key = ("proj", l, s, hd)
                ps = k.slot(key)[:, 0:w]
                if s == 0:
                    dve.wait_ge(*k.sig("q_exp").at((l, hd)))
                    link(dve.tensor_scalar(tmp(0, w), tmp(0, w), 1.0, None, ALU.add))
                    link(dve.reciprocal(tmp(0, w), tmp(0, w)))
                    dve.tensor_tensor(k.hg(0)[:, hd, 0:w], ps, tmp(0, w), ALU.mult).then_inc(*read.tick(key))
                    continue
                dve.wait_ge(*k.full(key))
                dve.wait_ge(*(read.at(("proj", l, 0, HEADS_G - 1)) if (s, hd) == (1, 0) else k.sig("head_done").at((l, s - (hd == 0), (hd - 1) % 4))))
                dve.tensor_scalar(tmp(0, w), ps, Z_MIN, None, ALU.max)
                dve.tensor_scalar(tmp(1, w), ps, -Z_MIN, 0.0, ALU.add, ALU.min).then_inc(*read.tick(key))
                dve.wait_ge(*read.at(key))
                dve.wait_ge(*k.sig("logs_ready").at(key))
                link(dve.tensor_tensor(tmp(2, w), tmp(2, w), tmp(3, w), ALU.subtract))
                dve.scalar_tensor_tensor(tmp(2, w), tmp(1, w), col(K_IND + 4 * (s - 1) + hd), tmp(2, w), ALU.mult, ALU.add)
                link(dve.tensor_scalar(tmp(3, w), tmp(0, w), 1.0, None, ALU.add))
                link(dve.reciprocal(tmp(3, w), tmp(3, w)))
                dve.scalar_tensor_tensor(k.hg(s)[:, hd, 0:w], tmp(0, w), col(K_OML + 4 * (s - 1) + hd), tmp(3, w), ALU.mult, ALU.mult)
                for c in range(NT):
                    ins = dve.tensor_tensor_scan(k.prefix(s - 1)[:, hd, c, 1:P + 1], k.c("ones"), tmp(2, w)[:, c * P:(c + 1) * P], 0.0, ALU.mult, ALU.add)
                ins.then_inc(*k.sig("head_done").tick((l, s, hd)))
        dve.wait_ge(*k.sig("head_done").at((l, 2, HEADS_G - 1)))
        for t in range(T):
            e, g = k.gate_exp(t), k.tokv(C_G, C_G + 256)[:, t, :]
            dve.wait_ge(*k.sig("gate_exp").at((l, t)))
            link(dve.tensor_scalar(e, e, 1.0, None, ALU.add))
            link(dve.reciprocal(e, e))
            dve.wait_ge(*k.sig("psum_read_by_scalar").at(("proj", l, 4, t)))
            dve.tensor_tensor(g, g, e, ALU.mult).then_inc(*k.sig("gate_silu").tick((l, t)))
        vector_hgrn(k, dve, l, link)
        o, g = (k.tokv(a, a + 256)[:, 0:T, :] for a in (C_P, C_G))
        n = 4 * T
        sq = k.scr[:, 0:T * 256].rearrange("p (t n) -> p t n", t=T)
        dve.wait_ge(*k.sig("psum_read_by_scalar").at(("hgout", l, HEADS_G - 1)))
        link(dve.tensor_tensor(sq, o, o, ALU.mult))
        dve.tensor_reduce(k.small[:, SM_SS:SM_SS + n], k.scr[:, 0:T * 256].rearrange("p (n e) -> p n e", e=DV_G), AX.X, ALU.add) \
           .then_inc(*k.sig("variance_ready").tick(("hg", l)))
        link(dve.tensor_tensor(o, o, g, ALU.mult))
        dve.wait_ge(*k.sig("rstd_ready").at(("hg", l)))
        o4, rs = o.rearrange("p t (h e) -> p t h e", e=DV_G), k.small[:, SM_RS:SM_RS + n].rearrange("p (t h) -> p t h", t=T)
        dve.tensor_tensor(o4, o4, rs.unsqueeze(3).to_broadcast([P, T, HEADS_G, DV_G]), ALU.mult).then_inc(*k.sig("readout_ready").tick(l))
        vector_mod(k, dve, *MOD_DURING[l][-1])
        vector_attention(k, dve, l, link)
        vector_post_mixer(k, dve, l, link, statistics, normalise)
        vector_route(k, dve, l, link)
        moe_vector(k, dve, l)
        for n in range(T + 2):
            if n >= 2 and l + 1 < DEPTH:
                h_normalised(l + 1, n - 2)
            if n < T:
                xa, xb = (k.expert_rows(n, j) for j in range(2))
                dve.wait_ge(*k.sig("y_gathered%d" % (n % 2)).at((l, n)))
                dve.wait_ge(*k.sig("second_gated").at((l, n)))
                link(dve.scalar_tensor_tensor(xa, xa, k.gates[:, n:n + 1], xb, ALU.mult, ALU.add))
                link(dve.tensor_tensor(xa, xa, k.row(R_G2L if n < LT else R_G2C), ALU.mult))
                dve.scalar_tensor_tensor(k.x[:, n, :], k.x[:, n, :], ALPHA, xa, ALU.mult, ALU.add).then_inc(*k.sig("y_used").tick((l, n)))
                dve.wait_ge(*k.sig("y_used").at((l, n)))
                statistics(("post2", l, n), n)
            if 1 <= n <= T:
                t = n - 1
                link(normalise(k.x[:, t, :], ("post2", l, t), t))
                link(dve.tensor_tensor(k.x[:, t, :], k.x[:, t, :], k.row(R_LN2G), ALU.mult))
                dve.tensor_tensor(k.x[:, t, :], k.x[:, t, :], k.row(R_LN2B), ALU.add).then_inc(*k.sig("x_ready").tick((l, t)))
                if l + 1 < DEPTH:
                    dve.wait_ge(*k.sig("x_ready").at((l, t)))
                    statistics(("h", l + 1, t), t)


def vector_mod(k, dve, l, n):
    key, m, read = ("modcol", l, n), k.mod(l), k.sig("psum_read_by_vector")
    dve.wait_ge(*k.full(key))
    b = k.bmod[:, 48 * l + 4 * n:48 * l + 4 * n + 4].unsqueeze(2).to_broadcast([P, 4, 2])
    dve.tensor_tensor(m[:, 4 * n:4 * n + 4, :], k.slot(key)[:, 0:8].rearrange("p (j s) -> p j s", s=2), b, ALU.add) \
       .then_inc(*read.tick(key))
    for last, v, name in ((RING_EARLY - 1, SC1, "early"), (RING_IN - 1, SC2, "late")):
        if n == last:
            dve.wait_ge(*read.at(key))
            dve.tensor_scalar(m[:, v * DC:(v + 1) * DC, :], m[:, v * DC:(v + 1) * DC, :], 1.0, None, ALU.add) \
               .then_inc(*k.sig("mod_ready").tick((l, name)))


def lower_bound(k, dve, l, link):
    if l == 0:
        dve.wait_ge(*k.sig("columns_loaded").at(0))
        lg = k.logits[:, 0:16].rearrange("p (l n) -> p l n", l=DEPTH)
        mx, e0, e1, p0 = (k.logits[:, 16 + 8 * n:24 + 8 * n] for n in range(4))
        link(dve.tensor_tensor(mx, lg[:, 0, :], lg[:, 1, :], ALU.max))
        dve.tensor_tensor(e0, lg[:, 0, :], mx, ALU.subtract)
        dve.tensor_tensor(e1, lg[:, 1, :], mx, ALU.subtract).then_inc(*k.sig("bound_gap").tick())
        dve.wait_ge(*k.sig("bound_exp").at())
        link(dve.tensor_tensor(mx, e0, e1, ALU.add))
        link(dve.reciprocal(mx, mx))
        dve.tensor_tensor(p0, e0, mx, ALU.mult)
        link(dve.tensor_tensor(e1, e1, mx, ALU.mult))
        link(dve.tensor_tensor(e1, p0, e1, ALU.add))
        dve.tensor_tensor(k.cols[:, K_LB:K_LB + 8], p0, p0, ALU.subtract)
        link(dve.tensor_tensor(k.cols[:, 32 + K_LB:32 + K_LB + 8], e1, p0, ALU.subtract))
    c = k.cols[:, 32 * l:32 * l + 32]
    dve.tensor_scalar(c[:, K_OML:K_OML + 8], c[:, K_LB:K_LB + 8], -1.0, 1.0, ALU.mult, ALU.add)
    link(dve.tensor_scalar(c[:, K_IND:K_IND + 8], c[:, K_LB:K_LB + 8], 0.0, None, ALU.is_equal))


def halves(ap, h):
    return ap.rearrange("p c (b t) -> p c b t", t=2 * h)


def vector_hgrn(k, dve, l, link):
    T = ROWS_PER_LAYER[l]
    read = k.sig("psum_read_by_vector")
    dring = lambda n: k.scr[:, (n % RING_D) * 768:(n % RING_D + 1) * 768].rearrange("p (c t) -> p c t", c=NT)
    st = k.feat[:, 3840:4608].rearrange("p (d c e) -> p d c e", d=2, c=NT)
    qd = k.feat[:, 4608:6144].rearrange("p (d c t) -> p d c t", d=2, c=NT)
    at = k.feat[:, 1536:2304].rearrange("p (c t) -> p c t", c=NT)
    arrays = [k.hg(n).rearrange("p h (c t) -> p h c t", c=NT) for n in range(3)]
    ends = k.small[:, SM_END:SM_END + 48].rearrange("p (d h c) -> p d h c", d=2, h=HEADS_G)
    masks = k.masks[:, :].rearrange("p (m t) -> p m t", t=P)
    decayed = k.sig("decayed")
    dve.wait_ge(*k.sig("ends_ready").at(l))

    def states(hd, dr):
        key = ("adds", l, hd, dr)
        dve.wait_ge(*k.full(key))
        for n in range(NT - 1):
            c = TURNS[dr][n]
            add = k.slot(key)[:, c * 64:(c + 1) * 64]
            if n == 0:
                if hd:
                    dve.wait_ge(*k.full(("hgout", l, hd - 1)))
                ins = dve.tensor_copy(st[:, dr, 1, :], add)
            else:
                ins = dve.scalar_tensor_tensor(st[:, dr, n + 1, :], st[:, dr, n, :], ends[:, dr, hd, c:c + 1], add, ALU.mult, ALU.add)
            if n < NT - 2:
                link(ins)
        ins.then_inc(*read.tick(key))

    def products(n):
        hd, m = HG_ITEMS[n]
        level = m - 4
        if level == 0:
            key = ("diag", l, hd)
            dve.wait_ge(*k.full(key))
            if hd:
                dve.wait_ge(*k.full(("hgout", l, hd - 1)))
            dve.tensor_copy(at[:, 0:T, :], k.slot(key)[:, 0:T * P].rearrange("p (c t) -> p c t", c=T)).then_inc(*read.tick(key))
        key = ("level", l, hd, level)
        dve.wait_ge(*k.full(key))
        dve.wait_ge(*read.at(("level", l, hd, level - 1) if level else ("diag", l, hd)))
        dve.copy_predicated(at[:, 0:T, :], masks[:, level, :].unsqueeze(1).to_broadcast([P, T, P]),
                            k.slot(key)[:, 0:T * P].rearrange("p (c t) -> p c t", c=T)).then_inc(*read.tick(key))
        item = mod_item(l, hd, level)
        if item and item != MOD_DURING[l][0]:
            vector_mod(k, dve, *mod_before(item))

    for n in range(len(HG_ITEMS) + LEVEL_LAG):
        if n < len(HG_ITEMS):
            hd, m = HG_ITEMS[n]
            q, kf, kb = (a[:, hd] for a in arrays)
            d = dring(n)
            dve.wait_ge(*k.sig("decay_ready").at((l, hd, m)))
            if m < 4:
                src, out = ((kf, d), (kb, d), (q, qd[:, 0]), (q, qd[:, 1]))[m]
                c = NT if m < 2 else T
                if m == 2:
                    dve.wait_ge(*k.full(("hgout", l, hd - 1) if hd else ("poolout", l, 1)))
                dve.tensor_tensor(out[:, 0:c, :], d[:, 0:c, :], src[:, 0:c, :], ALU.mult).then_inc(*decayed.tick((l, hd, m)))
            else:
                h, dr = LEVELS[(m - 4) // 2], m % 2
                d = halves(d[:, 0:T, :], h)
                first, second = (kf, q) if dr == 0 else (q, kb)
                dve.tensor_tensor(d[:, :, :, 0:h], d[:, :, :, 0:h], halves(first[:, 0:T, :], h)[:, :, :, 0:h], ALU.mult)
                dve.tensor_tensor(d[:, :, :, h:2 * h], d[:, :, :, h:2 * h], halves(second[:, 0:T, :], h)[:, :, :, h:2 * h], ALU.mult) \
                   .then_inc(*decayed.tick((l, hd, m)))
        if n >= LEVEL_LAG:
            hd, m = HG_ITEMS[n - LEVEL_LAG]
            if m >= 4:
                products(n - LEVEL_LAG)
            place = (n - LEVEL_LAG) % len(HG_ORDER)
            if place >= KEY_LAG and HG_ORDER[place - KEY_LAG] < 2:
                states(hd, HG_ORDER[place - KEY_LAG])


def vector_attention(k, dve, l, link):
    T = ROWS_PER_LAYER[l]
    read = k.sig("psum_read_by_vector")
    small = k.small
    dve.wait_ge(*k.sig("readout_ready").at(l))
    for o, w, n, key in ((C_CQ, 256, T, "cq"), (C_CKV, 128, NT, "ckv")):
        sq = (k.scr[:, 0:n * w] if key == "cq" else k.scr[:, 1536:1536 + n * w]).rearrange("p (t n) -> p t n", t=n)
        v = k.tokv(o, o + w)[:, 0:n, :]
        s = SM_QS + (0 if key == "cq" else 6)
        link(dve.tensor_tensor(sq, v, v, ALU.mult))
        dve.tensor_reduce(small[:, s:s + n], sq, AX.X, ALU.add).then_inc(*k.sig("variance_ready").tick((key, l)))
    for o, w, n, key in ((C_CQ, 256, T, "cq"), (C_CKV, 128, NT, "ckv")):
        v = k.tokv(o, o + w)[:, 0:n, :]
        r = SM_RS + (0 if key == "cq" else 6)
        dve.wait_ge(*k.sig("rstd_ready").at((key, l)))
        ins = dve.tensor_tensor(v, v, small[:, r:r + n].unsqueeze(2).to_broadcast([P, n, w]), ALU.mult)
    ins.then_inc(*k.sig("latents_normed").tick(l))

    def rope(x, heads, a, b, t):
        cos = k.c("cos")[:, t * ROPE:(t + 1) * ROPE].unsqueeze(1).to_broadcast([P, heads, ROPE])
        sin = k.c("sin")[:, t * ROPE:(t + 1) * ROPE].rearrange("p (a s f) -> p a s f", a=2, s=2)
        av, bv = (y.rearrange("p (h n) -> p h n", h=heads) for y in (a, b))
        b5, x5 = (y.rearrange("p h (a s f) -> p h a s f", a=2, s=2) for y in (bv, x))
        dve.tensor_tensor(av, x, cos, ALU.mult)
        for s in range(2):
            for ax in range(2):
                ins = dve.tensor_tensor(b5[:, :, ax, s, :], x5[:, :, ax, 1 - s, :],
                                        sin[:, ax, s, :].unsqueeze(1).to_broadcast([P, heads, ROPE // 4]), ALU.mult)
        link(ins)
        return dve.tensor_tensor(x, av, bv, ALU.add)

    qt, kt = (k.scr[:, o:o + 768].rearrange("p (h n) -> p h n", h=HEADS_A) for o in (0, 768))
    for t in range(NT):
        if t < T:
            if t < LT:
                dve.wait_ge(*k.sig("psum_read_by_scalar").at(("q", l, t)))
                rope(qt[:, :, NOPE:QK], HEADS_A, k.scr[:, 1536:1792], k.scr[:, 1792:2048], t).then_inc(*k.sig("q_roped").tick((l, t)))
        kr = k.tokv(C_KR, C_KR + ROPE)[:, t:t + 1, :]
        if t < LT:
            link(rope(kr, 1, k.scr[:, 2048:2080], k.scr[:, 2080:2112], t))
        if t:
            dve.wait_ge(*k.full(("kT", l, t - 1)))
        dve.tensor_copy(kt[:, :, NOPE:QK], kr.to_broadcast([P, HEADS_A, ROPE])).then_inc(*k.sig("k_roped").tick((l, t)))
        if t < T:
            key = ("qT", l, t)
            dve.wait_ge(*k.full(key))
            dve.tensor_copy(k.mla(0)[:, :, t * P:(t + 1) * P], k.slot(key)[0:QK, :].rearrange("p (h t) -> p h t", h=HEADS_A)).then_inc(*read.tick(key))
    turns = [(hd, t) for hd in range(HEADS_A) for t in range(T)]
    for n in range(len(turns) + 1):
        if n < len(turns):
            hd, t = turns[n]
            key = ("score", l, hd, t)
            a, b = (0, 768) if t < LT else (512, 768)
            mx = small[:, SM_MAX + n % 4:SM_MAX + n % 4 + 1]
            dve.wait_ge(*k.full(key))
            if n >= 4:
                dve.wait_ge(*k.sig("psum_read_by_scalar").at(("score", l) + turns[n - 4]))
            dve.tensor_reduce(mx, k.slot(key)[:, a:b], AX.X, ALU.max, negate=True).then_inc(*read.tick(key))
            dve.wait_ge(*read.at(key))
            dve.tensor_scalar(mx, mx, SCALE, None, ALU.mult).then_inc(*k.sig("max_ready").tick(key))
        if n:
            hd, t = turns[n - 1]
            i = (n - 1) % 4
            a, b = (0, 768) if t < LT else (512, 768)
            dve.wait_ge(*k.sig("psum_read_by_scalar").at(("score", l, hd, t)))
            if n >= 5:
                dve.wait_ge(*k.sig("psum_read_by_scalar").at(("pv", l) + turns[n - 5]))
            dve.reciprocal(small[:, SM_INV + i:SM_INV + i + 1], small[:, SM_SUM + i:SM_SUM + i + 1]).then_inc(*k.sig("sum_inverted").tick(("score", l, hd, t)))
            key = ("probT", l, hd, t)
            dve.wait_ge(*k.full(key))
            if n >= 3:
                dve.wait_ge(*k.full(("pv", l) + turns[n - 3]))
            o = 1536 + ((n - 1) % 2) * 768
            dve.tensor_copy(k.scr[:, o + a:o + b], k.slot(key)[:, a:b]).then_inc(*read.tick(key))


def vector_post_mixer(k, dve, l, link, statistics, normalise):
    T = ROWS_PER_LAYER[l]
    read = k.sig("psum_read_by_vector")
    dve.wait_ge(*k.sig("norm_rows_loaded").at(l))
    dve.wait_ge(*k.sig("psum_read_by_scalar").at(("row", l, mod_rows(l)[-1][0])))

    def logits(t):
        key = ("logit", l, t)
        dve.wait_ge(*k.full(key))
        dve.tensor_tensor(k.logits[:, 36 * t:36 * t + 36], k.slot(key)[:, 0:36], k.router_b(), ALU.add).then_inc(*read.tick(key))

    ctx = lambda t: t >= LT
    z = lambda t: k.w[:, 20480 + (t % 2) * D:20480 + (t % 2 + 1) * D]

    def gated(t):
        key = ("out", l, t)
        g = k.w[:, 18432 + (t % 2) * D:18432 + (t % 2 + 1) * D]
        dve.wait_ge(*k.full(key))
        dve.tensor_tensor(g, k.slot(key), k.row(R_G1C if ctx(t) else R_G1L), ALU.mult).then_inc(*read.tick(key))
        dve.wait_ge(*read.at(key))
        link(dve.scalar_tensor_tensor(k.x[:, t, :], k.x[:, t, :], ALPHA, g, ALU.mult, ALU.add))
        statistics(("post1", l, t), t)

    def normed(t):
        x = k.x[:, t, :]
        link(normalise(x, ("post1", l, t), t))
        link(dve.tensor_tensor(x, x, k.row(R_LN1G), ALU.mult))
        link(dve.tensor_tensor(x, x, k.row(R_LN1B), ALU.add))
        statistics(("h2", l, t), t)

    def modulated(t):
        if t >= 2:
            dve.wait_ge(*k.full(("h2", l, t - 2)))
            dve.wait_ge(*k.sig("h2_stored%d" % (t % 2)).at((l, t - 2)))
        link(normalise(z(t), ("h2", l, t), t))
        link(dve.tensor_tensor(z(t), z(t), k.row(R_SC2C if ctx(t) else R_SC2L), ALU.mult))
        dve.tensor_tensor(z(t), z(t), k.row(R_SH2C if ctx(t) else R_SH2L), ALU.add).then_inc(*k.sig("h2_ready").tick((l, t)))

    for n in range(T + 2):
        if n < T:
            gated(n)
            normed(n)
            modulated(n)
        if n >= 2:
            logits(n - 2)


RI_SLOT, RI_TABLE, RI_TURNS, RI_ROWS, RI_NOW = 96, 112, 156, 160, 208
BIG = 1e30


def vector_route(k, dve, l, link):
    T = ROWS_PER_LAYER[l]
    read = k.sig("psum_read_by_vector")
    f, ri = k.feat, k.routei
    gl, gm = (f[:, o:o + 48].rearrange("p (t n) -> p t n", t=NT)[:, 0:T, :] for o in (576, 624))
    eg = f[:, 672:672 + 4 * T].rearrange("p (t n) -> p t n", t=T)
    le = f[:, 704:896].rearrange("p (t n) -> p t n", t=NT)[:, 0:T, :]
    ev = f[:, 896:944].rearrange("p (t n) -> p t n", t=NT)[:, 0:T, :]
    gi, ei = (ri[:, o:o + 48].rearrange("p (t n) -> p t n", t=NT)[:, 0:T, :] for o in (0, 48))
    gf = f[:, 944:944 + T]
    ef = f[:, 952:952 + 2 * T].rearrange("p (t j) -> p t j", j=2)
    mg, ng = (f[:, o:o + 4 * T].rearrange("p (t n) -> p t n", t=T) for o in (968, 992))
    total, e2, inv = f[:, 1152:1152 + T], f[:, 1160:1160 + T], f[:, 1168:1168 + T]
    nb, pend, base = f[:, 1184:1216], f[:, 1216:1248], f[:, 1248:1280]
    place, prod = (f[:, o:o + 192].rearrange("p (t e) -> p t e", t=NT)[:, 0:T, :] for o in (1280, 1472))
    rows = f[:, 1664:1664 + 2 * NT]
    lg = k.logits[:, :].rearrange("p (t n) -> p t n", t=NT)[:, 0:T, :]
    iota = k.c("iota")[:, 0:NE]
    dve.wait_ge(*read.at(("logit", l, T - 1)))
    ahead = k.scr[:, 3328:3328 + (NT + 1) * NE].rearrange("p (t e) -> p t e", e=NE)
    dve.memset(ahead[:, 0, :], 0.0)
    dve.memset(gl[:, :, NG:8], -BIG)
    link(dve.tensor_copy(gl[:, :, 0:NG], lg[:, :, 0:NG]))
    for t in range(T):
        ins = dve.max(gm[:, t, :], gl[:, t, :])
    link(ins)
    dve.tensor_tensor(eg, lg[:, :, 0:NG], gm[:, :, 0:1].to_broadcast([P, T, NG]), ALU.subtract).then_inc(*k.sig("group_logits_ready").tick(l))
    for t in range(T):
        ins = dve.max_index(gi[:, t, :], gm[:, t, :], gl[:, t, :])
    link(ins)
    link(dve.tensor_copy(gf, gi[:, :, 0]))
    link(dve.tensor_tensor(mg, iota[:, 0:NG].unsqueeze(1).to_broadcast([P, T, NG]), gf.unsqueeze(2).to_broadcast([P, T, NG]), ALU.is_equal))
    dve.tensor_scalar(ng, mg, BIG, -BIG, ALU.mult, ALU.add)
    le4, shape = le.rearrange("p t (g e) -> p t g e", g=NG), [P, T, NG, EPG]
    link(dve.tensor_tensor(le4, lg[:, :, NG:].rearrange("p t (g e) -> p t g e", g=NG), mg.unsqueeze(3).to_broadcast(shape), ALU.mult))
    link(dve.tensor_tensor(le4, le4, ng.unsqueeze(3).to_broadcast(shape), ALU.add))
    for t in range(T):
        ins = dve.max(ev[:, t, :], le[:, t, :])
    link(ins)
    dve.tensor_tensor(e2, ev[:, :, 1], ev[:, :, 0], ALU.subtract).then_inc(*k.sig("second_minus_first").tick(l))
    for t in range(T):
        ins = dve.max_index(ei[:, t, :], ev[:, t, :], le[:, t, :])
    link(ins)
    link(dve.tensor_copy(ef, ei[:, :, 0:2]))
    for j in range(2):
        ins = dve.tensor_tensor(k.choices(j)[:, 0:T, :], iota.unsqueeze(1).to_broadcast([P, T, NE]), ef[:, :, j:j + 1].to_broadcast([P, T, NE]), ALU.is_equal)
    link(ins)
    dve.tensor_tensor(k.choices(2)[:, 0:T, :], k.choices(0)[:, 0:T, :], k.choices(1)[:, 0:T, :], ALU.add).then_inc(*k.sig("choices_ready").tick(l))
    dve.wait_ge(*k.sig("group_exp").at(l))
    link(dve.tensor_reduce(total, eg, AX.X, ALU.add))
    dve.wait_ge(*k.sig("second_exp").at(l))
    link(dve.tensor_scalar(inv, e2, 1.0, None, ALU.add))
    link(dve.tensor_tensor(inv, inv, total, ALU.mult))
    link(dve.reciprocal(k.gates[:, 0:T], inv))
    dve.tensor_tensor(k.gates[:, NT:NT + T], k.gates[:, 0:T], e2, ALU.mult)
    key = ("rank", l)
    dve.wait_ge(*k.full(key))
    rank, counts = (k.slot(key)[:, o:o + T * NE].rearrange("p (t e) -> p t e", t=T) for o in (0, 512))
    for t in range(T):
        link(dve.tensor_tensor(ahead[:, t + 1, :], ahead[:, t, :], counts[:, t, :], ALU.add))
    count = ahead[:, T, :]
    link(dve.tensor_scalar(nb, count, 0.0, None, ALU.is_gt))
    for n in range(1, T):
        link(dve.scalar_tensor_tensor(nb, count, float(P * n), nb, ALU.is_gt, ALU.add))
    link(dve.tensor_tensor_scan(pend, k.c("ones")[:, 0:NE], nb, 0.0, ALU.mult, ALU.add))
    cmp = f[:, 2048:2048 + MAXB * NE].rearrange("p (b e) -> p b e", b=MAXB)
    by, tn, tc = f[:, 1700:1700 + MAXB], f[:, 1760:1784], f[:, 1784:1785]
    link(dve.tensor_tensor(cmp, pend.unsqueeze(1).to_broadcast([P, MAXB, NE]), k.c("block").unsqueeze(2).to_broadcast([P, MAXB, NE]), ALU.is_le))
    link(dve.tensor_reduce(by, cmp, AX.X, ALU.add))
    link(dve.tensor_scalar(by, by, float(NE - 1), None, ALU.min))
    dve.tensor_copy(ri[:, RI_TABLE:RI_TABLE + MAXB], by)
    link(dve.tensor_scalar(tn, k.c("pairs"), pend[:, NE - 1:NE], None, ALU.is_lt))
    link(dve.tensor_reduce(tc, tn, AX.X, ALU.add))
    dve.tensor_copy(ri[:, RI_TURNS:RI_TURNS + 1], tc).then_inc(*k.sig("table_ready").tick(l))
    link(dve.tensor_tensor(base, pend, nb, ALU.subtract))
    link(dve.tensor_scalar(base, base, float(P), None, ALU.mult))
    link(dve.tensor_tensor(place, ahead[:, 0:T, :], base.unsqueeze(1).to_broadcast([P, T, NE]), ALU.add))
    dve.tensor_tensor(place, rank, place, ALU.add).then_inc(*read.tick(key))
    dve.wait_ge(*read.at(key))
    for j in range(2):
        link(dve.tensor_tensor(prod, k.choices(j)[:, 0:T, :], place, ALU.mult))
        link(dve.tensor_reduce(rows[:, NT * j:NT * j + T], prod, AX.X, ALU.add))
        ins = dve.tensor_copy(ri[:, RI_SLOT + NT * j:RI_SLOT + NT * j + T], rows[:, NT * j:NT * j + T])
    link(ins)
    s = k.scr
    hot = s[:, 0:2 * NT * P].rearrange("p (n r) -> p n r", r=P)
    past, inside, own = (s[:, o:o + 2 * NT * MAXB].rearrange("p (n b) -> p n b", b=MAXB) for o in (1536, 2112, 2688))
    row = s[:, 3264:3264 + 2 * NT]
    for j in range(2):
        a = slice(NT * j, NT * j + T)
        link(dve.tensor_tensor(past[:, a, :], rows[:, a].unsqueeze(2).to_broadcast([P, T, MAXB]),
                               k.c("begin").unsqueeze(1).to_broadcast([P, T, MAXB]), ALU.subtract))
        link(dve.tensor_scalar(own[:, a, :], past[:, a, :], -0.5, None, ALU.is_gt))
        link(dve.scalar_tensor_tensor(inside[:, a, :], past[:, a, :], float(P), own[:, a, :], ALU.is_lt, ALU.mult))
        dve.tensor_tensor(own[:, a, :], inside[:, a, :], k.c("token")[:, 0:T].unsqueeze(2).to_broadcast([P, T, MAXB]), ALU.mult)
        link(dve.tensor_tensor(past[:, a, :], inside[:, a, :], past[:, a, :], ALU.mult))
        link(dve.tensor_reduce(row[:, a], past[:, a, :], AX.X, ALU.add))
        ins = dve.tensor_tensor(hot[:, a, :], k.c("iota").unsqueeze(1).to_broadcast([P, T, P]), row[:, a].unsqueeze(2).to_broadcast([P, T, P]), ALU.is_equal)
    ins.then_inc(*k.sig("row_hots_ready").tick(l))
    dve.wait_ge(*k.full(("rows", l)))
    dve.tensor_copy(ri[:, RI_ROWS:RI_ROWS + MAXB], k.slot(("rows", l))[:, 0:MAXB]).then_inc(*read.tick(("rows", l)))


def pool_program(k, pool):
    io = k.io
    step = k.sig("pool_step")
    cols_in = k.sig("columns_loaded")

    def link(ins):
        ins.then_inc(*step.tick())
        pool.wait_ge(*step.last())

    def col(dst, src):
        pool.dma_start(dst, src, allow_slow_non_contiguous=True)

    def pool_weights(l):
        pool.dma_start(k.poolw().rearrange("p (g d) -> p g d", g=4), io["pool_w"][l].rearrange("g c d -> c g d")).then_inc(*cols_in.tick(l, 16))

    for l in range(DEPTH):
        c = lambda o, n: k.cols[:, 32 * l + o:32 * l + o + n]
        for dst, src in ((k.bmod[:, 48 * l:48 * l + 48], io["b_mod"][l].rearrange("(j p) -> p j", p=P)),
                         (c(K_PS, 2), io["pool_scale"][l].rearrange("(j p) -> p j", p=P)),
                         (c(K_HN, 2), io["hg_norm_g"][l].rearrange("(j p) -> p j", p=P)),
                         (c(K_QN, 2), io["mla_q_norm_g"][l].rearrange("(j p) -> p j", p=P)),
                         (c(K_KN, 1), io["mla_kv_norm_g"][l].rearrange("(j p) -> p j", p=P)),
                         (k.logits[:, 8 * l:8 * l + 8], io["hg_lb_logits"][l].rearrange("r (h p) -> p (r h)", p=P))):
            pool.dma_start(dst, src, allow_slow_non_contiguous=True).then_inc(*cols_in.tick(0, 16))
    pool.memset(k.tok[:, 0:D], 0.0).then_inc(*k.sig("rows_zero").tick())
    pool.wait_ge(*k.sig("rows_zero").at())
    pool_weights(0)
    pool.wait_ge(*k.full(("mod", 0, RING_EARLY - 1)))
    pool.dma_start(k.y_dram.rearrange("(b p) d -> p b d", p=P)[:, SURE_BLOCKS:MAXB, :],
                   k.tok[:, 0:D].unsqueeze(1).to_broadcast([P, MAXB - SURE_BLOCKS, D])).then_inc(*k.sig("y_cleared").tick(None, 16))
    for l in range(DEPTH):
        T = ROWS_PER_LAYER[l]
        if l:
            pool.wait_ge(*k.sig("moe_done").at(l - 1))
            pool_weights(l)
        gap = k.sig("gap_ready")
        dring = lambda n: k.scr[:, (n % RING_D) * 768:(n % RING_D + 1) * 768].rearrange("p (c t) -> p c t", c=NT)
        pool.wait_ge(*k.sig("head_done").at((l, 2, HEADS_G - 1)))
        for hd in range(HEADS_G):
            xf, xb = (k.prefix(dr)[:, hd] for dr in range(2))
            for n, (hd_, m) in enumerate(HG_ITEMS):
                if hd_ != hd or m in (1, 2):
                    continue
                wait_decay_room(k, pool, l, n)
                d = dring(n)
                if m == 0:
                    ins = pool.tensor_tensor(d, xf[:, :, P:P + 1].to_broadcast([P, NT, P]), xf[:, :, 1:P + 1], ALU.subtract)
                elif m == 3:
                    ins = pool.tensor_tensor(d[:, 0:T, :], xb[:, 0:T, P:P + 1].to_broadcast([P, T, P]), xb[:, 0:T, 0:P], ALU.subtract)
                else:
                    h, dr = LEVELS[(m - 4) // 2], m % 2
                    x = halves(xb[:, 0:T, 0:P] if dr else xf[:, 0:T, 1:P + 1], h)
                    e = halves(d[:, 0:T, :], h)
                    mid = x[:, :, :, h - 1 + dr:h + dr]
                    mid = mid.to_broadcast([P, T, P // (2 * h), h])
                    if dr == 0:
                        pool.tensor_tensor(e[:, :, :, 0:h], mid, x[:, :, :, 0:h], ALU.subtract)
                        ins = pool.tensor_tensor(e[:, :, :, h:2 * h], x[:, :, :, h:2 * h], mid, ALU.subtract)
                    else:
                        pool.tensor_tensor(e[:, :, :, 0:h], mid, x[:, :, :, 0:h], ALU.subtract)
                        ins = pool.tensor_tensor(e[:, :, :, h:2 * h], x[:, :, :, h:2 * h], mid, ALU.subtract)
                ins.then_inc(*gap.tick((l, hd, m)))
        pool.wait_ge(*k.sig("psum_read_by_vector").at(("rows", l)))
        for p in range(2):
            pool.wait_ge(*k.sig("h2_stored%d" % p).at((l, T - 2 + (T + p) % 2)))
        moe_pool(k, pool, l)


def block_turns(k, eng, l):
    return eng.value_load(k.routei[0:1, RI_TURNS:RI_TURNS + 1], min_val=1, max_val=MAXB // 2)


def lsig(k, name, l):
    return k.sig("%s%d" % (name, l), GatherSignal if name.startswith("rows_gathered") else LoopSignal)


def wbuf(k, p, which):
    o = p * 12288 + which * 4096
    return k.w[:, o:o + 4096]


X_ROWS = (0, 1024)
X_T = (2048, 5120)
Y_ROWS = (3072, 4096)
X_SLOT, Y_SLOT = (0, 3), (3, 1)
HID, GATE_EXP, HID_T = (0, 512), (1024, 1536), (2048, 2560)


def moe_sync(k, sp, l):
    io = k.io
    T = ROWS_PER_LAYER[l]
    pe = lsig(k, "moe_tensor", l)
    gu, dn = ([lsig(k, "%s_loaded%d_" % (n, p), l) for p in range(2)] for n in ("gate_up", "down"))
    sp.wait_ge(*k.sig("table_ready").at(l))
    sp.wait_ge(*k.full(("rank", l)))
    for p in range(2):
        sp.wait_ge(*k.sig("h2_stored%d" % p).at((l, T - 2 + (T + p) % 2)))
        sp.sem_inc(gu[p].sem, gu[p].per())
        sp.sem_inc(dn[p].sem, dn[p].per())
    turns = block_turns(k, sp, l)
    with sp.Fori(0, turns) as i:
        expert = []
        for p in range(2):
            expert.append(sp.value_load(k.routei[0:1, bass.ds(i * 2 + (RI_TABLE + p), 1)], min_val=0, max_val=NE - 1))
            e = expert[p]
            if p:
                sp.wait_ge(*lsig(k, "rows_gathered1_", l).now(None, i))
                sp.sem_inc(*k.sig("weights_turn").tick())
            sp.wait_ge(*pe.before(("gate_up", p), i))
            for which, name in ((0, "expert_w1"), (1, "expert_w3")):
                sp.dma_start(wbuf(k, p, which), io[name][l, bass.ds(e, 1)].rearrange("e (p c) n -> p (e c n)", p=P)).then_inc(*gu[p].tick(None, 16))
        for p, e in enumerate(expert):
            sp.wait_ge(*pe.before(("down", p), i))
            sp.dma_start(wbuf(k, p, 2), io["expert_w2"][l, bass.ds(e, 1)].rearrange("e (p c) n -> p (e c n)", p=P)).then_inc(*dn[p].tick(None, 16))
    for s in gu + dn:
        s.close()
    if l == DEPTH - 1:
        for t in range(LT):
            sp.wait_ge(*k.sig("x_ready").at((l, t)))
            sp.dma_start(io["out"][0, t * P:(t + 1) * P, :], k.x[:, t, :]).then_inc(*k.sig("out_stored").tick("all", 16))


def moe_pool(k, pool, l):
    T = ROWS_PER_LAYER[l]
    pe = lsig(k, "moe_tensor", l)
    xin = [lsig(k, "rows_gathered%d_" % p, l) for p in range(2)]
    now = lsig(k, "moe_pool", l)
    pool.sem_inc(now.sem, now.per())
    turns = block_turns(k, pool, l)
    with pool.Fori(0, turns) as i:
        for p in range(2):
            idx = k.routei[:, RI_NOW + p:RI_NOW + p + 1]
            pool.wait_ge(*pe.before(("x", p), i))
            pool.tensor_copy(idx, k.routei[:, bass.ds(i * 2 + (RI_ROWS + p), 1)]).then_inc(*now.tick(p))
            pool.wait_ge(*now.now(p, i))
            pool.sem_inc(*k.sig("gather_turn").tick())
            pool.indirect_dma_start(k.feat[:, X_ROWS[p]:X_ROWS[p] + D], None, k.h_dram[l], bass.IndirectOffsetOnAxis(ap=idx, axis=0)) \
                .then_inc(*xin[p].tick(None, 16))
    for s in xin + [now]:
        s.close()
    for p in range(2):
        s = lsig(k, "y_stored%d_" % p, l)
        pool.wait_ge(s.sem, turns * s.per() + s.per())
    pool.wait_ge(*k.sig("moe_done").at(l))
    pool.sem_inc(*k.sig("gather_turn").tick())
    for t in range(T):
        if t >= 2:
            pool.wait_ge(*k.sig("y_used").at((l, t - 2)))
        for j in range(2):
            i = RI_SLOT + NT * j + t
            pool.indirect_dma_start(k.expert_rows(t, j), None, k.y_dram,
                                    bass.IndirectOffsetOnAxis(ap=k.routei[:, i:i + 1], axis=0)).then_inc(*k.sig("y_gathered%d" % (t % 2)).tick((l, t), 16))


def moe_tensor(k, pe, l):
    ident = k.c("ident")
    sig, act, dve = (lsig(k, n, l) for n in ("moe_tensor", "moe_scalar", "moe_vector"))
    gu, dn = ([lsig(k, "%s_loaded%d_" % (n, p), l) for p in range(2)] for n in ("gate_up", "down"))
    xin = [lsig(k, "rows_gathered%d_" % p, l) for p in range(2)]
    slot = lambda n: k.psum[:, n * 1024:(n + 1) * 1024]
    for key in k.slots[-4:]:
        k.wait_read(pe, key)
    pe.wait_ge(*k.sig("table_ready").at(l))
    turns = block_turns(k, pe, l)
    with pe.Fori(0, turns) as i:
        def hidden_transposed(p):
            pe.wait_ge(*dve.now(("hidden", p), i))
            hid = k.scr[:, HID[p]:HID[p] + DE].rearrange("p (q c) -> p c q", c=EC)
            for c in range(EC):
                ins = pe.transpose(slot(0)[:, p * 512 + c * P:p * 512 + (c + 1) * P], hid[:, c, :], ident)
            ins.then_inc(*sig.tick(("hid_t", p)))

        for p in range(2):
            pe.wait_ge(*xin[p].now(None, i))
            if p == 0:
                pe.wait_ge(*dve.before(("hid_t", 1), i))
            else:
                for who in (act, dve):
                    pe.wait_ge(*who.before(("y", 0), i))
            x = k.feat[:, X_ROWS[p]:X_ROWS[p] + D].rearrange("p (q c) -> p c q", c=DC)
            for c in range(DC):
                ins = pe.transpose(slot(X_SLOT[p])[:, c * P:(c + 1) * P], x[:, c, :], ident)
            ins.then_inc(*sig.tick(("x", p)))
        for p in range(2):
            pe.wait_ge(*act.now(("x_t", p), i))
            pe.wait_ge(*gu[p].now(None, i))
            pe.wait_ge(*dve.before(("hidden", p), i))
            if p == 0:
                for who in (act, dve):
                    pe.wait_ge(*who.before(("y", 1), i))
            xt = k.feat[:, X_T[p]:X_T[p] + D].rearrange("p (c t) -> p c t", c=DC)
            for which in range(2):
                w = wbuf(k, p, which).rearrange("p (c n) -> p c n", c=DC)
                ins = matmuls(pe, slot(1 + p)[:, which * 512:which * 512 + 512], [(xt[:, c, :], w[:, c, :]) for c in range(DC)])
                if (p, which) == (1, 0):
                    hidden_transposed(0)
            ins.then_inc(*sig.tick(("gate_up", p)))

        for p in range(2):
            pe.wait_ge(*dve.now(("hid_t", p), i))
            pe.wait_ge(*dn[p].now(None, i))
            ht = k.scr[:, HID_T[p]:HID_T[p] + DE].rearrange("p (c t) -> p c t", c=EC)
            w = wbuf(k, p, 2).rearrange("p (c n) -> p c n", c=EC)
            for half in range(2):
                for c in range(EC):
                    ins = pe.matmul(slot(Y_SLOT[p])[:, half * 512:half * 512 + 512], ht[:, c, :], w[:, c, half * 512:half * 512 + 512],
                                    start=(c == 0), stop=(c == EC - 1))
                    if (p, half, c) == (0, 1, 2):
                        hidden_transposed(1)
            ins.then_inc(*sig.tick(("down", p)))
    sig.close()
    pe.wait_ge(sig.sem, turns * sig.per() + sig.per())
    pe.sem_inc(*k.sig("moe_done").tick(l))
    for who in (act, dve):
        pe.wait_ge(who.sem, turns * who.per() + who.per())


def moe_scalar(k, act, l):
    sig, pe, dve = (lsig(k, n, l) for n in ("moe_scalar", "moe_tensor", "moe_vector"))
    stored = [lsig(k, "y_stored%d_" % p, l) for p in range(2)]
    slot = lambda n: k.psum[:, n * 1024:(n + 1) * 1024]
    act.wait_ge(*k.sig("table_ready").at(l))
    act.sem_inc(sig.sem, sig.per())
    for p in range(2):
        act.sem_inc(stored[p].sem, stored[p].per())
    turns = block_turns(k, act, l)
    with act.Fori(0, turns) as i:
        for p in range(2):
            act.wait_ge(*pe.now(("x", p), i))
            act.wait_ge(*pe.before(("gate_up", p), i))
            act.copy(k.feat[:, X_T[p]:X_T[p] + D], slot(X_SLOT[p])).then_inc(*sig.tick(("x_t", p)))
        for p in range(2):
            act.wait_ge(*pe.now(("gate_up", p), i))
            act.wait_ge(*dve.before(("hidden", p), i))
            act.activation(k.scr[:, GATE_EXP[p]:GATE_EXP[p] + DE], slot(1 + p)[:, 0:DE], ACT.Exp, scale=-1.0).then_inc(*sig.tick(("exp", p)))
        for p in range(2):
            act.wait_ge(*pe.now(("down", p), i))
            act.wait_ge(*stored[p].before(None, i))
            act.copy(k.feat[:, Y_ROWS[p]:Y_ROWS[p] + 512], slot(Y_SLOT[p])[:, 0:512]).then_inc(*sig.tick(("y", p)))
            act.wait_ge(*sig.now(("y", p), i))
            act.wait_ge(*dve.now(("y", p), i))
            act.dma_start(k.y_dram.rearrange("(b p) d -> p b d", p=P)[:, bass.ds(i * 2 + p, 1), :],
                          k.feat[:, Y_ROWS[p]:Y_ROWS[p] + D].unsqueeze(1)).then_inc(*stored[p].tick(None, 16))
    for s in [sig] + stored:
        s.close()


def moe_vector(k, dve, l):
    sig, pe, act = (lsig(k, n, l) for n in ("moe_vector", "moe_tensor", "moe_scalar"))
    stored = [lsig(k, "y_stored%d_" % p, l) for p in range(2)]
    slot = lambda n: k.psum[:, n * 1024:(n + 1) * 1024]
    dve.sem_inc(sig.sem, sig.per())
    turns = block_turns(k, dve, l)
    with dve.Fori(0, turns) as i:
        for p in range(2):
            g, u = slot(1 + p)[:, 0:DE], slot(1 + p)[:, 512:512 + DE]
            e, h = k.scr[:, GATE_EXP[p]:GATE_EXP[p] + DE], k.scr[:, HID[p]:HID[p] + DE]

            def silu():
                dve.wait_ge(*act.now(("exp", p), i))
                dve.tensor_scalar(e, e, 1.0, None, ALU.add).then_inc(*sig.tick(("one", p)))
                dve.wait_ge(*sig.now(("one", p), i))
                dve.reciprocal(e, e).then_inc(*sig.tick(("inv", p)))
                dve.wait_ge(*sig.now(("inv", p), i))
                dve.wait_ge(*pe.before(("hid_t", p), i))
                dve.tensor_tensor(h, g, e, ALU.mult).then_inc(*sig.tick(("silu", p)))
                dve.wait_ge(*sig.now(("silu", p), i))
                dve.tensor_tensor(h, u, h, ALU.mult).then_inc(*sig.tick(("hidden", p)))

            silu()
            dve.wait_ge(*pe.now(("hid_t", p), i))
            dve.wait_ge(*pe.before(("down", p), i))
            dve.tensor_copy(k.scr[:, HID_T[p]:HID_T[p] + DE], slot(0)[:, p * 512:p * 512 + 512]).then_inc(*sig.tick(("hid_t", p)))
            if p:
                y_copy(k, dve, sig, pe, stored, slot, 0, i)
        y_copy(k, dve, sig, pe, stored, slot, 1, i)
    sig.close()


def y_copy(k, dve, sig, pe, stored, slot, p, i):
    dve.wait_ge(*pe.now(("down", p), i))
    dve.wait_ge(*stored[p].before(None, i))
    dve.tensor_copy(k.feat[:, Y_ROWS[p] + 512:Y_ROWS[p] + D], slot(Y_SLOT[p])[:, 512:1024]).then_inc(*sig.tick(("y", p)))


def build(nc, io, book):
    with ExitStack() as ctx:
        ctx.enter_context(nc.allow_non_contiguous_dma("columns of vectors"))
        k = Kernel(nc, io, book, ctx)
        block = ctx.enter_context(nc.Block())

        @block.tensor
        def _(pe):
            tensor_program(k, pe)

        @block.scalar
        def _(act):
            scalar_program(k, act)

        @block.vector
        def _(dve):
            vector_program(k, dve)

        @block.gpsimd
        def _(pool):
            pool_program(k, pool)

        @block.sync
        def _(sp):
            sync_program(k, sp)


_INS = ["x", "c", "ctx", "c_ctx", "w_mod", "b_mod", "w_in", "pool_w", "pool_scale", "hg_lb_logits", "hg_norm_g",
        "mla_q_norm_g", "mla_w_uq", "mla_kv_norm_g", "mla_w_ukv", "w_out", "ln1_g", "ln1_b", "ln2_g", "ln2_b",
        "router_group_w", "router_group_b", "router_expert_w", "router_expert_b", "expert_w1", "expert_w3", "expert_w2"]


def kernel(**inputs):
    import concourse.bacc as bacc
    from concourse.bass_utils import run_bass_kernel_spmd

    const, masks, bands = shape_constants()
    arrays = {"in_" + n: np.ascontiguousarray(inputs[n]) for n in _INS}
    arrays.update(shape_const=const, shape_masks=masks, shape_bands=bands)
    book = {}
    for _ in range(2):
        nc = bacc.Bacc("TRN2", target_bir_lowering=False, num_devices=1)
        io = {n.removeprefix("in_"): nc.dram_tensor(n, a.shape, mybir.dt.from_np(a.dtype), kind="ExternalInput").ap()
              for n, a in arrays.items()}
        io["out"] = nc.dram_tensor("out", (1, SEQ, D), F32, kind="ExternalOutput").ap()
        build(nc, io, book)
    r = run_bass_kernel_spmd(nc, [arrays], core_ids=[0])
    return r.results[0]["out"]
```
